# Optimizing a Trainium2 kernel written in Bass

```python
import math
import jax, jax.numpy as jnp
from jax import lax
import numpy as np

D_MODEL = 2048
BATCH = 1
SEQ = 256
DEPTH = 2
DEC_BATCH = 8
DEC_SEQ = 8
PAST_LEN = 2048
PAGE_SIZE = 128

MIX_WIDTH = D_MODEL
SB_HEAD_DIM = 64
SB_WIDTH = MIX_WIDTH // 4
SB_HEADS = SB_WIDTH // SB_HEAD_DIM
SB_BLOCK = 128
SB_BIAS_NEAR = -4.0
SB_BIAS_FAR = -10.0
SSD_HEAD_DIM = 64
SSD_WIDTH = MIX_WIDTH // 2
SSD_HEADS = SSD_WIDTH // SSD_HEAD_DIM
SSD_GROUPS = 2
SSD_STATE = 128
SSD_CONV = 4
SSD_CHUNK = 128
SSD_CONV_DIM = SSD_WIDTH + 2 * SSD_GROUPS * SSD_STATE
POOL_WIDTH = MIX_WIDTH - SB_WIDTH - SSD_WIDTH
POOL_WINDOWS = (2, 4, 8, 16)
POOL_GROUPS = len(POOL_WINDOWS)
POOL_GROUP_DIM = POOL_WIDTH // POOL_GROUPS
POOL_HIST = max(POOL_WINDOWS) - 1
D_FF = ((8 * D_MODEL // 3 + 255) // 256) * 256
FFN_CONV = 3
RMS_EPS = 1e-6

SPLITS = (SB_WIDTH, 2 * SB_WIDTH, 3 * SB_WIDTH,
          3 * SB_WIDTH + SSD_WIDTH,
          3 * SB_WIDTH + SSD_WIDTH + SSD_CONV_DIM,
          3 * SB_WIDTH + SSD_WIDTH + SSD_CONV_DIM + SSD_HEADS)
IN_DIM = 3 * SB_WIDTH + SSD_WIDTH + SSD_CONV_DIM + SSD_HEADS + POOL_WIDTH

kernel_name = 'hybrid_stickbreak_ssd_pool_convffn_step'

def rms_norm(x, gain):
    xf = x.astype(jnp.float32)
    y = xf * lax.rsqrt(jnp.mean(xf * xf, axis=-1, keepdims=True) + RMS_EPS)
    return (y * gain.astype(jnp.float32)).astype(x.dtype)

def causal_dwconv(hist, x, w, bias):
    width = w.shape[0]
    L = x.shape[1]
    xh = jnp.concatenate([hist.astype(x.dtype), x], axis=1)
    out = bias + xh[:, 0:L] * w[0]
    for k in range(1, width):
        out = out + xh[:, k:k + L] * w[k]
    return out, xh[:, L:]

def stick_breaking_attention(q, k, v, pos0, head_bias):
    b, L, H, Dh = q.shape
    Tk = k.shape[1]
    scale = 1.0 / math.sqrt(Dh)
    blk = SB_BLOCK if L % SB_BLOCK == 0 else L
    nb = L // blk
    k_pos = jnp.arange(Tk)
    q_blocks = q.reshape(b, nb, blk, H, Dh).swapaxes(0, 1)
    q_pos = (pos0 + jnp.arange(L)).reshape(nb, blk)
    hb = head_bias.astype(jnp.float32)[None, :, None, None]

    def one_block(args):
        qi, pi = args
        z = jnp.einsum('bqhd,bkhd->bhqk', qi, k, preferred_element_type=jnp.float32) * scale + hb
        mask = k_pos[None, :] < pi[:, None]
        log_keep = jnp.where(mask, jax.nn.log_sigmoid(-z), 0.0)
        later = lax.cumsum(log_keep, axis=3, reverse=True) - log_keep
        w = jnp.where(mask, jnp.exp(jax.nn.log_sigmoid(z) + later), 0.0)
        return jnp.einsum('bhqk,bkhd->bqhd', w.astype(v.dtype), v)

    o = lax.map(one_block, (q_blocks, q_pos))
    return o.swapaxes(0, 1).reshape(b, L, H * Dh)

def ssd_chunked(x, dt, a, bm, cm, s0):
    b, L, H, P = x.shape
    G, N = bm.shape[2], bm.shape[3]
    E = H // G
    Q = SSD_CHUNK if L % SSD_CHUNK == 0 else L
    c = L // Q
    xc = x.reshape(b, c, Q, G, E, P)
    dtc = dt.reshape(b, c, Q, G, E)
    bc = bm.reshape(b, c, Q, G, N)
    cc = cm.reshape(b, c, Q, G, N)
    cum = jnp.cumsum(dtc * a.reshape(G, E), axis=2)
    causal = jnp.tril(jnp.ones((Q, Q), dtype=bool))[:, :, None, None]
    seg = cum[:, :, :, None] - cum[:, :, None, :]
    decay = jnp.exp(jnp.where(causal, seg, -jnp.inf))
    cb = jnp.einsum('bctgn,bcsgn->bctsg', cc, bc)
    w_ts = cb[..., None] * decay * dtc[:, :, None]
    y = jnp.einsum('bctsge,bcsgep->bctgep', w_ts, xc)
    to_end = jnp.exp(cum[:, :, -1:] - cum) * dtc
    chunk_states = jnp.einsum('bcsgn,bcsge,bcsgep->bcgepn', bc, to_end, xc)
    chunk_decay = jnp.exp(cum[:, :, -1])

    def step(s, inp):
        dec, st = inp
        return dec[..., None, None] * s + st, s

    s_final, s_in = lax.scan(step, s0.reshape(b, G, E, P, N),
                             (chunk_decay.swapaxes(0, 1), chunk_states.swapaxes(0, 1)))
    s_in = s_in.swapaxes(0, 1)
    y = y + jnp.einsum('bctgn,bcgepn,bctge->bctgep', cc, s_in, jnp.exp(cum))
    return y.reshape(b, L, H, P), s_final.reshape(b, H, P, N)

def multiscale_pool(xp, hist, pos0, pool_w, pool_scale):
    b, L, C = xp.shape
    xh = jnp.concatenate([hist.astype(xp.dtype), xp], axis=1)
    xf = xh.astype(jnp.float32)
    cs = jnp.concatenate([jnp.zeros((b, 1, C), jnp.float32), jnp.cumsum(xf, axis=1)], axis=1)
    pos = pos0 + jnp.arange(L)
    pooled = []
    for g, win in enumerate(POOL_WINDOWS):
        ch = slice(g * POOL_GROUP_DIM, (g + 1) * POOL_GROUP_DIM)
        wsum = cs[:, POOL_HIST + 1:POOL_HIST + 1 + L, ch] - cs[:, POOL_HIST + 1 - win:POOL_HIST + 1 - win + L, ch]
        count = jnp.minimum(win, pos + 1).astype(jnp.float32)
        pooled.append(wsum / count[None, :, None])
    diff = jnp.concatenate(pooled, axis=-1) - xf[:, POOL_HIST:]
    diff = diff.reshape(b, L, POOL_GROUPS, POOL_GROUP_DIM)
    y = jnp.einsum('blgc,gcd->blgd', diff, pool_w).reshape(b, L, C) * pool_scale
    return y.astype(xp.dtype), xh[:, L:]

def hybrid_layer(x, l, pos0, past_k, past_v, ssm0, conv_hist, pool_hist, ffn_hist, weights):
    (norm1, w_in, sb_bias, ssd_conv_w, ssd_conv_b, dt_bias, a_log, d_skip, ssd_norm,
     pool_w, pool_scale, w_out, norm2, w_gate, w_up, ffn_conv_w, ffn_conv_b, w_down) = weights
    b, L, _ = x.shape
    h = rms_norm(x, norm1[l])
    proj = h @ w_in[l]
    q, k, v, z, xbc, dt_raw, xp = jnp.split(proj, SPLITS, axis=-1)

    q = q.reshape(b, L, SB_HEADS, SB_HEAD_DIM)
    k = k.reshape(b, L, SB_HEADS, SB_HEAD_DIM)
    v = v.reshape(b, L, SB_HEADS, SB_HEAD_DIM)
    k_all = k if past_k is None else jnp.concatenate([past_k.astype(k.dtype), k], axis=1)
    v_all = v if past_v is None else jnp.concatenate([past_v.astype(v.dtype), v], axis=1)
    o_sb = stick_breaking_attention(q, k_all, v_all, pos0, sb_bias[l]).astype(x.dtype)

    xbc_c, conv_new = causal_dwconv(conv_hist, xbc, ssd_conv_w[l], ssd_conv_b[l])
    xbc_c = jax.nn.silu(xbc_c)
    xs, bm, cm = jnp.split(xbc_c, (SSD_WIDTH, SSD_WIDTH + SSD_GROUPS * SSD_STATE), axis=-1)
    xs4 = xs.reshape(b, L, SSD_HEADS, SSD_HEAD_DIM).astype(jnp.float32)
    dt = jax.nn.softplus(dt_raw.astype(jnp.float32) + dt_bias[l].astype(jnp.float32))
    a = -jnp.exp(a_log[l].astype(jnp.float32))
    y_ssd, ssm_new = ssd_chunked(xs4, dt, a,
                                 bm.reshape(b, L, SSD_GROUPS, SSD_STATE).astype(jnp.float32),
                                 cm.reshape(b, L, SSD_GROUPS, SSD_STATE).astype(jnp.float32),
                                 ssm0.astype(jnp.float32))
    y_ssd = (y_ssd + d_skip[l].astype(jnp.float32)[:, None] * xs4).reshape(b, L, SSD_WIDTH)
    y_ssd = rms_norm(y_ssd * jax.nn.silu(z.astype(jnp.float32)), ssd_norm[l]).astype(x.dtype)

    y_pool, pool_new = multiscale_pool(xp, pool_hist, pos0, pool_w[l], pool_scale[l])

    x = x + jnp.concatenate([o_sb, y_ssd, y_pool], axis=-1) @ w_out[l]

    h2 = rms_norm(x, norm2[l])
    g = h2 @ w_gate[l]
    u = h2 @ w_up[l]
    g_c, ffn_new = causal_dwconv(ffn_hist, g, ffn_conv_w[l], ffn_conv_b[l])
    x = x + (jax.nn.silu(g_c) * u) @ w_down[l]
    return x, k, v, ssm_new, conv_new, pool_new, ffn_new

def run_trunk(x, pos0, cache_k, cache_v, page_table, st_ssm, st_conv, st_pool, st_ffn, weights, final_norm):
    b = x.shape[0]
    new_rows = [[] for _ in range(6)]
    for l in range(DEPTH):
        if cache_k is None:
            past_k = past_v = None
            ssm0 = jnp.zeros((b, SSD_HEADS, SSD_HEAD_DIM, SSD_STATE), jnp.float32)
            conv_hist = jnp.zeros((b, SSD_CONV - 1, SSD_CONV_DIM), x.dtype)
            pool_hist = jnp.zeros((b, POOL_HIST, POOL_WIDTH), x.dtype)
            ffn_hist = jnp.zeros((b, FFN_CONV - 1, D_FF), x.dtype)
        else:
            past_k = cache_k[l][page_table].reshape(b, -1, SB_HEADS, SB_HEAD_DIM)
            past_v = cache_v[l][page_table].reshape(b, -1, SB_HEADS, SB_HEAD_DIM)
            ssm0, conv_hist, pool_hist, ffn_hist = st_ssm[l], st_conv[l], st_pool[l], st_ffn[l]
        x, k_new, v_new, ssm_new, conv_new, pool_new, ffn_new = hybrid_layer(
            x, l, pos0, past_k, past_v, ssm0, conv_hist, pool_hist, ffn_hist, weights)
        for lst, arr in zip(new_rows, (k_new, v_new, ssm_new, conv_new, pool_new, ffn_new)):
            lst.append(arr)
    stacked = [jnp.stack(lst) for lst in new_rows]
    return rms_norm(x, final_norm), stacked

def setup_inputs(seed: int = 0) -> dict:
    key = jax.random.key(seed)
    ks = jax.random.split(key, 32)
    f32 = jnp.float32
    n_pages = PAST_LEN // PAGE_SIZE
    n_used = DEC_BATCH * n_pages
    n_pool = n_used + max(1, n_used // 4)
    out_scale = (2 * DEPTH) ** -0.5

    def nrm(k, shape, s=1.0):
        return jax.random.normal(k, shape, f32) * s

    dt0 = jnp.exp(jax.random.uniform(ks[14], (DEPTH, SSD_HEADS), f32) * (math.log(0.1) - math.log(0.001)) + math.log(0.001))
    sb_bias0 = jnp.linspace(SB_BIAS_NEAR, SB_BIAS_FAR, SB_HEADS, dtype=f32)[None, :]
    inputs = {
        'x_prompt': nrm(ks[0], (BATCH, SEQ, D_MODEL)),
        'x_sample': nrm(ks[1], (DEC_BATCH, DEC_SEQ, D_MODEL)),
        'cache_k': nrm(ks[2], (DEPTH, n_pool, PAGE_SIZE, SB_HEADS, SB_HEAD_DIM)),
        'cache_v': nrm(ks[3], (DEPTH, n_pool, PAGE_SIZE, SB_HEADS, SB_HEAD_DIM)),
        'page_table': jax.random.permutation(ks[4], n_pool)[:n_used].reshape(DEC_BATCH, n_pages).astype(jnp.int32),
        'state_ssm': nrm(ks[5], (DEPTH, DEC_BATCH, SSD_HEADS, SSD_HEAD_DIM, SSD_STATE), 0.1),
        'state_ssm_conv': nrm(ks[6], (DEPTH, DEC_BATCH, SSD_CONV - 1, SSD_CONV_DIM)),
        'state_pool': nrm(ks[7], (DEPTH, DEC_BATCH, POOL_HIST, POOL_WIDTH)),
        'state_ffn_conv': nrm(ks[8], (DEPTH, DEC_BATCH, FFN_CONV - 1, D_FF)),
        'norm1': 1.0 + nrm(ks[9], (DEPTH, D_MODEL), 0.02),
        'w_in': nrm(ks[10], (DEPTH, D_MODEL, IN_DIM), D_MODEL ** -0.5),
        'sb_bias': sb_bias0 + nrm(ks[28], (DEPTH, SB_HEADS), 0.1),
        'ssd_conv_w': nrm(ks[11], (DEPTH, SSD_CONV, SSD_CONV_DIM), SSD_CONV ** -0.5),
        'ssd_conv_b': nrm(ks[12], (DEPTH, SSD_CONV_DIM), 0.02),
        'dt_bias': dt0 + jnp.log(-jnp.expm1(-dt0)),
        'a_log': jnp.log(jax.random.uniform(ks[15], (DEPTH, SSD_HEADS), f32, 1.0, 16.0)),
        'd_skip': 1.0 + nrm(ks[16], (DEPTH, SSD_HEADS), 0.1),
        'ssd_norm': 1.0 + nrm(ks[17], (DEPTH, SSD_WIDTH), 0.02),
        'pool_w': nrm(ks[18], (DEPTH, POOL_GROUPS, POOL_GROUP_DIM, POOL_GROUP_DIM), POOL_GROUP_DIM ** -0.5),
        'pool_scale': 1.0 + nrm(ks[19], (DEPTH, POOL_WIDTH), 0.02),
        'w_out': nrm(ks[20], (DEPTH, MIX_WIDTH, D_MODEL), MIX_WIDTH ** -0.5 * out_scale),
        'norm2': 1.0 + nrm(ks[21], (DEPTH, D_MODEL), 0.02),
        'w_gate': nrm(ks[22], (DEPTH, D_MODEL, D_FF), D_MODEL ** -0.5),
        'w_up': nrm(ks[23], (DEPTH, D_MODEL, D_FF), D_MODEL ** -0.5),
        'ffn_conv_w': nrm(ks[24], (DEPTH, FFN_CONV, D_FF), FFN_CONV ** -0.5),
        'ffn_conv_b': nrm(ks[25], (DEPTH, D_FF), 0.02),
        'w_down': nrm(ks[26], (DEPTH, D_FF, D_MODEL), D_FF ** -0.5 * out_scale),
        'final_norm': 1.0 + nrm(ks[27], (D_MODEL,), 0.02),
    }
    return inputs

def reference(x_prompt, x_sample, cache_k, cache_v, page_table, state_ssm, state_ssm_conv, state_pool,
              state_ffn_conv, norm1, w_in, sb_bias, ssd_conv_w, ssd_conv_b, dt_bias, a_log, d_skip, ssd_norm,
              pool_w, pool_scale, w_out, norm2, w_gate, w_up, ffn_conv_w, ffn_conv_b, w_down, final_norm):
    weights = (norm1, w_in, sb_bias, ssd_conv_w, ssd_conv_b, dt_bias, a_log, d_skip, ssd_norm,
               pool_w, pool_scale, w_out, norm2, w_gate, w_up, ffn_conv_w, ffn_conv_b, w_down)
    y_prompt, (k_p, v_p, ssm_p, conv_p, pool_p, ffn_p) = run_trunk(
        x_prompt, 0, None, None, None, None, None, None, None, weights, final_norm)
    y_sample, (k_s, v_s, ssm_s, conv_s, pool_s, ffn_s) = run_trunk(
        x_sample, PAST_LEN, cache_k, cache_v, page_table, state_ssm, state_ssm_conv, state_pool,
        state_ffn_conv, weights, final_norm)
    return (y_prompt, y_sample, k_p, v_p, ssm_p, conv_p, pool_p, ffn_p,
            k_s, v_s, ssm_s, conv_s, pool_s, ffn_s)


_drawn_inputs = setup_inputs


def setup_inputs(seed=0):
    import zlib

    import numpy as np

    out = dict(_drawn_inputs(seed))
    spreads = {}
    factors = {'ssd_norm': 5.981,
     'pool_scale': 23.289,
     'norm2': 2.669,
     'ffn_conv_b': 7.301,
     'final_norm': 7.966,
     'cache_k': 6.45,
     'cache_v': 4.907,
     'sb_bias': 5.585}
    for name, (base, spread) in spreads.items():
        noise = np.random.default_rng([zlib.crc32(name.encode()), seed]).standard_normal(out[name].shape)
        drawn = base * np.exp(spread * noise) if base else spread * noise
        out[name] = __import__('jax').numpy.asarray(drawn.astype(out[name].dtype))
    for name, factor in factors.items():
        out[name] = (out[name] * factor).astype(out[name].dtype)
    return out
```

```python
import concourse.bass as bass
from concourse import mybir
from contextlib import ExitStack

F32 = mybir.dt.float32
F32R = mybir.dt.float32r
I32 = mybir.dt.int32
ALU = mybir.AluOpType
ACT = mybir.ActivationFunctionType
AX = mybir.AxisListType
ds = bass.ds

P = 128
D = 2048
DEPTH = 2
SEQ = 256
NB = 8
NT = 8
PAST = 2048
PAGE = 128
PAGES = PAST // PAGE
SAMP = NB * NT
TOK = SEQ + SAMP
KT = D // P
SBW = 512
SBH = 8
SBT = SBW // P
DH = 64
SSW = 1024
SSH = 16
SST = SSW // P
NG = 2
NS = 128
CVD = SSW + 2 * NG * NS
CVT = CVD // P
CVK = 4
POOLW = 512
PLT = POOLW // P
WINS = (2, 4, 8, 16)
PH = 15
FF = 5632
FT = FF // P
FK = 3
EPS = 1e-6
DTC = 3 * SBW + SSW + CVD
XPC = DTC + SSH
ZC = 3 * SBW
XBC = ZC + SSW
NEG = -1.0e30

PARTS = (16, 16, 12)

B_XBC, B_QKV, B_Z, B_XP, B_OUT = 0, 3, 6, 8, 9
B_PART = []
_b = 13
for _t in PARTS:
    B_PART.append((_b, _b + _t // 2))
    _b += _t // 2 + 4
BODIES = _b

M_NORM1, M_IN, M_ATTN, M_MIX, M_OUT, M_NORM2, M_FFN = 1, 2, 3, 4, 5, 6, 7
MEETS = 7

C_N1, C_N2, C_CW, C_CB, C_SN, C_PS = 0, 16, 32, 80, 92, 100
C_FW, C_FB, NPAR = 104, 236, 280

K_ID, K_GE, K_LE, K_ONE, K_NEG, K_SLE, K_SONE, K_SNEG, K_CNT, K_SEQ, K_HEAD, K_TOK, NCON = (
    0, 128, 256, 384, 512, 896, 960, 1024, 1088, 1152, 1160, 1168, 1176)


def build(nc, a, o):
    with ExitStack() as ctx:
        at = [16512]

        def sb_at(name, shape, dt, offset):
            return nc.alloc_sbuf_tensor_at(name, shape, dt, offset=offset)

        def size(shape):
            n = 4
            for s in shape[1:]:
                n *= s
            return n

        def sb(name, shape, dt=F32):
            off = at[0]
            at[0] += (size(shape) + 31) // 32 * 32
            return sb_at(name, shape, dt, off)

        def sem(name):
            return ctx.enter_context(nc.semaphore(name))

        x = sb("x", [P, KT, TOK])
        hh_at = at[0]
        hh = sb("hh", [P, KT, TOK], F32R)
        hl_at = at[0]
        hl = sb("hl", [P, KT, TOK], F32R)
        ah_at = at[0]
        ah = sb("ah", [P, KT, TOK], F32R)
        al_at = at[0]
        al = sb("al", [P, KT, TOK], F32R)
        raw_at = at[0]
        raw = sb("raw", [P, 4, 8, 256])
        w_at = at[0]
        wh = sb("wh", [P, 2, 8, 256], F32R)
        wl = sb("wl", [P, 2, 8, 256], F32R)
        con = sb("con", [P, NCON])
        par = sb("par", [P, NPAR])
        fgain = sb("fgain", [P, KT])
        hbias = sb("hbias", [P, SBH])
        bias64 = sb("bias64", [P, SBH * NT])
        dskip = sb("dskip", [P, SST])
        skips = sb("skips", [P, SSH])
        dtb = sb("dtb", [SSH, 2])
        ext = sb("ext", [P, 2, SEQ + CVK - 1 + NB * (NT + CVK - 1)])
        rstd = sb("rstd", [P, TOK])
        hist_c = sb("hist_c", [P, CVT, 24])
        tail_c = sb("tail_c", [P, CVT, 27])
        wdt_raw = sb("wdt_raw", [P, KT, SSH])
        wdt_hi = sb("wdt_hi", [P, KT, SSH], F32R)
        wdt_lo = sb("wdt_lo", [P, KT, SSH], F32R)
        dtT = sb("dtT", [SSH, 2, TOK])
        pages = sb("pages", [1, NB * PAGES], I32)
        xc_at = at[0]
        xc = sb("xc", [P, CVT, TOK])
        xp_at = at[0]
        XPL = SEQ + PH + NB * (NT + PH)
        xp = sb("xp", [P, PLT, XPL])
        assert at[0] <= nc.sbuf_usable_end, at[0]

        sb_qkv = sb_at("qkv", [P, 3 * SBT, TOK], F32, ah_at)
        q, k, v = (sb_qkv[:, i * SBT:(i + 1) * SBT, :] for i in range(3))
        z = sb_at("z", [P, SST, TOK], F32, ah_at + 15360)
        zz = sb_at("zz", [P, PAGES, SBH * NT], F32, ah_at + 25600)
        sp = sb_at("sp", [P, PAGES, SBH * NT], F32, ah_at + 25600 + 4096)
        rs = sb_at("rs", [P, PAGES, SBH * NT], F32, ah_at + 25600 + 8192)
        sq = sb_at("sq", [P, KT, TOK], F32, ah_at)
        prow = sb_at("prow", [P, 3, P], F32, al_at)
        crow = sb_at("crow", [24, CVD], F32, al_at + 1536)
        plrow = sb_at("plrow", [120, POOLW], F32, al_at + 1536 + 6144)
        frow = sb_at("frow", [48, FF // 2], F32, al_at)
        v_tok = sb_at("v_tok", [P, 3, SBW], F32, hh_at + 4 * TOK * 4)
        k_tok = sb_at("k_tok", [P, 3, SBW], F32, hh_at + 4 * TOK * 4 + 6144)
        qd = sb_at("qd", [P, SBT, NB, 2, NT], F32, hh_at + 4 * TOK * 4 + 12288)
        kT = sb_at("kT", [P, 2, SBW], F32, hl_at + 4 * TOK * 4)
        zn = sb_at("zn", [SAMP, SBH, SAMP], F32, hl_at + 4 * TOK * 4 + 4096)
        spn = sb_at("spn", [SAMP, SBH, SAMP], F32, hl_at + 4 * TOK * 4 + 6144)
        za = sb_at("za", [P, PAGES, SBH * NT], F32, hl_at + 4 * TOK * 4 + 8192)
        o_rows = sb_at("o_rows", [SBH * NT, SBW], F32, hl_at + 4 * TOK * 4 + 12288)
        znb = sb_at("znb", [SAMP, SBH * NT], F32, hl_at + 4 * TOK * 4 + 14336)
        kring = sb_at("kring", [P, PAGES, SBW], F32, raw_at)
        vring = sb_at("vring", [P, PAGES, SBW], F32, w_at)
        y = sb_at("y", [P, SST, TOK], F32, w_at)
        xtok = sb_at("xtok", [P, SSW + NG * NS], F32, w_at + 10240)
        xw = sb_at("xw", [P, SSW], F32, w_at + 15360)
        s1T = sb_at("s1T", [P, SSW], F32, w_at + 19456)
        sbT = s1T
        snat = sb_at("snat", [P, SST, NS], F32, w_at + 23552)
        snew = sb_at("snew", [P, SST, NS], F32, w_at + 27648)
        seg = sb_at("seg", [P, 4, P], F32, ah_at)
        wts = sb_at("wts", [P, 4, P], F32, ah_at + 2048)
        cs = sb_at("cs", [P, 4, P], F32, ah_at + 4096)
        csS = sb_at("csS", [P, SSH, SAMP], F32, ah_at + 6144)
        cbm = sb_at("cbm", [P, NG, P], F32, ah_at + 10240)
        tk = sb_at("tk", [P, 8, SSH], F32, ah_at + 11264)
        dec = sb_at("dec", [P, SST, 10], F32, ah_at + 11776)
        cend = sb_at("cend", [SSH, 10], F32, ah_at + 12096)
        bm = sb_at("bm", [SAMP, NG * NS], F32, ah_at + 12288)
        sel = sb_at("sel", [SSH, SST, P], F32, ah_at + 25600)
        ctail = sb_at("ctail", [27, CVD], F32, ah_at + 29696)
        sqy = sb_at("sqy", [P, SST, TOK], F32, w_at + 10240)
        p1 = sb_at("p1", [P, XPL], F32, ah_at)
        p2 = sb_at("p2", [P, XPL], F32, ah_at + 1920)
        pdiff = sb_at("pdiff", [P, PLT, TOK], F32, ah_at + 3840)
        poolw = sb_at("poolw", [P, PLT, P], F32, ah_at + 8960)
        ptailP = sb_at("ptailP", [PH, POOLW], F32, ah_at + 11008)
        ptail = sb_at("ptail", [P, POOLW], F32, ah_at + 13056)
        ptmp = sb_at("ptmp", [P, PLT, NB * PH], F32, ah_at + 25600)
        hist_f = sb_at("hist_f", [P, FT, 16], F32, xc_at)
        tail_f = sb_at("tail_f", [P, FT, 18], F32, xc_at + 2816)
        gc = sb_at("gc", [P, 2, TOK], F32, xc_at + 2816 + 3168)
        ftail = sb_at("ftail", [18, FF], F32, ah_at)
        xrow = sb_at("xrow", [P, 3, D], F32, ah_at)
        frows = sb_at("frows", [KT, P], F32, xc_at)
        xout = xrow

        ps = [ctx.enter_context(nc.psum_tensor(f"ps{i}", [P, 512], F32)) for i in range(8)]

        ident = con[:, K_ID:K_ID + P]
        tri_ge = con[:, K_GE:K_GE + P]
        tri_le = con[:, K_LE:K_LE + P]
        ones = con[:, K_ONE:K_ONE + P]

        at_stage = {n: sem(f"{n}_at_stage") for n in ("pe", "act", "dve", "pool")}
        raw_loaded = [sem(f"raw_loaded{i}") for i in range(4)]
        hi_done, lo_done, unit_done, group_out = sem("hi_done"), sem("lo_done"), sem("unit_done"), sem("group_out")
        conv_done, silu_done, part_ready = sem("conv_done"), sem("silu_done"), sem("part_ready")
        pages_loaded, first_loaded, first_T, first_out = (sem("pages_loaded"), sem("first_loaded"), sem("first_T"),
                                                          sem("first_out"))
        last_T, last_out, last_stored, root_taken = sem("last_T"), sem("last_out"), sem("last_stored"), sem("root_taken")
        rows_loaded, rows_T, par_out = sem("rows_loaded"), sem("rows_T"), sem("par_out")
        frow_loaded, frow_T = sem("frow_loaded"), sem("frow_T")
        h_hi, squares, sq_acc, sq_sum, mean_sq, root = (sem("h_hi"), sem("squares"), sem("sq_acc"), sem("sq_sum"),
                                                        sem("mean_sq"), sem("root"))
        wdt_split, wdt_ready, dt_mm = sem("wdt_split"), sem("wdt_ready"), sem("dt_mm")
        tok_T, tok_out, kv_stored, q_ready = sem("tok_T"), sem("tok_out"), sem("kv_stored"), sem("q_ready")
        z_mm, z_out, z_abs, z_log, z_sp, s_mm, z_arg, z_w = (
            sem("z_mm"), sem("z_out"), sem("z_abs"), sem("z_log"), sem("z_sp"), sem("s_mm"), sem("z_arg"), sem("z_w"))
        o_mm, o_hi, o_out = sem("o_mm"), sem("o_hi"), sem("o_out")
        o_masked, o_fold = sem("o_masked"), sem("o_fold")
        k_loaded = [sem(f"k_loaded{i}") for i in range(4)]
        v_loaded = sem("v_loaded")
        k_T, kT_out, z_page = sem("k_T"), sem("kT_out"), sem("z_page")
        sel_loaded, dt_abs, dt_log, cend_sum, cend_exp, dec_mm, dec_out = (
            sem("sel_loaded"), sem("dt_abs"), sem("dt_log"), sem("cend_sum"), sem("cend_exp"), sem("dec_mm"),
            sem("dec_out"))
        ctail_T, ctail_out = sem("ctail_T"), sem("ctail_out")
        blk_T, blk_tok, blk_cum, blk_end, blk_exp, blk_xw = (
            sem("blk_T"), sem("blk_tok"), sem("blk_cum"), sem("blk_end"), sem("blk_exp"), sem("blk_xw"))
        c_mm, c_seg, c_exp, c_w, y_mm, y_out = (sem("c_mm"), sem("c_seg"), sem("c_exp"), sem("c_w"), sem("y_mm"),
                                                sem("y_out"))
        st_mm, st_new = sem("st_mm"), sem("st_new")
        s_loaded, s_stored, s_T, s_Tout, s_mm2, s_new = (sem("s_loaded"), sem("s_stored"), sem("s_T"), sem("s_Tout"),
                                                         sem("s_mm2"), sem("s_new"))
        y_gated, y_sq, y_acc, y_sum, y_ms, y_root, y_normed, y_hi = (
            sem("y_gated"), sem("y_sq"), sem("y_acc"), sem("y_sum"), sem("y_ms"), sem("y_root"), sem("y_normed"),
            sem("y_hi"))
        poolw_loaded, p_diff, p_mm, p_hi, ptail_T, ptail_out, ptail_in = (
            sem("poolw_loaded"), sem("p_diff"), sem("p_mm"), sem("p_hi"), sem("ptail_T"), sem("ptail_out"),
            sem("ptail_in"))
        tail_stored, ftail_T, ftail_out = sem("tail_stored"), sem("ftail_T"), sem("ftail_out")

        passed = sem("passed")

        block = ctx.enter_context(nc.Block())

        def alone(eng):
            eng.sem_inc(passed, 1)

        def meet(eng, me, stage):
            if not isinstance(stage, int):
                alone(eng)
            eng.drain().then_inc(at_stage[me], 1)
            for other in at_stage:
                if other != me:
                    eng.wait_ge(at_stage[other], stage)
            if not isinstance(stage, int):
                alone(eng)

        def stage(l, m):
            return l * MEETS + (m + 1)

        def tokens(blk):
            return (blk * P, P) if blk < 2 else (SEQ, SAMP)

        def wrow(name, l, rows):
            return a[name][l].rearrange(rows, p=P)

        @block.sync
        def _(sync):
            def unit(l, body, s, w, row, rows, col):
                sync.wait_ge(lo_done, (l * BODIES + body) * 4 + (s + 1))
                sync.dma_start(raw[:, s, 0:rows, :],
                               w.rearrange("l (k p) n -> l p k n", p=P)[l, :, row:row + rows, ds(col, 256)]
                               ).then_inc(raw_loaded[s], 16)

            def body(l, b, w, row, rows, col0, col1, w1=None):
                for s in range(4):
                    unit(l, b, s, w if s < 2 or w1 is None else w1, row + (s % 2) * rows, rows,
                         col0 if s < 2 else col1)

            sync.dma_start(pages[:], a["page_table"].rearrange("b p -> (b p)").unsqueeze(0)
                           ).then_inc(pages_loaded, 16)
            sync.wait_ge(pages_loaded, 16)
            with sync.Fori(0, DEPTH) as l:
                with sync.Fori(0, 3) as i:
                    body(l, i + B_XBC, a["w_in"], 0, 8, i * 512 + XBC, i * 512 + (XBC + 256))
                with sync.Fori(0, 3) as i:
                    body(l, i + B_QKV, a["w_in"], 0, 8, i * 512, i * 512 + 256)
                with sync.Fori(0, 2) as i:
                    body(l, i + B_Z, a["w_in"], 0, 8, i * 512 + ZC, i * 512 + (ZC + 256))
                body(l, B_XP, a["w_in"], 0, 8, XPC, XPC + 256)
                sync.wait_ge(at_stage["pe"], stage(l, M_IN))
                alone(sync)
                sync.wait_ge(at_stage["dve"], stage(l, M_IN))
                alone(sync)

                def keys(b, slots_free):
                    for c in range(4):
                        sync.wait_ge(k_T, slots_free + (4 * c + 4))
                        alone(sync)
                        for j in range(4 * c, 4 * c + 4):
                            page = sync.value_load(pages[0:1, ds(b * PAGES + j, 1)], min_val=0,
                                                   max_val=a["cache_k"].shape[1] - 1)
                            sync.dma_start(kring[:, j, :], a["cache_k"][l, page].rearrange("s h d -> s (h d)")
                                           ).then_inc(k_loaded[c], 16)

                with sync.Fori(0, NB) as b:
                    keys(b, (l * NB + b) * PAGES)
                sync.wait_ge(at_stage["pe"], stage(l, M_ATTN))
                alone(sync)
                with sync.Fori(0, 4) as i:
                    body(l, i + B_OUT, a["w_out"], 0, 8, i * 512, i * 512 + 256)
                t0 = 0
                for part, tiles in enumerate(PARTS):
                    up, down = B_PART[part]
                    with sync.Fori(0, tiles // 2) as i:
                        body(l, i + up, a["w_gate"], 0, 8, i * 256 + t0 * P, i * 256 + t0 * P, a["w_up"])
                    with sync.Fori(0, 4) as i:
                        body(l, i + down, a["w_down"], t0, tiles // 2, i * 512, i * 512 + 256)
                    t0 += tiles

        @block.gpsimd
        def _(pool):
            for dst, src in (
                (con[:], a["con"]),
                (frows[:], a["final_norm"].rearrange("(t p) -> t p", p=P)),
                (xrow[:, 0, :], a["x_prompt"][0, 0:P, :]),
                (xrow[:, 1, :], a["x_prompt"][0, P:SEQ, :]),
                (xrow[0:SAMP, 2, :], a["x_sample"].rearrange("b t d -> (b t) d")),
            ):
                pool.dma_start(dst, src).then_inc(first_loaded, 16)
            pool.wait_ge(pages_loaded, 16)
            meet(pool, "pool", 1)

            def square():
                pool.tensor_tensor(sq[:].rearrange("p k t -> p (k t)"), x[:].rearrange("p k t -> p (k t)"),
                                   x[:].rearrange("p k t -> p (k t)"), ALU.mult).then_inc(squares, 1)

            with pool.Fori(0, DEPTH) as l:
                for dst, src in (
                    (prow[0:16, 0, :], wrow("norm1", l, "(t p) -> t p")),
                    (prow[16:32, 0, :], wrow("norm2", l, "(t p) -> t p")),
                    (prow[32:80, 0, :], wrow("ssd_conv_w", l, "k (t p) -> (k t) p")),
                    (prow[80:92, 0, :], wrow("ssd_conv_b", l, "(t p) -> t p")),
                    (prow[92:100, 0, :], wrow("ssd_norm", l, "(t p) -> t p")),
                    (prow[100:104, 0, :], wrow("pool_scale", l, "(t p) -> t p")),
                    (prow[0:88, 1, :], wrow("ffn_conv_w", l, "k (t p) -> (k t) p")[0:88, :]),
                    (prow[0:44, 2, :], wrow("ffn_conv_w", l, "k (t p) -> (k t) p")[88:132, :]),
                    (prow[44:88, 2, :], wrow("ffn_conv_b", l, "(t p) -> t p")),
                    (crow[:], a["state_ssm_conv"][l].rearrange("b k c -> (b k) c")),
                    (plrow[:], a["state_pool"][l].rearrange("b k c -> (b k) c")),
                    (hbias[:], a["sb_bias"][l].unsqueeze(0).broadcast_to([P, SBH])),
                    (skips[:], a["d_skip"][l].unsqueeze(0).broadcast_to([P, SSH])),
                    (dtb[:, 0:1], a["dt_bias"][l].unsqueeze(1)),
                    (dtb[:, 1:2], a["a_log"][l].unsqueeze(1)),
                    (wdt_raw[:], a["w_in"].rearrange("l (k p) n -> l p k n", p=P)[l, :, :, DTC:DTC + SSH]),
                ):
                    pool.dma_start(dst, src).then_inc(rows_loaded, 16)
                square()
                meet(pool, "pool", stage(l, M_NORM1))
                meet(pool, "pool", stage(l, M_IN))

                pool.wait_ge(tok_out, l * 6 + 6)
                alone(pool)
                for name, src in (("k", k_tok), ("v", v_tok)):
                    pool.dma_start(o[f"new_{name}_prompt"][l, 0].rearrange("(c p) h d -> p c (h d)", p=P),
                                   src[:, 0:2, :]).then_inc(kv_stored, 16)
                    pool.dma_start(o[f"new_{name}_sample"][l].rearrange("b t h d -> (b t) (h d)"),
                                   src[0:SAMP, 2, :]).then_inc(kv_stored, 16)
                with pool.Fori(0, NB) as b:
                    pool.wait_ge(o_mm, b + l * 16 + 8)
                    alone(pool)
                    for j in range(PAGES):
                        page = pool.value_load(pages[0:1, ds(b * PAGES + j, 1)], min_val=0,
                                               max_val=a["cache_v"].shape[1] - 1)
                        pool.dma_start(vring[:, j, :], a["cache_v"][l, page].rearrange("s h d -> s (h d)")
                                       ).then_inc(v_loaded, 16)
                pool.wait_ge(kv_stored, l * 64 + 64)
                alone(pool)
                meet(pool, "pool", stage(l, M_ATTN))

                pool.dma_start(sel[:], a["sel"]).then_inc(sel_loaded, 16)
                pool.wait_ge(ctail_out, l * 3 + 3)
                alone(pool)
                pool.dma_start(o["new_ssm_conv_prompt"][l, 0], ctail[0:3, :]).then_inc(tail_stored, 16)
                pool.dma_start(o["new_ssm_conv_sample"][l].rearrange("b k c -> (b k) c"), ctail[3:27, :]
                               ).then_inc(tail_stored, 16)
                pool.wait_ge(st_new, l * 2 + 2)
                alone(pool)
                pool.dma_start(o["new_ssm_prompt"][l, 0].rearrange("(j e) p n -> (e p) j n", e=2), snew[:]
                               ).then_inc(s_stored, 16)
                with pool.Fori(0, NB) as b:
                    pool.dma_start(snat[:], a["state_ssm"][l, b].rearrange("(j e) p n -> (e p) j n", e=2)
                                   ).then_inc(s_loaded, 16)
                    pool.wait_ge(s_new, l * NB + b + 1)
                    alone(pool)
                    pool.dma_start(o["new_ssm_sample"][l, b].rearrange("(j e) p n -> (e p) j n", e=2), snew[:]
                                   ).then_inc(s_stored, 16)
                pool.wait_ge(y_gated, l + 1)
                alone(pool)
                pool.tensor_tensor(sqy[:].rearrange("p k t -> p (k t)"), y[:].rearrange("p k t -> p (k t)"),
                                   y[:].rearrange("p k t -> p (k t)"), ALU.mult).then_inc(y_sq, 1)
                pool.dma_start(poolw[:], a["pool_w"][l].rearrange("g c d -> c g d")).then_inc(poolw_loaded, 16)
                pool.wait_ge(ptail_out, l * 2 + 2)
                alone(pool)
                pool.dma_start(o["new_pool_prompt"][l, 0], ptailP[:]).then_inc(tail_stored, 16)
                pool.dma_start(o["new_pool_sample"][l].rearrange("b k c -> (b k) c"), ptail[0:NB * PH, :]
                               ).then_inc(tail_stored, 16)
                pool.wait_ge(s_stored, (l * (NB + 1) + NB + 1) * 16)
                alone(pool)
                pool.wait_ge(tail_stored, l * 96 + 64)
                alone(pool)
                meet(pool, "pool", stage(l, M_MIX))
                meet(pool, "pool", stage(l, M_OUT))
                for half in range(2):
                    pool.dma_start(frow[32 * half:32 * half + 16, :],
                                   a["state_ffn_conv"][l].rearrange("b k c -> (b k) c")[
                                       :, half * (FF // 2):(half + 1) * (FF // 2)]).then_inc(frow_loaded, 16)
                square()
                meet(pool, "pool", stage(l, M_NORM2))
                pool.wait_ge(ftail_out, l * 11 + 11)
                alone(pool)
                pool.dma_start(o["new_ffn_conv_prompt"][l, 0], ftail[0:2, :]).then_inc(tail_stored, 16)
                pool.dma_start(o["new_ffn_conv_sample"][l].rearrange("b k c -> (b k) c"), ftail[2:18, :]
                               ).then_inc(tail_stored, 16)
                pool.wait_ge(tail_stored, l * 96 + 96)
                alone(pool)
                meet(pool, "pool", stage(l, M_FFN))
            square()
            pool.wait_ge(last_out, 12)
            pool.dma_start(o["y_prompt"][0].rearrange("(c p) d -> p c d", p=P), xrow[:, 0:2, :]
                           ).then_inc(last_stored, 16)
            pool.dma_start(o["y_sample"].rearrange("b t d -> (b t) d"), xrow[0:SAMP, 2, :]).then_inc(last_stored, 16)
            pool.wait_ge(last_stored, 32)

        @block.scalar
        def _(act):
            def hi(l, body, s, rows=8):
                act.wait_ge(raw_loaded[s], (l * BODIES + body + 1) * 16)
                act.wait_ge(unit_done, (l * BODIES + body) * 4 + (s + 1))
                act.activation(wh[:, s % 2, 0:rows, :], raw[:, s, 0:rows, :], ACT.Copy).then_inc(hi_done, 1)

            def body(l, b, before, after, rows=8):
                hi(l, b, 0, rows)
                hi(l, b, 1, rows)
                if before:
                    before()
                hi(l, b, 2, rows)
                hi(l, b, 3, rows)
                if after:
                    after()

            def bodies(l, base, n, pending, task, rows=8):
                body(l, base, pending, task and (lambda: task(0, 0)), rows)
                if n > 1:
                    with act.Fori(1, n) as i:
                        body(l, i + base, task and (lambda: task(i - 1, 1)), task and (lambda: task(i, 0)), rows)
                return task and (lambda: task(n - 1, 1))

            def norm_high(l, col):
                for t in range(KT):
                    act.activation(hh[:, t, :], x[:, t, :], ACT.Copy, scale=par[:, col + t:col + t + 1]
                                   ).then_inc(h_hi, 1)

            def norm_root(n):
                act.wait_ge(mean_sq, n)
                act.activation(rstd[:], rstd[:], ACT.Sqrt).then_inc(root, 1)

            def log1p_exp(ap):
                act.activation(ap, ap, ACT.Exp, scale=-1.0)
                act.drain()
                return act.activation(ap, ap, ACT.Ln, bias=1.0)

            act.sem_inc(kT_out, 2)
            meet(act, "act", 1)
            with act.Fori(0, DEPTH) as l:
                act.wait_ge(par_out, l + 1)
                norm_high(l, C_N1)
                act.activation(wdt_hi[:], wdt_raw[:], ACT.Copy).then_inc(wdt_split, 1)
                norm_root(l * 2 + 1)
                meet(act, "act", stage(l, M_NORM1))

                def silu_xbc(i, g):
                    act.wait_ge(conv_done, l * 32 + i * 2 + (g + 1))
                    t = xc[:, ds(i * 4 + 2 * g, 2), :]
                    act.activation(t, t, ACT.Silu)

                def silu_z(i, g):
                    act.wait_ge(conv_done, l * 32 + i * 2 + (g + 7))
                    t = z[:, ds(i * 4 + 2 * g, 2), :]
                    act.activation(t, t, ACT.Silu)

                left = bodies(l, B_XBC, 3, None, silu_xbc)
                left = bodies(l, B_QKV, 3, left, None)
                left = bodies(l, B_Z, 2, left, silu_z)
                left = bodies(l, B_XP, 1, left, None)
                meet(act, "act", stage(l, M_IN))

                def z_logs(n, ap):
                    act.wait_ge(z_abs, l * 17 + n + 1)
                    log1p_exp(ap).then_inc(z_log, 1)

                def z_weights(n, ap):
                    act.wait_ge(z_arg, l * 17 + n + 1)
                    act.activation(ap, ap, ACT.Exp).then_inc(z_w, 1)

                def head(buf, n):
                    return buf[:].rearrange("p a c -> p (a c)")[:, 512 * (n % 2):512 * (n % 2) + 384]

                z_logs(0, head(za, 0))
                for n in range(8):
                    if n < 7:
                        z_logs(n + 1, head(za, n + 1))
                    else:
                        z_logs(8, za[0:SAMP, 0:8, :])
                    z_weights(n, head(zz, n))
                    r = slice(DH * (n % 2), DH * (n % 2) + DH)
                    act.wait_ge(o_mm, l * 16 + n + 1)
                    act.activation(hh[r, n // 2, 0:SEQ], ps[6 + n % 2][r, 0:SEQ], ACT.Copy).then_inc(o_hi, 1)
                z_weights(8, zn[:])

                def page_copies(b, between={}):
                    for p in range(PAGES):
                        act.wait_ge(k_T, (l * NB + b) * PAGES + (p + PAGES + 1))
                        act.wait_ge(z_page, (l * NB + b) * PAGES + (p + 1))
                        act.activation(kT[:, p % 2, :], ps[4 + p % 2][:], ACT.Copy).then_inc(kT_out, 1)
                        if p in between:
                            between[p]()

                def weigh(b):
                    z_weights(b + 9, zz[:])

                def outputs(b):
                    act.wait_ge(o_fold, b + (l * NB + 1))
                    act.activation(hh[:, 0:SBT, ds(b * NT + SEQ, NT)],
                                   ps[7][:, 0:SBT * NT].rearrange("p (j t) -> p j t", j=SBT), ACT.Copy
                                   ).then_inc(o_hi, 1)

                page_copies(0)
                page_copies(1, {2: lambda: z_logs(9, za[:]), 11: lambda: weigh(0)})
                with act.Fori(1, NB - 1) as b:
                    page_copies(b + 1, {1: lambda: outputs(b - 1), 2: lambda: z_logs(b + 9, za[:]),
                                        11: lambda: weigh(b)})
                outputs(NB - 2)
                z_logs(NB + 8, za[:])
                weigh(NB - 1)
                outputs(NB - 1)
                meet(act, "act", stage(l, M_ATTN))

                act.wait_ge(dt_abs, l + 1)
                act.activation(dtb[:, 1:2], dtb[:, 1:2], ACT.Exp)
                log1p_exp(dtT[:, 1, :]).then_inc(dt_log, 1)
                act.wait_ge(cend_sum, l + 1)
                act.activation(cend[:], cend[:], ACT.Exp).then_inc(cend_exp, 1)
                for blk in range(3):
                    t0, T = tokens(blk)
                    act.wait_ge(blk_end, l * 3 + blk + 1)
                    act.activation(tk[0:T, 3, :], tk[0:T, 3, :], ACT.Exp).then_inc(blk_exp, 1)
                    for j in range(4):
                        act.wait_ge(c_seg, l * 12 + blk * 4 + j + 1)
                        mm = act.activation(seg[0:T, :, 0:T], seg[0:T, :, 0:T], ACT.Exp)
                        if blk:
                            dst = cs[:] if blk == 1 else csS[:, 4 * j:4 * j + 4, :]
                            mm = act.activation(dst, ps[5 + j % 2][:, 0:4 * T].rearrange("p (h t) -> p h t", h=4),
                                                ACT.Exp)
                        mm.then_inc(c_exp, 1)
                act.wait_ge(y_ms, l + 1)
                act.activation(rstd[:], rstd[:], ACT.Sqrt).then_inc(y_root, 1)
                act.wait_ge(y_normed, l + 1)
                act.activation(hh[:, SBT:SBT + SST, :], y[:], ACT.Copy).then_inc(y_hi, 1)
                act.wait_ge(p_mm, l + 1)
                for g in range(PLT):
                    mm = act.activation(hh[:, SBT + SST + g, :], ps[g][:, 0:TOK], ACT.Copy,
                                        scale=par[:, C_PS + g:C_PS + g + 1])
                mm.then_inc(p_hi, 1)
                meet(act, "act", stage(l, M_MIX))

                bodies(l, B_OUT, 4, None, None)
                meet(act, "act", stage(l, M_OUT))
                norm_high(l, C_N2)
                norm_root(l * 2 + 2)
                meet(act, "act", stage(l, M_NORM2))
                done = 10
                for part, tiles in enumerate(PARTS):
                    up, down = B_PART[part]

                    def silu_gate(i, g, done=done):
                        if g == 0:
                            act.wait_ge(conv_done, l * 32 + i + (done + 1))
                            act.activation(gc[:], gc[:], ACT.Silu).then_inc(silu_done, 1)

                    bodies(l, up, tiles // 2, None, silu_gate)
                    bodies(l, down, 4, None, None, tiles // 2)
                    done += tiles // 2
                meet(act, "act", stage(l, M_FFN))
            norm_root(2 * DEPTH + 1)

        @block.tensor
        def _(pe):
            def products(l, base, n, hi, lo, half=8):
                def one(b):
                    g0 = (l * BODIES + b)
                    for s in range(4):
                        if s % 2 == 0:
                            pe.wait_ge(group_out, g0 * 2 + (s // 2 + 1))
                        if s % 2 == 1 and base in DOWN:
                            pe.wait_ge(part_ready, l * 3 + DOWN.index(base) + 1)
                        pe.wait_ge(lo_done, g0 * 4 + (s + 5))
                        for t in range(2):
                            for kk in range(half):
                                row = (s % 2) * half + kk
                                out = ps[2 * (s // 2) + t][:, 0:TOK]
                                w = slice(t * P, t * P + P)
                                first, last = row == 0, row == 2 * half - 1
                                pe.matmul(out, wh[:, s % 2, kk, w], hi[:, row, :], start=first, stop=False)
                                pe.matmul(out, wh[:, s % 2, kk, w], lo[:, row, :], start=False, stop=False)
                                mm = pe.matmul(out, wl[:, s % 2, kk, w], hi[:, row, :], start=False, stop=last)
                        mm.then_inc(unit_done, 1)

                if n == 1:
                    one(base)
                else:
                    with pe.Fori(0, n) as i:
                        one(i + base)

            DOWN = [down for _, down in B_PART]

            def norm_sum(n):
                pe.wait_ge(sq_acc, n)
                pe.matmul(ps[7][:, 0:TOK], ones, rstd[:], start=True, stop=True).then_inc(sq_sum, 1)

            pe.sem_inc(unit_done, 2)
            pe.sem_inc(k_T, PAGES)
            pe.sem_inc(z_page, 2)
            pe.wait_ge(first_loaded, 80)
            pe.transpose(ps[7][:, 0:KT], frows[:], ident[0:KT, 0:KT]).then_inc(first_T, 1)
            for n in range(12):
                c, j = n // 4, n % 4
                T = P if c < 2 else SAMP
                if c:
                    pe.wait_ge(first_out, n - 2)
                for i in range(4):
                    mm = pe.transpose(ps[j][:, i * T:(i + 1) * T], xrow[0:T, c, (4 * j + i) * P:(4 * j + i + 1) * P],
                                      ident[0:T, 0:T])
                mm.then_inc(first_T, 1)
            meet(pe, "pe", 1)

            with pe.Fori(0, DEPTH) as l:
                pe.wait_ge(rows_loaded, l * (16 * 16) + 16 * 16)
                for c, (n, col) in enumerate(((104, 0), (88, 104), (88, 192))):
                    mm = pe.transpose(ps[4][:, col:col + n], prow[0:n, c, :], ident[0:n, 0:n])
                mm.then_inc(rows_T, 1)
                for t in range(CVT):
                    mm = pe.transpose(ps[5][:, t * 24:t * 24 + 24], crow[:, t * P:(t + 1) * P], ident[0:24, 0:24])
                mm.then_inc(rows_T, 1)
                for t in range(PLT):
                    mm = pe.transpose(ps[6][:, t * 120:t * 120 + 120], plrow[:, t * P:(t + 1) * P],
                                      ident[0:120, 0:120])
                mm.then_inc(rows_T, 1)
                norm_sum(l * 2 + 1)
                meet(pe, "pe", stage(l, M_NORM1))

                pe.wait_ge(wdt_ready, l + 1)
                for t in range(KT):
                    pe.matmul(ps[4][0:SSH, 0:TOK], wdt_hi[:, t, :], hh[:, t, :], start=(t == 0), stop=False)
                    pe.matmul(ps[4][0:SSH, 0:TOK], wdt_hi[:, t, :], hl[:, t, :], start=False, stop=False)
                    mm = pe.matmul(ps[4][0:SSH, 0:TOK], wdt_lo[:, t, :], hh[:, t, :], start=False,
                                   stop=(t == KT - 1))
                mm.then_inc(dt_mm, 1)
                products(l, B_XBC, 3, hh, hl)
                products(l, B_QKV, 3, hh, hl)
                products(l, B_Z, 2, hh, hl)
                products(l, B_XP, 1, hh, hl)
                meet(pe, "pe", stage(l, M_IN))

                for n in range(6):
                    c, src = n // 2, (k, v)[n % 2]
                    T = P if c < 2 else SAMP
                    if n >= 2:
                        pe.wait_ge(tok_out, l * 6 + (n - 1))
                        alone(pe)
                    for t in range(SBT):
                        mm = pe.transpose(ps[4 + n % 2][0:T, t * P:(t + 1) * P], src[:, t, c * P:c * P + T], ident)
                    mm.then_inc(tok_T, 1)

                def head_z(n):
                    if n >= 2:
                        pe.wait_ge(z_out, l * 17 + (n - 1))
                        alone(pe)
                    r, b = slice(DH * (n % 2), DH * (n % 2) + DH), ps[n % 2]
                    pe.matmul(b[:, 0:SEQ], k[r, n // 2, 0:P], q[r, n // 2, 0:SEQ], start=True, stop=True)
                    pe.matmul(b[:, SEQ:SEQ + P], k[r, n // 2, P:SEQ], q[r, n // 2, P:SEQ], start=True, stop=True
                              ).then_inc(z_mm, 1)

                def head_sums(n):
                    pe.wait_ge(z_sp, l * 17 + (n + 1))
                    if n >= 2:
                        pe.wait_ge(z_arg, l * 17 + (n - 1))
                    b = ps[2 + n % 2]
                    s_ = sp[:].rearrange("p a c -> p (a c)")[:, 512 * (n % 2):512 * (n % 2) + 384]
                    pe.matmul(b[:, 0:P], tri_ge, s_[:, 0:P], start=True, stop=True)
                    pe.matmul(b[:, P:SEQ], tri_ge, s_[:, P:SEQ], start=True, stop=False)
                    pe.matmul(b[:, P:SEQ], ones, s_[:, SEQ:384], start=False, stop=True)
                    pe.matmul(b[:, SEQ:384], tri_ge, s_[:, SEQ:384], start=True, stop=True).then_inc(s_mm, 1)

                def head_out(n):
                    pe.wait_ge(z_w, l * 17 + (n + 1))
                    if n >= 2:
                        pe.wait_ge(o_out, l * 16 + (n - 1))
                    r, b = slice(DH * (n % 2), DH * (n % 2) + DH), ps[6 + n % 2]
                    w = zz[:].rearrange("p a c -> p (a c)")[:, 512 * (n % 2):512 * (n % 2) + 384]
                    pe.matmul(b[r, 0:P], v_tok[:, 0, n * DH:(n + 1) * DH], w[:, 0:P], start=True, stop=True)
                    pe.matmul(b[r, P:SEQ], v_tok[:, 0, n * DH:(n + 1) * DH], w[:, P:SEQ], start=True, stop=False)
                    pe.matmul(b[r, P:SEQ], v_tok[:, 1, n * DH:(n + 1) * DH], w[:, SEQ:384], start=False, stop=True
                              ).then_inc(o_mm, 1)

                head_z(0)
                pe.wait_ge(tok_out, l * 6 + 6)
                alone(pe)
                for n in range(8):
                    if n < 7:
                        head_z(n + 1)
                    else:
                        pe.wait_ge(z_out, l * 17 + 7)
                        alone(pe)
                        for h in range(SBH):
                            r = slice(DH * (h % 2), DH * (h % 2) + DH)
                            mm = pe.matmul(ps[4 * (h % 2)][0:SAMP, h * SAMP:(h + 1) * SAMP], k[r, h // 2, SEQ:TOK],
                                           q[r, h // 2, SEQ:TOK], start=True, stop=True)
                        mm.then_inc(z_mm, 1)
                    head_sums(n)
                    head_out(n)
                pe.wait_ge(z_sp, l * 17 + 9)
                pe.wait_ge(z_arg, l * 17 + 7)
                alone(pe)
                pe.matmul(ps[2][0:SAMP, :], tri_ge[0:SAMP, 0:SAMP], spn[:].rearrange("p h c -> p (h c)"), start=True,
                          stop=True).then_inc(s_mm, 1)

                def page_z(b, p):
                    g = (l * NB + b) * PAGES
                    pe.wait_ge(kT_out, g + (p + 3))
                    if p == 0:
                        pe.wait_ge(z_out, b + l * 17 + 9)
                    for j in range(SBT):
                        mm = pe.matmul(ps[p // 8][:, (p % 8) * 64 + j * 16:(p % 8) * 64 + j * 16 + 16],
                                       kT[:, p % 2, j * P:(j + 1) * P],
                                       qd[:, j, ds(b, 1), :, :].rearrange("p b e t -> p (b e t)"),
                                       start=True, stop=True)
                    mm.then_inc(z_page, 1)

                def pages_z(b, between={}):
                    g = l * NB + b
                    for p in range(PAGES):
                        if p % 4 == 0:
                            pe.wait_ge(k_loaded[p // 4], g * 64 + 64)
                        pe.wait_ge(kT_out, g * PAGES + (p + 1))
                        for j in range(SBT):
                            mm = pe.transpose(ps[4 + p % 2][:, j * P:(j + 1) * P], kring[:, p, j * P:(j + 1) * P],
                                              ident)
                        mm.then_inc(k_T, 1)
                        if p:
                            page_z(b, p - 1)
                        if p in between:
                            between[p]()
                    page_z(b, PAGES - 1)

                def pages_sums(b):
                    pe.wait_ge(z_sp, b + l * 17 + 10)
                    pe.wait_ge(z_arg, b + l * 17 + 9)
                    for half in range(2):
                        pe.matmul(ps[2 + half][:], tri_ge, sp[:, 8 * half:8 * half + 8, :], start=True, stop=False)
                        mm = pe.matmul(ps[2 + half][:], ones, rs[:, 8 * half:8 * half + 8, :], start=False, stop=True)
                    mm.then_inc(s_mm, 1)

                def pages_out(b, first=False):
                    pe.wait_ge(z_w, b + l * 17 + 10)
                    pe.wait_ge(v_loaded, (l * NB + b) * 256 + 256)
                    if first:
                        pe.wait_ge(o_out, l * 16 + 7)
                    else:
                        pe.wait_ge(o_masked, b + l * NB)
                    for p in range(PAGES):
                        pe.matmul(ps[6][0:SBH * NT, :], zz[:, p, :], vring[:, p, :], start=(p == 0), stop=False)
                    pe.matmul(ps[6][0:SBH * NT, :], znb[:], v_tok[0:SAMP, 2, :], start=False, stop=True
                              ).then_inc(o_mm, 1)

                def pages_fold(b):
                    pe.wait_ge(o_masked, b + (l * NB + 1))
                    pe.wait_ge(o_out, b + (l * 16 + 8))
                    for j in range(SBT):
                        mm = pe.matmul(ps[7][:, j * NT:(j + 1) * NT], o_rows[:, j * P:(j + 1) * P],
                                       con[0:SBH * NT, K_TOK:K_TOK + NT], start=True, stop=True)
                    mm.then_inc(o_fold, 1)

                pe.wait_ge(q_ready, l + 1)
                pe.wait_ge(z_out, l * 17 + 9)
                alone(pe)
                pages_z(0)
                pe.wait_ge(z_w, l * 17 + 9)
                alone(pe)
                pages_z(1, {7: lambda: pages_sums(0)})
                pages_out(0, first=True)
                with pe.Fori(1, NB - 1) as b:
                    pages_z(b + 1, {1: lambda: pages_fold(b - 1), 7: lambda: pages_sums(b)})
                    pages_out(b)
                pages_fold(NB - 2)
                pages_sums(NB - 1)
                pages_out(NB - 1)
                pages_fold(NB - 1)
                meet(pe, "pe", stage(l, M_ATTN))

                for c in range(3):
                    for t in range(4):
                        mm = pe.transpose(ps[c][0:27, t * P:(t + 1) * P], tail_c[:, 4 * c + t, :], ident)
                    mm.then_inc(ctail_T, 1)
                pe.wait_ge(cend_exp, l + 1)
                pe.wait_ge(sel_loaded, l * 16 + 16)
                for j in range(SST):
                    mm = pe.matmul(ps[3][:, j * 10:(j + 1) * 10], sel[:, j, :], cend[:], start=True, stop=True)
                mm.then_inc(dec_mm, 1)
                pe.wait_ge(dec_out, l + 1)
                pe.wait_ge(ctail_out, l * 3 + 3)
                for blk in range(3):
                    t0, T = tokens(blk)
                    cols = slice(t0, t0 + T)
                    if blk:
                        pe.wait_ge(y_out, l * 12 + blk * 4)
                        pe.wait_ge(st_new, l * 2 + blk)
                        alone(pe)
                    for t in range(SST + NG):
                        pe.transpose(ps[t // 4][0:T, (t % 4) * P:(t % 4 + 1) * P], xc[:, t, cols], ident)
                    for i in range(2):
                        mm = pe.transpose(ps[3][0:T, i * SSH:(i + 1) * SSH], dtT[:, i, cols], ident[0:SSH, 0:SSH])
                    mm.then_inc(blk_T, 1)
                    le = tri_le if blk < 2 else con[0:T, K_SLE:K_SLE + T]
                    one = ones if blk < 2 else con[0:T, K_SONE:K_SONE + T]
                    pe.wait_ge(blk_tok, l * 3 + blk + 1)
                    alone(pe)
                    pe.matmul(ps[3][0:T, 32:48], le, tk[0:T, 1, :], start=True, stop=True)
                    pe.matmul(ps[3][0:T, 48:64], one, tk[0:T, 1, :], start=True, stop=True)
                    for g in range(NG):
                        mm = pe.matmul(ps[4][0:T, g * T:(g + 1) * T], xc[:, SST + g, cols], xc[:, SST + NG + g, cols],
                                       start=True, stop=True)
                    mm.then_inc(blk_cum, 1)
                    for j in range(4):
                        n = blk * 4 + j
                        if n >= 2:
                            pe.wait_ge(c_w, l * 12 + n - 1)
                        for i in range(4):
                            h = 4 * j + i
                            mm = pe.matmul(ps[5 + j % 2][:, i * T:(i + 1) * T],
                                           tk[0:T, 1, h:h + 1].broadcast_to([T, P]), le, start=True, stop=True)
                        mm.then_inc(c_mm, 1)
                        pe.wait_ge(c_w, l * 12 + n + 1)
                        if j >= 2:
                            pe.wait_ge(y_out, l * 12 + n - 1)
                        alone(pe)
                        for i in range(4):
                            h = 4 * j + i
                            out = ps[j % 2][DH * (i % 2):DH * (i % 2) + DH, (i // 2) * T:(i // 2 + 1) * T]
                            mm = pe.matmul(out, xtok[0:T, h * DH:(h + 1) * DH], wts[0:T, i, 0:T], start=True,
                                           stop=(blk != 1))
                            if blk == 1:
                                mm = pe.matmul(out, s1T[:, h * DH:(h + 1) * DH], cs[:, i, :], start=False, stop=True)
                        mm.then_inc(y_mm, 1)
                    if blk < 2:
                        pe.wait_ge(blk_xw, l * 3 + blk + 1)
                        pe.wait_ge(c_w, l * 12 + blk * 4 + 4)
                        if blk == 0:
                            for g, b in enumerate((2, 4)):
                                pe.matmul(ps[b][:], xtok[:, SSW + g * NS:SSW + (g + 1) * NS],
                                          xw[:, g * 512:(g + 1) * 512], start=True, stop=True)
                        for j in range(SST):
                            g = j // 4
                            mm = pe.matmul(ps[5 + g][:, (j % 4) * NS:(j % 4 + 1) * NS], xw[:, j * P:(j + 1) * P],
                                           xtok[:, SSW + g * NS:SSW + (g + 1) * NS], start=True, stop=True)
                        mm.then_inc(st_mm, 1)
                pe.wait_ge(blk_xw, l * 3 + 3)
                pe.wait_ge(y_out, l * 12 + 12)
                alone(pe)
                with pe.Fori(0, NB) as b:
                    g8 = l * NB + b
                    pe.wait_ge(s_loaded, g8 * 16 + 16)
                    for j in range(SST):
                        mm = pe.transpose(ps[j // 4][:, (j % 4) * P:(j % 4 + 1) * P], snat[:, j, :], ident)
                    mm.then_inc(s_T, 1)
                    pe.wait_ge(s_Tout, g8 + 1)
                    for j in range(SST):
                        v5 = ps[2 + j // 4][:].rearrange("p (j e t) -> p j e t", j=4, e=2)
                        pe.matmul(v5[:, j % 4, :, ds(b * NT, NT)], sbT[:, j * P:(j + 1) * P],
                                  csS[:, 2 * j:2 * j + 2, ds(b * NT, NT)], start=True, stop=True)
                    for j in range(SST):
                        g = j // 4
                        mm = pe.matmul(ps[5 + g][:, (j % 4) * NS:(j % 4 + 1) * NS], xw[0:SAMP, j * P:(j + 1) * P],
                                       bm[:, g * NS:(g + 1) * NS], start=True, stop=True)
                    mm.then_inc(s_mm2, 1)
                    pe.wait_ge(s_new, g8 + 1)
                pe.wait_ge(y_acc, l + 1)
                pe.matmul(ps[7][:, 0:TOK], ones, rstd[:], start=True, stop=True).then_inc(y_sum, 1)
                pe.wait_ge(ptail_in, l + 1)
                for t in range(PLT):
                    mm = pe.transpose(ps[4][0:PH, t * P:(t + 1) * P], xp[:, t, SEQ:SEQ + PH], ident)
                mm.then_inc(ptail_T, 1)
                for t in range(PLT):
                    mm = pe.transpose(ps[5][0:NB * PH, t * P:(t + 1) * P], ptmp[:, t, :], ident)
                mm.then_inc(ptail_T, 1)
                pe.wait_ge(poolw_loaded, l * 16 + 16)
                pe.wait_ge(p_diff, l + 1)
                for g in range(PLT):
                    mm = pe.matmul(ps[g][:, 0:TOK], poolw[:, g, :], pdiff[:, g, :], start=True, stop=True)
                mm.then_inc(p_mm, 1)
                meet(pe, "pe", stage(l, M_MIX))

                products(l, B_OUT, 4, hh, hl)
                meet(pe, "pe", stage(l, M_OUT))
                pe.wait_ge(frow_loaded, l * 32 + 32)
                alone(pe)
                for t in range(FT):
                    r = slice(32 * (t // 22), 32 * (t // 22) + 16)
                    mm = pe.transpose(ps[4 + t // 22][:, (t % 22) * 16:(t % 22 + 1) * 16],
                                      frow[r, (t % 22) * P:(t % 22 + 1) * P], ident[r, r])
                mm.then_inc(frow_T, 1)
                norm_sum(l * 2 + 2)
                meet(pe, "pe", stage(l, M_NORM2))
                for part, tiles in enumerate(PARTS):
                    up, down = B_PART[part]
                    products(l, up, tiles // 2, hh, hl)
                    products(l, down, 4, ah, al, tiles // 2)
                for n in range(11):
                    if n >= 4:
                        pe.wait_ge(ftail_out, l * 11 + (n - 3))
                    for t in range(4):
                        mm = pe.transpose(ps[4 + n % 4][0:18, t * P:(t + 1) * P], tail_f[:, 4 * n + t, :], ident)
                    mm.then_inc(ftail_T, 1)
                meet(pe, "pe", stage(l, M_FFN))
            norm_sum(2 * DEPTH + 1)
            pe.wait_ge(root_taken, 1)
            for n in range(12):
                c, j = n // 4, n % 4
                T = P if c < 2 else SAMP
                if n >= 4:
                    pe.wait_ge(last_out, n - 3)
                for i in range(4):
                    mm = pe.transpose(ps[j][0:T, i * P:(i + 1) * P], x[:, 4 * j + i, c * P:c * P + T], ident)
                mm.then_inc(last_T, 1)

        @block.vector
        def _(dve):
            def lo(l, body, s, rows=8):
                dve.wait_ge(hi_done, (l * BODIES + body) * 4 + (s + 1))
                dve.tensor_tensor(wl[:, s % 2, 0:rows, :], raw[:, s, 0:rows, :], wh[:, s % 2, 0:rows, :].bitcast(F32),
                                  ALU.subtract).then_inc(lo_done, 1)

            def body(l, b, before, after, rows=8):
                lo(l, b, 0, rows)
                lo(l, b, 1, rows)
                before and before()
                lo(l, b, 2, rows)
                lo(l, b, 3, rows)
                after()

            def bodies(l, base, n, pending, task, rows=8):
                def take(i, g):
                    u = (l * BODIES + i + base) * 4
                    dve.wait_ge(unit_done, u + (2 * g + 4))
                    task(i, g, (ps[2 * g], ps[2 * g + 1]))
                body(l, base, pending, lambda: take(0, 0), rows)
                if n > 1:
                    with dve.Fori(1, n) as i:
                        body(l, i + base, lambda: take(i - 1, 1), lambda: take(i, 0), rows)
                return lambda: take(n - 1, 1)

            def scaled(dst, bank, scale=None, n=TOK):
                if scale is None:
                    return dve.tensor_tensor(dst, bank[:, 0:TOK], rstd[:], ALU.mult)
                return dve.scalar_tensor_tensor(dst, bank[:, 0:TOK], scale, rstd[:], ALU.mult, ALU.mult)

            def norm_low(l, n, col):
                for t in range(KT):
                    dve.wait_ge(h_hi, (n - 1) * KT + (t + 1))
                    dve.scalar_tensor_tensor(hl[:, t, :], x[:, t, :], par[:, col + t:col + t + 1],
                                             hh[:, t, :].bitcast(F32), ALU.mult, ALU.subtract)

            def norm_scale(n):
                dve.wait_ge(squares, n)
                dve.tensor_reduce(rstd[:], sq[:].rearrange("p k t -> p t k"), AX.X, ALU.add).then_inc(sq_acc, 1)
                dve.wait_ge(sq_sum, n)
                dve.tensor_scalar(rstd[:], ps[7][:, 0:TOK], 1.0 / D, EPS, ALU.mult, ALU.add).then_inc(mean_sq, 1)
                dve.wait_ge(root, n)
                return dve.reciprocal(rstd[:], rstd[:])

            def split(c0, T):
                return None

            H3 = CVK - 1
            E0 = SEQ + H3

            def ext_fill(banks, hist, nh):
                e2 = ext[:, :, E0:].rearrange("p c (b t) -> p c b t", b=NB)
                for t in range(2):
                    dve.tensor_copy(e2[:, t, :, H3 - nh:H3], hist(t))
                    dve.tensor_tensor(ext[:, t, H3:E0], banks[t][:, 0:SEQ], rstd[:, 0:SEQ], ALU.mult)
                    mm = dve.tensor_tensor(e2[:, t, :, H3:], banks[t][:, SEQ:TOK].rearrange("p (b t) -> p b t", b=NB),
                                           rstd[:, SEQ:TOK].rearrange("p (b t) -> p b t", b=NB), ALU.mult)
                mm.then_inc(group_out, 1)
                dve.drain()
                return e2

            def conv(dst, e2, taps, wcol, bcol):
                first = H3 - (taps - 1)
                for kk in range(taps):
                    for t in range(2):
                        d1 = dst(t)[:, 0:SEQ]
                        d2 = dst(t)[:, SEQ:TOK].rearrange("p (b t) -> p b t", b=NB)
                        s1 = ext[:, t, first + kk:first + kk + SEQ]
                        s2 = e2[:, t, :, first + kk:first + kk + NT]
                        if kk == 0:
                            dve.tensor_scalar(d1, s1, wcol(kk, t), bcol(t), ALU.mult, ALU.add)
                            mm = dve.tensor_scalar(d2, s2, wcol(kk, t), bcol(t), ALU.mult, ALU.add)
                        else:
                            dve.scalar_tensor_tensor(d1, s1, wcol(kk, t), d1, ALU.mult, ALU.add)
                            mm = dve.scalar_tensor_tensor(d2, s2, wcol(kk, t), d2, ALU.mult, ALU.add)
                    if kk < taps - 1:
                        dve.drain()
                return mm

            dve.sem_inc(lo_done, 4)
            dve.sem_inc(group_out, 2)
            dve.memset(ext[:], 0.0)
            dve.memset(xp[:, :, 0:PH], 0.0)
            dve.wait_ge(first_T, 1)
            dve.tensor_copy(fgain[:], ps[7][:, 0:KT]).then_inc(first_out, 1)
            for n in range(12):
                c, j = n // 4, n % 4
                T = P if c < 2 else SAMP
                dve.wait_ge(first_T, n + 2)
                dve.tensor_copy(x[:, 4 * j:4 * j + 4, c * P:c * P + T],
                                ps[j][:, 0:4 * T].rearrange("p (i t) -> p i t", i=4)).then_inc(first_out, 1)
            meet(dve, "dve", 1)

            with dve.Fori(0, DEPTH) as l:
                dve.wait_ge(rows_T, l * 3 + 1)
                dve.tensor_copy(par[:], ps[4][:, 0:NPAR]).then_inc(par_out, 1)
                dve.wait_ge(rows_T, l * 3 + 2)
                dve.tensor_copy(hist_c[:].rearrange("p c k -> p (c k)"), ps[5][:, 0:CVT * 24])
                dve.wait_ge(rows_T, l * 3 + 3)
                xps = xp[:, :, SEQ + PH:].rearrange("p g (b t) -> p g b t", b=NB)
                dve.tensor_copy(xps[:, :, :, 0:PH], ps[6][:, 0:480].rearrange("p (g b t) -> p g b t", g=PLT, b=NB))
                dve.tensor_copy(bias64[:].rearrange("p (h t) -> p h t", h=SBH),
                                hbias[:].unsqueeze(2).broadcast_to([P, SBH, NT]))
                for e in range(2):
                    r = slice(DH * e, DH * e + DH)
                    dve.tensor_copy(dskip[r, :], skips[r, :].rearrange("p (j e) -> p j e", e=2)[:, :, e])
                dve.drain()
                norm_low(l, l * 2 + 1, C_N1)
                dve.wait_ge(wdt_split, l + 1)
                dve.tensor_tensor(wdt_lo[:], wdt_raw[:], wdt_hi[:].bitcast(F32), ALU.subtract).then_inc(wdt_ready, 1)
                norm_scale(l * 2 + 1)
                meet(dve, "dve", stage(l, M_NORM1))

                def take_xbc(i, g, banks):
                    c0 = i * 4 + 2 * g
                    e2 = ext_fill(banks, lambda t: hist_c[:, ds(c0 + t, 1), :].rearrange("p c (b k) -> p (c b) k", b=NB), H3)
                    for t in range(2):
                        dve.tensor_copy(tail_c[:, ds(c0 + t, 1), 0:H3].rearrange("p c k -> p (c k)"), ext[:, t, SEQ:E0])
                        dve.tensor_copy(tail_c[:, ds(c0 + t, 1), H3:].rearrange("p c (b k) -> p (c b) k", b=NB),
                                        e2[:, t, :, NT:])
                    conv(lambda t: xc[:, ds(c0 + t, 1), :].rearrange("p c k -> p (c k)"), e2, CVK,
                         lambda kk, t: par[:, ds(c0 + (t + C_CW + kk * CVT), 1)],
                         lambda t: par[:, ds(c0 + (t + C_CB), 1)]).then_inc(conv_done, 1)

                def take_qkv(i, g, banks):
                    qkv = sb_qkv[:]
                    for t in range(2):
                        mm = scaled(qkv[:, ds(i * 4 + (2 * g + t), 1), :].rearrange("p c k -> p (c k)"), banks[t])
                    mm.then_inc(group_out, 1)

                def take_z(i, g, banks):
                    for t in range(2):
                        mm = scaled(z[:, ds(i * 4 + (2 * g + t), 1), :].rearrange("p c k -> p (c k)"), banks[t])
                    mm.then_inc(group_out, 1)
                    dve.drain().then_inc(conv_done, 1)

                def take_xp(i, g, banks):
                    for t in range(2):
                        j = 2 * g + t
                        dve.tensor_tensor(xp[:, j, PH:PH + SEQ], banks[t][:, 0:SEQ], rstd[:, 0:SEQ], ALU.mult)
                        mm = dve.tensor_tensor(xps[:, j, :, PH:], banks[t][:, SEQ:TOK].rearrange("p (b t) -> p b t", b=NB),
                                               rstd[:, SEQ:TOK].rearrange("p (b t) -> p b t", b=NB), ALU.mult)
                    mm.then_inc(group_out, 1)

                left = bodies(l, B_XBC, 3, None, take_xbc)
                left = bodies(l, B_QKV, 3, left, take_qkv)
                left = bodies(l, B_Z, 2, left, take_z)
                left = bodies(l, B_XP, 1, left, take_xp)
                left()
                dve.wait_ge(dt_mm, l + 1)
                dve.tensor_tensor(dtT[:, 0, :], ps[4][0:SSH, 0:TOK], rstd[0:SSH, :], ALU.mult)
                dve.drain()
                dve.tensor_scalar(q[:], q[:], DH ** -0.5, None, ALU.mult)
                meet(dve, "dve", stage(l, M_IN))

                dve.memset(qd[:], 0.0)
                dve.memset(rs[:, PAGES - 1, :], 0.0)
                dve.drain()
                for e in range(2):
                    r = slice(DH * e, DH * e + DH)
                    for j in range(SBT):
                        mm = dve.tensor_copy(qd[r, j, :, e, :], q[r, j, SEQ:TOK].rearrange("p (b t) -> p b t", b=NB))
                mm.then_inc(q_ready, 1)
                for n in range(6):
                    c, dst = n // 2, (k_tok, v_tok)[n % 2]
                    T = P if c < 2 else SAMP
                    dve.wait_ge(tok_T, l * 6 + n + 1)
                    dve.tensor_copy(dst[0:T, c, :], ps[4 + n % 2][0:T, :]).then_inc(tok_out, 1)

                def absolute(dst, src):
                    return dve.scalar_tensor_tensor(dst, src, -1.0, src, ALU.mult, ALU.max)

                def head(buf, n):
                    return buf[:].rearrange("p a c -> p (a c)")[:, 512 * (n % 2):512 * (n % 2) + 384]

                def head_in(n):
                    dve.wait_ge(z_mm, l * 9 + n + 1)
                    dve.scalar_tensor_tensor(head(zz, n), ps[n % 2][:, 0:384], hbias[:, n:n + 1],
                                             con[:, K_NEG:K_NEG + 384], ALU.add, ALU.add).then_inc(z_out, 1)
                    dve.drain()
                    absolute(head(za, n), head(zz, n)).then_inc(z_abs, 1)

                def softplus(n, dst, z_, l_):
                    dve.wait_ge(z_log, l * 17 + n + 1)
                    return dve.scalar_tensor_tensor(dst, z_, 0.0, l_, ALU.max, ALU.add)

                def argument(n, z_, s_):
                    dve.wait_ge(s_mm, l * 17 + n + 1)
                    return dve.tensor_tensor(z_, z_, s_, ALU.subtract)

                head_in(0)
                softplus(0, head(sp, 0), head(zz, 0), head(za, 0)).then_inc(z_sp, 1)
                for n in range(8):
                    if n < 7:
                        head_in(n + 1)
                    else:
                        dve.wait_ge(z_mm, l * 9 + 9)
                        for h in range(SBH):
                            mm = dve.scalar_tensor_tensor(zn[:, h, :], ps[4 * (h % 2)][0:SAMP, h * SAMP:(h + 1) * SAMP],
                                                          hbias[0:SAMP, h:h + 1], con[0:SAMP, K_SNEG:K_SNEG + SAMP],
                                                          ALU.add, ALU.add)
                        mm.then_inc(z_out, 1)
                        dve.drain()
                        absolute(za[0:SAMP, 0:8, :], zn[:]).then_inc(z_abs, 1)
                    argument(n, head(zz, n), ps[2 + n % 2][:, 0:384]).then_inc(z_arg, 1)
                    if n < 7:
                        softplus(n + 1, head(sp, n + 1), head(zz, n + 1), head(za, n + 1)).then_inc(z_sp, 1)
                    else:
                        softplus(8, spn[:], zn[:], za[0:SAMP, 0:8, :]).then_inc(z_sp, 1)
                    r = slice(DH * (n % 2), DH * (n % 2) + DH)
                    dve.wait_ge(o_hi, l * 16 + n + 1)
                    dve.tensor_tensor(hl[r, n // 2, 0:SEQ], ps[6 + n % 2][r, 0:SEQ], hh[r, n // 2, 0:SEQ].bitcast(F32),
                                      ALU.subtract).then_inc(o_out, 1)
                argument(8, zn[:].rearrange("p h c -> p (h c)"), ps[2][0:SAMP, :]).then_inc(z_arg, 1)

                def pages_in(b):
                    dve.wait_ge(z_page, (l * NB + b) * PAGES + (PAGES + 2))
                    dve.wait_ge(o_mm, b + l * 16 + 8)
                    for half in range(2):
                        mm = dve.tensor_tensor(zz[:, 8 * half:8 * half + 8, :],
                                               ps[half][:].rearrange("p (a c) -> p a c", a=8),
                                               bias64[:].unsqueeze(1).broadcast_to([P, 8, 64]), ALU.add)
                    mm.then_inc(z_out, 1)
                    dve.drain()
                    absolute(za[:].rearrange("p a c -> p (a c)"), zz[:].rearrange("p a c -> p (a c)")).then_inc(z_abs, 1)
                    dve.tensor_copy(rs[0:SAMP, PAGES - 1, :].rearrange("p (h t) -> p h t", h=SBH),
                                    spn[:, :, ds(b * NT, NT)])
                    softplus(b + 9, sp[:].rearrange("p a c -> p (a c)"), zz[:].rearrange("p a c -> p (a c)"),
                             za[:].rearrange("p a c -> p (a c)"))
                    for p in reversed(range(PAGES - 1)):
                        dve.drain()
                        mm = dve.tensor_tensor(rs[:, p, :], rs[:, p + 1, :], sp[:, p + 1, :], ALU.add)
                    mm.then_inc(z_sp, 1)

                def pages_weigh(b):
                    dve.tensor_copy(znb[:].rearrange("p (h t) -> p h t", h=SBH), zn[:, :, ds(b * NT, NT)])
                    dve.wait_ge(s_mm, b + l * 17 + 10)
                    for half in range(2):
                        zh = zz[:, 8 * half:8 * half + 8, :].rearrange("p a c -> p (a c)")
                        mm = dve.tensor_tensor(zh, zh, ps[2 + half][:], ALU.subtract)
                    mm.then_inc(z_arg, 1)

                def mask(b):
                    dve.wait_ge(o_mm, b + (l * 16 + 9))
                    dve.tensor_tensor(o_rows[:].rearrange("p (h d) -> p h d", h=SBH),
                                      ps[6][0:SBH * NT, :].rearrange("p (h d) -> p h d", h=SBH),
                                      con[0:SBH * NT, K_HEAD:K_HEAD + SBH].unsqueeze(2).broadcast_to(
                                          [SBH * NT, SBH, DH]), ALU.mult).then_inc(o_masked, 1)

                def outputs_low(b):
                    dve.wait_ge(o_hi, b + l * 16 + 9)
                    dst = (hl[:, 0:SBT, ds(b * NT + SEQ, NT)], hh[:, 0:SBT, ds(b * NT + SEQ, NT)].bitcast(F32))
                    dve.tensor_tensor(dst[0], ps[7][:, 0:SBT * NT].rearrange("p (j t) -> p j t", j=SBT), dst[1],
                                      ALU.subtract).then_inc(o_out, 1)

                pages_in(0)
                dve.wait_ge(z_w, l * 17 + 9)
                alone(dve)
                pages_weigh(0)
                mask(0)
                pages_in(1)
                with dve.Fori(1, NB - 1) as b:
                    outputs_low(b - 1)
                    pages_weigh(b)
                    mask(b)
                    pages_in(b + 1)
                outputs_low(NB - 2)
                pages_weigh(NB - 1)
                mask(NB - 1)
                outputs_low(NB - 1)
                meet(dve, "dve", stage(l, M_ATTN))

                dve.tensor_scalar(dtT[:, 0, :], dtT[:, 0, :], dtb[:, 0:1], None, ALU.add)
                dve.drain()
                absolute(dtT[:, 1, :], dtT[:, 0, :]).then_inc(dt_abs, 1)
                for c in range(3):
                    dve.wait_ge(ctail_T, l * 3 + c + 1)
                    dve.tensor_copy(ctail[:, c * 512:(c + 1) * 512], ps[c][0:27, :]).then_inc(ctail_out, 1)
                dve.wait_ge(dt_log, l + 1)
                dve.scalar_tensor_tensor(dtT[:, 0, :], dtT[:, 0, :], 0.0, dtT[:, 1, :], ALU.max, ALU.add)
                dve.drain()
                dve.tensor_scalar(dtT[:, 1, :], dtT[:, 0, :], dtb[:, 1:2], -1.0, ALU.mult, ALU.mult)
                dve.drain()
                dve.tensor_reduce(cend[:, 0:2], dtT[:, 1, 0:SEQ].rearrange("p (c t) -> p c t", c=2), AX.X, ALU.add)
                dve.tensor_reduce(cend[:, 2:10], dtT[:, 1, SEQ:TOK].rearrange("p (c t) -> p c t", c=NB), AX.X, ALU.add
                                  ).then_inc(cend_sum, 1)
                dve.wait_ge(dec_mm, l + 1)
                dve.tensor_copy(dec[:], ps[3][:, 0:80].rearrange("p (j c) -> p j c", j=SST)).then_inc(dec_out, 1)
                for blk in range(3):
                    t0, T = tokens(blk)
                    cols = slice(t0, t0 + T)
                    dve.wait_ge(blk_T, l * 3 + blk + 1)
                    for c, w in enumerate((512, 512, 256)):
                        dve.tensor_copy(xtok[0:T, c * 512:c * 512 + w], ps[c][0:T, 0:w])
                    dve.tensor_copy(tk[0:T, 0:2, :], ps[3][0:T, 0:32].rearrange("p (i h) -> p i h", i=2)
                                    ).then_inc(blk_tok, 1)
                    dve.wait_ge(blk_cum, l * 3 + blk + 1)
                    dve.tensor_copy(tk[0:T, 2, :], ps[3][0:T, 32:48])
                    dve.drain()
                    dve.tensor_tensor(tk[0:T, 3, :], ps[3][0:T, 48:64], tk[0:T, 2, :], ALU.subtract
                                      ).then_inc(blk_end, 1)
                    le = tri_le if blk < 2 else con[0:T, K_SLE:K_SLE + T]
                    dve.tensor_tensor(cbm[0:T, :, 0:T], ps[4][0:T, 0:2 * T].rearrange("p (g t) -> p g t", g=2),
                                      le.unsqueeze(1).broadcast_to([T, NG, T]), ALU.mult)
                    dve.wait_ge(blk_exp, l * 3 + blk + 1)
                    dve.tensor_tensor(tk[0:T, 4, :], tk[0:T, 3, :], tk[0:T, 0, :], ALU.mult)
                    dve.drain()
                    dve.tensor_tensor(xw[0:T, :].rearrange("p (h d) -> p h d", h=SSH),
                                      xtok[0:T, 0:SSW].rearrange("p (h d) -> p h d", h=SSH),
                                      tk[0:T, 4, :].unsqueeze(2).broadcast_to([T, SSH, DH]), ALU.mult
                                      ).then_inc(blk_xw, 1)
                    for j in range(4):
                        n = blk * 4 + j
                        dve.wait_ge(c_mm, l * 12 + n + 1)
                        for i in range(4):
                            mm = dve.tensor_scalar(seg[0:T, i, 0:T], ps[5 + j % 2][0:T, i * T:(i + 1) * T],
                                                   tk[0:T, 2, 4 * j + i:4 * j + i + 1], 0.0, ALU.subtract, ALU.min)
                        mm.then_inc(c_seg, 1)
                        dve.wait_ge(c_exp, l * 12 + n + 1)
                        if n:
                            dve.wait_ge(y_mm, l * 12 + n)
                        for i in range(4):
                            mm = dve.scalar_tensor_tensor(wts[0:T, i, 0:T], seg[0:T, i, 0:T],
                                                          tk[0:T, 0, 4 * j + i:4 * j + i + 1], cbm[0:T, j // 2, 0:T],
                                                          ALU.mult, ALU.mult)
                        if blk:
                            dst = cs[:] if blk == 1 else csS[:, 4 * j:4 * j + 4, :]
                            mm = dve.tensor_tensor(dst, dst, xc[:, SST + NG + j // 2, cols].unsqueeze(1).broadcast_to(
                                [P, 4, T]), ALU.mult)
                        mm.then_inc(c_w, 1)
                        dve.wait_ge(y_mm, l * 12 + n + 1)
                        for i in range(2):
                            mm = dve.scalar_tensor_tensor(y[:, 2 * j + i, cols], xc[:, 2 * j + i, cols],
                                                          dskip[:, 2 * j + i:2 * j + i + 1],
                                                          ps[j % 2][:, i * T:(i + 1) * T], ALU.mult, ALU.add)
                        mm.then_inc(y_out, 1)
                    if blk == 0:
                        dve.wait_ge(st_mm, l * 2 + 1)
                        for g, b in enumerate((2, 4)):
                            dve.tensor_copy(s1T[:, g * 512:(g + 1) * 512], ps[b][:])
                        for g in range(NG):
                            mm = dve.tensor_copy(snat[:, 4 * g:4 * g + 4, :], ps[5 + g][:].rearrange("p (j n) -> p j n", j=4))
                        mm.then_inc(st_new, 1)
                    elif blk == 1:
                        dve.wait_ge(st_mm, l * 2 + 2)
                        alone(dve)
                        dve.drain()
                        for j in range(SST):
                            mm = dve.scalar_tensor_tensor(snew[:, j, :], snat[:, j, :], dec[:, j, 1:2],
                                                          ps[5 + j // 4][:, (j % 4) * NS:(j % 4 + 1) * NS],
                                                          ALU.mult, ALU.add)
                        mm.then_inc(st_new, 1)
                with dve.Fori(0, NB) as b:
                    g8 = l * NB + b
                    dve.tensor_scalar(bm[:], xtok[0:SAMP, SSW:], con[0:SAMP, ds(b + K_SEQ, 1)], None, ALU.mult)
                    dve.wait_ge(s_T, g8 + 1)
                    for c in range(2):
                        mm = dve.tensor_copy(sbT[:, c * 512:(c + 1) * 512], ps[c][:])
                    mm.then_inc(s_Tout, 1)
                    dve.wait_ge(s_mm2, g8 + 1)
                    dve.wait_ge(s_stored, (l * (NB + 1) + b + 1) * 16)
                    for j in range(SST):
                        mm = dve.scalar_tensor_tensor(snew[:, j, :], snat[:, j, :],
                                                      dec[:, j, ds(b + 2, 1)],
                                                      ps[5 + j // 4][:, (j % 4) * NS:(j % 4 + 1) * NS],
                                                      ALU.mult, ALU.add)
                    mm.then_inc(s_new, 1)
                for c in range(2):
                    for e in range(2):
                        r = slice(DH * e, DH * e + DH)
                        dst = y[r, 4 * c:4 * c + 4, SEQ:TOK]
                        dve.tensor_tensor(dst, dst, ps[2 + c][r, :].rearrange("p (j e t) -> p j e t", j=4, e=2)[:, :, e, :],
                                          ALU.add)
                dve.drain()
                dve.tensor_tensor(y[:], y[:], z[:], ALU.mult).then_inc(y_gated, 1)
                dve.wait_ge(y_sq, l + 1)
                dve.tensor_reduce(rstd[:], sqy[:].rearrange("p k t -> p t k"), AX.X, ALU.add).then_inc(y_acc, 1)
                dve.tensor_copy(ptmp[:].rearrange("p g (b t) -> p g b t", b=NB), xps[:, :, :, NT:]).then_inc(ptail_in, 1)
                for g, win in enumerate(WINS):
                    src, w, bufs = xp[:, g, :], 1, [p1, p2]
                    while w < win:
                        dst = bufs[0][:]
                        bufs.reverse()
                        dve.tensor_tensor(dst[:, 2 * w - 1:], src[:, 2 * w - 1:], src[:, w - 1:XPL - w], ALU.add)
                        dve.drain()
                        src, w = dst, 2 * w
                    dve.scalar_tensor_tensor(pdiff[:, g, 0:SEQ], src[:, PH:PH + SEQ], 1.0 / win, xp[:, g, PH:PH + SEQ],
                                             ALU.mult, ALU.subtract)
                    mm = dve.scalar_tensor_tensor(
                        pdiff[:, g, SEQ:TOK].rearrange("p (b t) -> p b t", b=NB),
                        src[:, SEQ + PH:].rearrange("p (b t) -> p b t", b=NB)[:, :, PH:], 1.0 / win,
                        xps[:, g, :, PH:], ALU.mult, ALU.subtract)
                    dve.drain()
                    dve.tensor_tensor(pdiff[:, g, 0:16], src[:, PH:PH + 16], con[:, K_CNT + 16 * g:K_CNT + 16 * g + 16],
                                      ALU.mult)
                    dve.drain()
                    mm = dve.tensor_tensor(pdiff[:, g, 0:16], pdiff[:, g, 0:16], xp[:, g, PH:PH + 16], ALU.subtract)
                mm.then_inc(p_diff, 1)
                dve.wait_ge(y_sum, l + 1)
                dve.tensor_scalar(rstd[:], ps[7][:, 0:TOK], 1.0 / SSW, EPS, ALU.mult, ALU.add).then_inc(y_ms, 1)
                dve.wait_ge(ptail_T, l * 2 + 1)
                dve.tensor_copy(ptailP[:], ps[4][0:PH, :]).then_inc(ptail_out, 1)
                dve.wait_ge(ptail_T, l * 2 + 2)
                dve.tensor_copy(ptail[0:NB * PH, :], ps[5][0:NB * PH, :]).then_inc(ptail_out, 1)
                dve.wait_ge(y_root, l + 1)
                dve.reciprocal(rstd[:], rstd[:])
                dve.drain()
                for t in range(SST):
                    mm = dve.scalar_tensor_tensor(y[:, t, :], y[:, t, :], par[:, C_SN + t:C_SN + t + 1], rstd[:],
                                                  ALU.mult, ALU.mult)
                mm.then_inc(y_normed, 1)
                dve.wait_ge(y_hi, l + 1)
                dve.tensor_tensor(hl[:, SBT:SBT + SST, :], y[:], hh[:, SBT:SBT + SST, :].bitcast(F32), ALU.subtract)
                dve.wait_ge(p_hi, l + 1)
                for g in range(PLT):
                    dve.scalar_tensor_tensor(hl[:, SBT + SST + g, :], ps[g][:, 0:TOK], par[:, C_PS + g:C_PS + g + 1],
                                             hh[:, SBT + SST + g, :].bitcast(F32), ALU.mult, ALU.subtract)
                meet(dve, "dve", stage(l, M_MIX))

                def take_sum(i, g, banks):
                    for t in range(2):
                        dst = x[:, ds(i * 4 + (2 * g + t), 1), :].rearrange("p c k -> p (c k)")
                        mm = dve.tensor_tensor(dst, banks[t][:, 0:TOK], dst, ALU.add)
                    mm.then_inc(group_out, 1)

                left = bodies(l, B_OUT, 4, None, take_sum)
                left()
                meet(dve, "dve", stage(l, M_OUT))
                norm_low(l, l * 2 + 2, C_N2)
                dve.wait_ge(frow_T, l + 1)
                for half in range(2):
                    dve.tensor_copy(hist_f[:, 22 * half:22 * half + 22, :].rearrange("p c k -> p (c k)"),
                                    ps[4 + half][:, 0:22 * 16])
                norm_scale(l * 2 + 2)
                meet(dve, "dve", stage(l, M_NORM2))

                left, t0, done = None, 0, 0
                for part, tiles in enumerate(PARTS):
                    up, down = B_PART[part]

                    def take_gate_up(i, g, banks, t0=t0, done=done):
                        if g == 0:
                            c0 = i * 2 + t0
                            e2 = ext_fill(banks, lambda t: hist_f[:, ds(c0 + t, 1), :].rearrange(
                                "p c (b k) -> p (c b) k", b=NB), 2)
                            for t in range(2):
                                dve.tensor_copy(tail_f[:, ds(c0 + t, 1), 0:2].rearrange("p c k -> p (c k)"),
                                                ext[:, t, E0 - 2:E0])
                                dve.tensor_copy(tail_f[:, ds(c0 + t, 1), 2:].rearrange("p c (b k) -> p (c b) k", b=NB),
                                                e2[:, t, :, H3 + NT - 2:])
                            conv(lambda t: gc[:, t, :], e2, FK, lambda kk, t: par[:, ds(c0 + (t + C_FW + kk * FT), 1)],
                                 lambda t: par[:, ds(c0 + (t + C_FB), 1)]).then_inc(conv_done, 1)
                        else:
                            dve.wait_ge(silu_done, l * 22 + i + (done + 1))
                            for t in range(2):
                                dve.tensor_tensor(gc[:, t, :], gc[:, t, :], rstd[:], ALU.mult)
                            dve.drain()
                            for t in range(2):
                                mm = dve.tensor_tensor(gc[:, t, :], gc[:, t, :], banks[t][:, 0:TOK], ALU.mult)
                            mm.then_inc(group_out, 1)
                            dve.drain()
                            dve.tensor_copy(ah[:, ds(i * 2, 2), :], gc[:])
                            dve.drain()
                            dve.tensor_tensor(al[:, ds(i * 2, 2), :], gc[:], ah[:, ds(i * 2, 2), :].bitcast(F32),
                                              ALU.subtract)
                            dve.drain()

                    left = bodies(l, up, tiles // 2, left, take_gate_up)

                    def last_of_part(left=left):
                        left()
                        dve.drain().then_inc(part_ready, 1)

                    left = bodies(l, down, 4, last_of_part, take_sum, tiles // 2)
                    t0 += tiles
                    done += tiles // 2
                left()
                for n in range(11):
                    dve.wait_ge(ftail_T, l * 11 + n + 1)
                    dve.tensor_copy(ftail[:, n * 512:(n + 1) * 512], ps[4 + n % 4][0:18, :]).then_inc(ftail_out, 1)
                meet(dve, "dve", stage(l, M_FFN))

            norm_scale(2 * DEPTH + 1)
            dve.drain()
            for t in range(KT):
                mm = dve.scalar_tensor_tensor(x[:, t, :], x[:, t, :], fgain[:, t:t + 1], rstd[:], ALU.mult, ALU.mult)
            mm.then_inc(root_taken, 1)
            for n in range(12):
                c, j = n // 4, n % 4
                T = P if c < 2 else SAMP
                dve.wait_ge(last_T, n + 1)
                dve.tensor_copy(xrow[0:T, c, j * 512:(j + 1) * 512], ps[j][0:T, :]).then_inc(last_out, 1)


_INS = ["x_prompt", "x_sample", "cache_k", "cache_v", "page_table", "state_ssm", "state_ssm_conv", "state_pool",
        "state_ffn_conv", "norm1", "w_in", "sb_bias", "ssd_conv_w", "ssd_conv_b", "dt_bias", "a_log", "d_skip",
        "ssd_norm", "pool_w", "pool_scale", "w_out", "norm2", "w_gate", "w_up", "ffn_conv_w", "ffn_conv_b", "w_down",
        "final_norm"]
_OUTS = [
    ("y_prompt", (1, SEQ, D)), ("y_sample", (NB, NT, D)),
    ("new_k_prompt", (DEPTH, 1, SEQ, SBH, DH)), ("new_v_prompt", (DEPTH, 1, SEQ, SBH, DH)),
    ("new_ssm_prompt", (DEPTH, 1, SSH, DH, NS)), ("new_ssm_conv_prompt", (DEPTH, 1, CVK - 1, CVD)),
    ("new_pool_prompt", (DEPTH, 1, PH, POOLW)), ("new_ffn_conv_prompt", (DEPTH, 1, FK - 1, FF)),
    ("new_k_sample", (DEPTH, NB, NT, SBH, DH)), ("new_v_sample", (DEPTH, NB, NT, SBH, DH)),
    ("new_ssm_sample", (DEPTH, NB, SSH, DH, NS)), ("new_ssm_conv_sample", (DEPTH, NB, CVK - 1, CVD)),
    ("new_pool_sample", (DEPTH, NB, PH, POOLW)), ("new_ffn_conv_sample", (DEPTH, NB, FK - 1, FF)),
]


def shape_constants():
    import numpy as np
    i = np.arange(P)
    con = np.zeros((P, NCON), np.float32)
    con[:, K_ID:K_ID + P] = np.eye(P)
    con[:, K_GE:K_GE + P] = i[:, None] >= i[None, :]
    con[:, K_LE:K_LE + P] = i[:, None] <= i[None, :]
    con[:, K_ONE:K_ONE + P] = 1.0
    neg = np.where(i[:, None] < i[None, :], 0.0, NEG)
    con[:, K_NEG:K_NEG + P] = neg
    con[:, K_NEG + 2 * P:K_NEG + 3 * P] = neg
    s = np.arange(SAMP)
    same = (s[:, None] // NT) == (s[None, :] // NT)
    con[0:SAMP, K_SLE:K_SLE + SAMP] = same & (s[:, None] <= s[None, :])
    con[0:SAMP, K_SONE:K_SONE + SAMP] = same
    con[0:SAMP, K_SNEG:K_SNEG + SAMP] = np.where(same & (s[:, None] < s[None, :]), 0.0, NEG)
    for g, win in enumerate(WINS):
        con[:, K_CNT + 16 * g:K_CNT + 16 * g + 16] = 1.0 / np.minimum(win, np.arange(16) + 1)
    con[0:SAMP, K_SEQ:K_SEQ + NB] = (s[:, None] // NT) == np.arange(NB)[None, :]
    con[0:SAMP, K_HEAD:K_HEAD + SBH] = (s[:, None] // NT) == np.arange(SBH)[None, :]
    con[0:SAMP, K_TOK:K_TOK + NT] = (s[:, None] % NT) == np.arange(NT)[None, :]
    sel = np.zeros((SSH, SST, P), np.float32)
    for j in range(SST):
        for m in range(P):
            sel[2 * j + m // DH, j, m] = 1.0
    return con, sel


def kernel(**inputs):
    import numpy as _np
    import concourse.bacc as _bacc
    from concourse import mybir as _mybir
    from concourse.bass_utils import run_bass_kernel_spmd as _run

    nc = _bacc.Bacc("TRN2", target_bir_lowering=False, num_devices=1)
    arrays, ins, outs = {}, {}, {}
    con, sel = shape_constants()
    for name in _INS + ["con", "sel"]:
        arr = _np.ascontiguousarray({"con": con, "sel": sel}[name] if name in ("con", "sel") else inputs[name])
        arrays[f"in_{name}"] = arr
        ins[name] = nc.dram_tensor(f"in_{name}", arr.shape, _mybir.dt.from_np(arr.dtype), kind="ExternalInput").ap()
    for name, shape in _OUTS:
        outs[name] = nc.dram_tensor(f"out_{name}", shape, F32, kind="ExternalOutput").ap()
    build(nc, ins, outs)
    r = _run(nc, [arrays], core_ids=[0])
    return tuple(r.results[0][f"out_{name}"] for name, _ in _OUTS)
```

```python
import concourse.bass as bass
from concourse import mybir
from contextlib import ExitStack

F32 = mybir.dt.float32
F32R = mybir.dt.float32r
I32 = mybir.dt.int32
ALU = mybir.AluOpType
ACT = mybir.ActivationFunctionType
AX = mybir.AxisListType
ds = bass.ds

P = 128
D = 2048
DEPTH = 2
SEQ = 256
NB = 8
NT = 8
PAST = 2048
PAGE = 128
PAGES = PAST // PAGE
SAMP = NB * NT
TOK = SEQ + SAMP
KT = D // P
SBW = 512
SBH = 8
SBT = SBW // P
DH = 64
SSW = 1024
SSH = 16
SST = SSW // P
NG = 2
NS = 128
CVD = SSW + 2 * NG * NS
CVT = CVD // P
CVK = 4
POOLW = 512
PLT = POOLW // P
WINS = (2, 4, 8, 16)
PH = 15
FF = 5632
FT = FF // P
FK = 3
EPS = 1e-6
DTC = 3 * SBW + SSW + CVD
XPC = DTC + SSH
ZC = 3 * SBW
XBC = ZC + SSW
NEG = -1.0e30

PARTS = (16, 16, 12)

B_XBC, B_QKV, B_Z, B_XP, B_OUT = 0, 3, 6, 8, 9
B_PART = []
_b = 13
for _t in PARTS:
    B_PART.append((_b, _b + _t // 2))
    _b += _t // 2 + 4
BODIES = _b

DVE_PAGES = (5, 7, 9, 11, 13, 15)
ACT_PAGES = tuple(p for p in range(PAGES) if p not in DVE_PAGES)

M_NORM1, M_IN, M_ATTN, M_MIX, M_OUT, M_NORM2, M_FFN = 1, 2, 3, 4, 5, 6, 7
MEETS = 7

C_N1, C_N2, C_CW, C_CB, C_SN, C_PS = 0, 16, 32, 80, 92, 100
C_FW, C_FB, NPAR = 104, 236, 280

K_ID, K_GE, K_LE, K_ONE, K_NEG, K_SLE, K_SONE, K_SNEG, K_CNT, K_SEQ, K_HEAD, K_TOK, NCON = (
    0, 128, 256, 384, 512, 896, 960, 1024, 1088, 1152, 1160, 1168, 1176)


def build(nc, a, o):
    with ExitStack() as ctx:
        at = [16512]

        def sb_at(name, shape, dt, offset):
            return nc.alloc_sbuf_tensor_at(name, shape, dt, offset=offset)

        def size(shape):
            n = 4
            for s in shape[1:]:
                n *= s
            return n

        def sb(name, shape, dt=F32):
            off = at[0]
            at[0] += (size(shape) + 31) // 32 * 32
            return sb_at(name, shape, dt, off)

        def sem(name):
            return ctx.enter_context(nc.semaphore(name))

        x = sb("x", [P, KT, TOK])
        hh_at = at[0]
        hh = sb("hh", [P, KT, TOK], F32R)
        hl_at = at[0]
        hl = sb("hl", [P, KT, TOK], F32R)
        ah_at = at[0]
        ah = sb("ah", [P, KT, TOK], F32R)
        al_at = at[0]
        al = sb("al", [P, KT, TOK], F32R)
        raw_at = at[0]
        raw = sb("raw", [P, 4, 8, 256])
        w_at = at[0]
        wh = sb("wh", [P, 2, 8, 256], F32R)
        wl = sb("wl", [P, 2, 8, 256], F32R)
        con = sb("con", [P, NCON])
        par = sb("par", [P, NPAR])
        fgain = sb("fgain", [P, KT])
        hbias = sb("hbias", [P, SBH])
        bias64 = sb("bias64", [P, SBH * NT])
        dskip = sb("dskip", [P, SST])
        skips = sb("skips", [P, SSH])
        dtb = sb("dtb", [SSH, 2])
        ext = sb("ext", [P, 2, SEQ + CVK - 1 + NB * (NT + CVK - 1)])
        rstd = sb("rstd", [P, TOK])
        hist_c = sb("hist_c", [P, CVT, 24])
        tail_c = sb("tail_c", [P, CVT, 27])
        wdt_raw = sb("wdt_raw", [P, KT, SSH])
        wdt_hi = sb("wdt_hi", [P, KT, SSH], F32R)
        wdt_lo = sb("wdt_lo", [P, KT, SSH], F32R)
        dtT = sb("dtT", [SSH, 2, TOK])
        pages = sb("pages", [1, NB * PAGES], I32)
        xc_at = at[0]
        xc = sb("xc", [P, CVT, TOK])
        xp_at = at[0]
        XPL = SEQ + PH + NB * (NT + PH)
        xp = sb("xp", [P, PLT, XPL])
        assert at[0] <= nc.sbuf_usable_end, at[0]

        sb_qkv = sb_at("qkv", [P, 3 * SBT, TOK], F32, ah_at)
        q, k, v = (sb_qkv[:, i * SBT:(i + 1) * SBT, :] for i in range(3))
        z = sb_at("z", [P, SST, TOK], F32, ah_at + 15360)
        zz = sb_at("zz", [P, PAGES, SBH * NT], F32, ah_at + 25600)
        sp = sb_at("sp", [P, PAGES, SBH * NT], F32, ah_at + 25600 + 4096)
        rs = sb_at("rs", [P, PAGES, SBH * NT], F32, ah_at + 25600 + 8192)
        sq = sb_at("sq", [P, KT, TOK], F32, ah_at)
        prow = sb_at("prow", [P, 3, P], F32, al_at)
        crow = sb_at("crow", [24, CVD], F32, al_at + 1536)
        plrow = sb_at("plrow", [120, POOLW], F32, al_at + 1536 + 6144)
        frow = sb_at("frow", [48, FF // 2], F32, al_at)
        v_tok = sb_at("v_tok", [P, 3, SBW], F32, hh_at + 4 * TOK * 4)
        k_tok = sb_at("k_tok", [P, 3, SBW], F32, hh_at + 4 * TOK * 4 + 6144)
        zz_odd = sb_at("zz_odd", [P, PAGES, SBH * NT], F32, hh_at + 4 * TOK * 4 + 6144)
        zz_of = (zz, zz_odd)
        qd = sb_at("qd", [P, SBT, NB, 2, NT], F32, hh_at + 4 * TOK * 4 + 12288)
        kT = sb_at("kT", [P, 2, SBW], F32, hl_at + 4 * TOK * 4)
        zn = sb_at("zn", [SAMP, SBH, SAMP], F32, hl_at + 4 * TOK * 4 + 4096)
        spn = sb_at("spn", [SAMP, SBH, SAMP], F32, hl_at + 4 * TOK * 4 + 6144)
        za = sb_at("za", [P, PAGES, SBH * NT], F32, hl_at + 4 * TOK * 4 + 8192)
        o_rows = sb_at("o_rows", [SBH * NT, SBW], F32, hl_at + 4 * TOK * 4 + 12288)
        znb = sb_at("znb", [SAMP, SBH * NT], F32, hl_at + 4 * TOK * 4 + 14336)
        kring = sb_at("kring", [P, PAGES, SBW], F32, raw_at)
        vring = sb_at("vring", [P, PAGES, SBW], F32, w_at)
        y = sb_at("y", [P, SST, TOK], F32, w_at)
        xtok = sb_at("xtok", [P, SSW + NG * NS], F32, w_at + 10240)
        xw = sb_at("xw", [P, SSW], F32, w_at + 15360)
        sT = sb_at("sT", [P, 2, SSW], F32, w_at + 19456)
        s1T = sT[:, 0, :]
        snat = sT[:, 1, :].rearrange("p (j n) -> p j n", j=SST)
        s_in = sb_at("s_in", [P, 2, SST, NS], F32, hl_at + 4 * TOK * 4)
        s_new_rows = sb_at("s_new_rows", [P, 2, SST, NS], F32, xc_at)
        snew = sb_at("snew", [P, SST, NS], F32, w_at + 27648)
        seg2 = [sb_at("seg0", [P, 4, P], F32, ah_at), sb_at("seg1", [P, 4, P], F32, ah_at + 35840)]
        wts = sb_at("wts", [P, 4, P], F32, ah_at + 2048)
        cs2 = [sb_at("cs0", [P, 4, P], F32, ah_at + 4096), sb_at("cs1", [P, 4, P], F32, ah_at + 37888)]
        csS = sb_at("csS", [P, SSH, SAMP], F32, ah_at + 6144)
        cbm = sb_at("cbm", [P, NG, P], F32, ah_at + 10240)
        tk = sb_at("tk", [P, 8, SSH], F32, ah_at + 11264)
        dec = sb_at("dec", [P, SST, 10], F32, ah_at + 11776)
        cend = sb_at("cend", [SSH, 10], F32, ah_at + 12096)
        bm = sb_at("bm", [SAMP, 2, NG * NS], F32, ah_at + 12288)
        sel = sb_at("sel", [SSH, SST, P], F32, ah_at + 25600)
        ctail = sb_at("ctail", [27, CVD], F32, ah_at + 29696)
        sqy = sb_at("sqy", [P, SST, TOK], F32, w_at + 10240)
        p1 = sb_at("p1", [P, XPL], F32, ah_at)
        p2 = sb_at("p2", [P, XPL], F32, ah_at + 1920)
        pdiff = sb_at("pdiff", [P, PLT, TOK], F32, ah_at + 3840)
        poolw = sb_at("poolw", [P, PLT, P], F32, ah_at + 8960)
        ptailP = sb_at("ptailP", [PH, POOLW], F32, ah_at + 11008)
        ptail = sb_at("ptail", [P, POOLW], F32, ah_at + 13056)
        ptmp = sb_at("ptmp", [P, PLT, NB * PH], F32, ah_at + 25600)
        hist_f = sb_at("hist_f", [P, FT, 16], F32, xc_at)
        tail_f = sb_at("tail_f", [P, FT, 18], F32, xc_at + 2816)
        gc = sb_at("gc", [P, 2, TOK], F32, xc_at + 2816 + 3168)
        ftail = sb_at("ftail", [18, FF], F32, ah_at)
        xrow = sb_at("xrow", [P, 3, D], F32, ah_at)
        frows = sb_at("frows", [KT, P], F32, xc_at)
        xout = xrow

        ps = [ctx.enter_context(nc.psum_tensor(f"ps{i}", [P, 512], F32)) for i in range(8)]

        ident = con[:, K_ID:K_ID + P]
        tri_ge = con[:, K_GE:K_GE + P]
        tri_le = con[:, K_LE:K_LE + P]
        ones = con[:, K_ONE:K_ONE + P]

        at_stage = {n: sem(f"{n}_at_stage") for n in ("pe", "act", "dve", "pool")}
        raw_loaded = [sem(f"raw_loaded{i}") for i in range(4)]
        hi_done, lo_done, unit_done, group_out = sem("hi_done"), sem("lo_done"), sem("unit_done"), sem("group_out")
        conv_done, silu_done, part_ready = sem("conv_done"), sem("silu_done"), sem("part_ready")
        pages_loaded, first_loaded, first_T, first_out = (sem("pages_loaded"), sem("first_loaded"), sem("first_T"),
                                                          sem("first_out"))
        last_T, last_out, last_stored, root_taken = sem("last_T"), sem("last_out"), sem("last_stored"), sem("root_taken")
        rows_loaded, rows_T, par_out = sem("rows_loaded"), sem("rows_T"), sem("par_out")
        frow_loaded, frow_T = sem("frow_loaded"), sem("frow_T")
        h_hi, squares, sq_acc, sq_sum, mean_sq, root = (sem("h_hi"), sem("squares"), sem("sq_acc"), sem("sq_sum"),
                                                        sem("mean_sq"), sem("root"))
        wdt_split, wdt_ready, dt_mm = sem("wdt_split"), sem("wdt_ready"), sem("dt_mm")
        tok_T, tok_out, kv_stored, q_ready = sem("tok_T"), sem("tok_out"), sem("kv_stored"), sem("q_ready")
        z_mm, z_out, z_abs, z_log, z_sp, s_mm, z_arg, z_w = (
            sem("z_mm"), sem("z_out"), sem("z_abs"), sem("z_log"), sem("z_sp"), sem("s_mm"), sem("z_arg"), sem("z_w"))
        o_mm, o_hi, o_out = sem("o_mm"), sem("o_hi"), sem("o_out")
        o_masked, o_fold = sem("o_masked"), sem("o_fold")
        k_loaded = [sem(f"k_loaded{i}") for i in range(4)]
        v_loaded = sem("v_loaded")
        k_T, z_page = sem("k_T"), sem("z_page")
        kT_out = {"act": sem("kT_out_act"), "dve": sem("kT_out_dve")}
        sel_loaded, dt_abs, dt_log, cend_sum, cend_exp, dec_mm, dec_out = (
            sem("sel_loaded"), sem("dt_abs"), sem("dt_log"), sem("cend_sum"), sem("cend_exp"), sem("dec_mm"),
            sem("dec_out"))
        ctail_T, ctail_out = sem("ctail_T"), sem("ctail_out")
        blk_T, blk_tok, blk_cum, blk_end, blk_exp, blk_xw = (
            sem("blk_T"), sem("blk_tok"), sem("blk_cum"), sem("blk_end"), sem("blk_exp"), sem("blk_xw"))
        c_mm, c_seg, c_exp, c_w, y_mm, y_out = (sem("c_mm"), sem("c_seg"), sem("c_exp"), sem("c_w"), sem("y_mm"),
                                                sem("y_out"))
        st_mm, st_new = sem("st_mm"), sem("st_new")
        s_loaded, s_stored = [sem(f"s_loaded{i}") for i in range(2)], [sem(f"s_stored{i}") for i in range(2)]
        s_T, s_Tout, s_bm, s_mm2, s_new = sem("s_T"), sem("s_Tout"), sem("s_bm"), sem("s_mm2"), sem("s_new")
        y_gated, y_sq, y_acc, y_sum, y_ms, y_root, y_normed, y_hi = (
            sem("y_gated"), sem("y_sq"), sem("y_acc"), sem("y_sum"), sem("y_ms"), sem("y_root"), sem("y_normed"),
            sem("y_hi"))
        poolw_loaded, p_diff, p_mm, p_hi, ptail_T, ptail_out, ptail_in = (
            sem("poolw_loaded"), sem("p_diff"), sem("p_mm"), sem("p_hi"), sem("ptail_T"), sem("ptail_out"),
            sem("ptail_in"))
        tail_stored, ftail_T, ftail_out = sem("tail_stored"), sem("ftail_T"), sem("ftail_out")

        passed = sem("passed")

        block = ctx.enter_context(nc.Block())

        def alone(eng):
            eng.sem_inc(passed, 1)

        def meet(eng, me, stage):
            if not isinstance(stage, int):
                alone(eng)
            eng.drain().then_inc(at_stage[me], 1)
            for other in at_stage:
                if other != me:
                    eng.wait_ge(at_stage[other], stage)
            if not isinstance(stage, int):
                alone(eng)

        def stage(l, m):
            return l * MEETS + (m + 1)

        def tokens(blk):
            return (blk * P, P) if blk < 2 else (SEQ, SAMP)

        def wrow(name, l, rows):
            return a[name][l].rearrange(rows, p=P)

        @block.sync
        def _(sync):
            def unit(l, body, s, w, row, rows, col):
                sync.wait_ge(lo_done, (l * BODIES + body) * 8 + (2 * s + 2))
                sync.dma_start(raw[:, s, 0:rows, :],
                               w.rearrange("l (k p) n -> l p k n", p=P)[l, :, row:row + rows, ds(col, 256)]
                               ).then_inc(raw_loaded[s], 16)

            def body(l, b, w, row, rows, col0, col1, w1=None):
                for s in range(4):
                    unit(l, b, s, w if s < 2 or w1 is None else w1, row + (s % 2) * rows, rows,
                         col0 if s < 2 else col1)

            sync.dma_start(pages[:], a["page_table"].rearrange("b p -> (b p)").unsqueeze(0)
                           ).then_inc(pages_loaded, 16)
            sync.wait_ge(pages_loaded, 16)
            with sync.Fori(0, DEPTH) as l:
                with sync.Fori(0, 3) as i:
                    body(l, i + B_XBC, a["w_in"], 0, 8, i * 512 + XBC, i * 512 + (XBC + 256))
                with sync.Fori(0, 3) as i:
                    body(l, i + B_QKV, a["w_in"], 0, 8, i * 512, i * 512 + 256)
                with sync.Fori(0, 2) as i:
                    body(l, i + B_Z, a["w_in"], 0, 8, i * 512 + ZC, i * 512 + (ZC + 256))
                body(l, B_XP, a["w_in"], 0, 8, XPC, XPC + 256)
                sync.wait_ge(at_stage["pe"], stage(l, M_IN))
                alone(sync)
                sync.wait_ge(at_stage["dve"], stage(l, M_IN))
                alone(sync)

                def keys(b, slots_free):
                    for c in range(4):
                        sync.wait_ge(k_T, slots_free + (4 * c + 4))
                        alone(sync)
                        for j in range(4 * c, 4 * c + 4):
                            page = sync.value_load(pages[0:1, ds(b * PAGES + j, 1)], min_val=0,
                                                   max_val=a["cache_k"].shape[1] - 1)
                            sync.dma_start(kring[:, j, :], a["cache_k"][l, page].rearrange("s h d -> s (h d)")
                                           ).then_inc(k_loaded[c], 16)

                with sync.Fori(0, NB) as b:
                    keys(b, (l * NB + b) * PAGES)
                sync.wait_ge(at_stage["pe"], stage(l, M_ATTN))
                alone(sync)
                with sync.Fori(0, 4) as i:
                    body(l, i + B_OUT, a["w_out"], 0, 8, i * 512, i * 512 + 256)
                t0 = 0
                for part, tiles in enumerate(PARTS):
                    up, down = B_PART[part]
                    with sync.Fori(0, tiles // 2) as i:
                        body(l, i + up, a["w_gate"], 0, 8, i * 256 + t0 * P, i * 256 + t0 * P, a["w_up"])
                    with sync.Fori(0, 4) as i:
                        body(l, i + down, a["w_down"], t0, tiles // 2, i * 512, i * 512 + 256)
                    t0 += tiles

        @block.gpsimd
        def _(pool):
            for dst, src in (
                (con[:], a["con"]),
                (frows[:], a["final_norm"].rearrange("(t p) -> t p", p=P)),
                (xrow[:, 0, :], a["x_prompt"][0, 0:P, :]),
                (xrow[:, 1, :], a["x_prompt"][0, P:SEQ, :]),
                (xrow[0:SAMP, 2, :], a["x_sample"].rearrange("b t d -> (b t) d")),
            ):
                pool.dma_start(dst, src).then_inc(first_loaded, 16)
            pool.wait_ge(pages_loaded, 16)
            meet(pool, "pool", 1)

            def square():
                pool.tensor_tensor(sq[:].rearrange("p k t -> p (k t)"), x[:].rearrange("p k t -> p (k t)"),
                                   x[:].rearrange("p k t -> p (k t)"), ALU.mult).then_inc(squares, 1)

            with pool.Fori(0, DEPTH) as l:
                for dst, src in (
                    (prow[0:16, 0, :], wrow("norm1", l, "(t p) -> t p")),
                    (prow[16:32, 0, :], wrow("norm2", l, "(t p) -> t p")),
                    (prow[32:80, 0, :], wrow("ssd_conv_w", l, "k (t p) -> (k t) p")),
                    (prow[80:92, 0, :], wrow("ssd_conv_b", l, "(t p) -> t p")),
                    (prow[92:100, 0, :], wrow("ssd_norm", l, "(t p) -> t p")),
                    (prow[100:104, 0, :], wrow("pool_scale", l, "(t p) -> t p")),
                    (prow[0:88, 1, :], wrow("ffn_conv_w", l, "k (t p) -> (k t) p")[0:88, :]),
                    (prow[0:44, 2, :], wrow("ffn_conv_w", l, "k (t p) -> (k t) p")[88:132, :]),
                    (prow[44:88, 2, :], wrow("ffn_conv_b", l, "(t p) -> t p")),
                    (crow[:], a["state_ssm_conv"][l].rearrange("b k c -> (b k) c")),
                    (plrow[:], a["state_pool"][l].rearrange("b k c -> (b k) c")),
                    (hbias[:], a["sb_bias"][l].unsqueeze(0).broadcast_to([P, SBH])),
                    (skips[:], a["d_skip"][l].unsqueeze(0).broadcast_to([P, SSH])),
                    (dtb[:, 0:1], a["dt_bias"][l].unsqueeze(1)),
                    (dtb[:, 1:2], a["a_log"][l].unsqueeze(1)),
                    (wdt_raw[:], a["w_in"].rearrange("l (k p) n -> l p k n", p=P)[l, :, :, DTC:DTC + SSH]),
                ):
                    pool.dma_start(dst, src).then_inc(rows_loaded, 16)
                square()
                meet(pool, "pool", stage(l, M_NORM1))
                meet(pool, "pool", stage(l, M_IN))

                pool.wait_ge(tok_out, l * 6 + 6)
                alone(pool)
                for name, src in (("k", k_tok), ("v", v_tok)):
                    pool.dma_start(o[f"new_{name}_prompt"][l, 0].rearrange("(c p) h d -> p c (h d)", p=P),
                                   src[:, 0:2, :]).then_inc(kv_stored, 16)
                    pool.dma_start(o[f"new_{name}_sample"][l].rearrange("b t h d -> (b t) (h d)"),
                                   src[0:SAMP, 2, :]).then_inc(kv_stored, 16)
                with pool.Fori(0, NB) as b:
                    pool.wait_ge(o_mm, b + l * 16 + 8)
                    alone(pool)
                    for j in range(PAGES):
                        page = pool.value_load(pages[0:1, ds(b * PAGES + j, 1)], min_val=0,
                                               max_val=a["cache_v"].shape[1] - 1)
                        pool.dma_start(vring[:, j, :], a["cache_v"][l, page].rearrange("s h d -> s (h d)")
                                       ).then_inc(v_loaded, 16)
                pool.wait_ge(kv_stored, l * 64 + 64)
                alone(pool)
                meet(pool, "pool", stage(l, M_ATTN))

                def state_in(b, i):
                    pool.dma_start(s_in[:, i, :, :], a["state_ssm"][l, b].rearrange("(j e) p n -> (e p) j n", e=2)
                                   ).then_inc(s_loaded[i], 16)

                def state_out(bb, i):
                    pool.wait_ge(s_new, bb * 2 + (l * NB + i + 1))
                    alone(pool)
                    pool.dma_start(o["new_ssm_sample"][l, bb * 2 + i].rearrange("(j e) p n -> (e p) j n", e=2),
                                   s_new_rows[:, i, :, :]).then_inc(s_stored[i], 16)

                pool.dma_start(sel[:], a["sel"]).then_inc(sel_loaded, 16)
                state_in(0, 0)
                state_in(1, 1)
                pool.wait_ge(ctail_out, l * 3 + 3)
                alone(pool)
                pool.dma_start(o["new_ssm_conv_prompt"][l, 0], ctail[0:3, :]).then_inc(tail_stored, 16)
                pool.dma_start(o["new_ssm_conv_sample"][l].rearrange("b k c -> (b k) c"), ctail[3:27, :]
                               ).then_inc(tail_stored, 16)
                pool.wait_ge(st_new, l * 2 + 2)
                alone(pool)
                pool.dma_start(o["new_ssm_prompt"][l, 0].rearrange("(j e) p n -> (e p) j n", e=2), snew[:]
                               ).then_inc(tail_stored, 16)
                with pool.Fori(0, NB // 2 - 1) as bb:
                    for i in range(2):
                        state_out(bb, i)
                        state_in(bb * 2 + (i + 2), i)
                for i in range(2):
                    state_out(NB // 2 - 1, i)
                pool.wait_ge(y_gated, l + 1)
                alone(pool)
                pool.tensor_tensor(sqy[:].rearrange("p k t -> p (k t)"), y[:].rearrange("p k t -> p (k t)"),
                                   y[:].rearrange("p k t -> p (k t)"), ALU.mult).then_inc(y_sq, 1)
                pool.dma_start(poolw[:], a["pool_w"][l].rearrange("g c d -> c g d")).then_inc(poolw_loaded, 16)
                pool.wait_ge(ptail_out, l * 2 + 2)
                alone(pool)
                pool.dma_start(o["new_pool_prompt"][l, 0], ptailP[:]).then_inc(tail_stored, 16)
                pool.dma_start(o["new_pool_sample"][l].rearrange("b k c -> (b k) c"), ptail[0:NB * PH, :]
                               ).then_inc(tail_stored, 16)
                for i in range(2):
                    pool.wait_ge(s_stored[i], l * 64 + 64)
                    alone(pool)
                pool.wait_ge(tail_stored, l * 112 + 80)
                alone(pool)
                meet(pool, "pool", stage(l, M_MIX))
                meet(pool, "pool", stage(l, M_OUT))
                for half in range(2):
                    pool.dma_start(frow[32 * half:32 * half + 16, :],
                                   a["state_ffn_conv"][l].rearrange("b k c -> (b k) c")[
                                       :, half * (FF // 2):(half + 1) * (FF // 2)]).then_inc(frow_loaded, 16)
                square()
                meet(pool, "pool", stage(l, M_NORM2))
                pool.wait_ge(ftail_out, l * 11 + 11)
                alone(pool)
                pool.dma_start(o["new_ffn_conv_prompt"][l, 0], ftail[0:2, :]).then_inc(tail_stored, 16)
                pool.dma_start(o["new_ffn_conv_sample"][l].rearrange("b k c -> (b k) c"), ftail[2:18, :]
                               ).then_inc(tail_stored, 16)
                pool.wait_ge(tail_stored, l * 112 + 112)
                alone(pool)
                meet(pool, "pool", stage(l, M_FFN))
            square()
            pool.wait_ge(last_out, 12)
            pool.dma_start(o["y_prompt"][0].rearrange("(c p) d -> p c d", p=P), xrow[:, 0:2, :]
                           ).then_inc(last_stored, 16)
            pool.dma_start(o["y_sample"].rearrange("b t d -> (b t) d"), xrow[0:SAMP, 2, :]).then_inc(last_stored, 16)
            pool.wait_ge(last_stored, 32)

        @block.scalar
        def _(act):
            def hi(l, body, s, rows=8):
                act.wait_ge(raw_loaded[s], (l * BODIES + body + 1) * 16)
                for h in range(2):
                    act.wait_ge(unit_done, (l * BODIES + body) * 8 + (2 * s + h + 1))
                    half = slice(h * rows // 2, (h + 1) * rows // 2)
                    act.activation(wh[:, s % 2, half, :], raw[:, s, half, :], ACT.Copy).then_inc(hi_done, 1)

            def body(l, b, first, second, rows=8):
                hi(l, b, 0, rows)
                first and first()
                for s in range(1, 4):
                    hi(l, b, s, rows)
                second and second()

            def bodies(l, base, n, pending, task, rows=8):
                body(l, base, *(pending or (None, None)), rows)
                if n > 1:
                    with act.Fori(1, n) as i:
                        body(l, i + base, task and (lambda: task(i - 1, 0)), task and (lambda: task(i - 1, 1)), rows)
                return task and (lambda: task(n - 1, 0), lambda: task(n - 1, 1))

            def norm_high(l, col):
                for t in range(KT):
                    act.activation(hh[:, t, :], x[:, t, :], ACT.Copy, scale=par[:, col + t:col + t + 1]
                                   ).then_inc(h_hi, 1)

            def norm_root(n):
                act.wait_ge(mean_sq, n)
                act.activation(rstd[:], rstd[:], ACT.Sqrt).then_inc(root, 1)

            def log1p_exp(ap):
                act.activation(ap, ap, ACT.Exp, scale=-1.0)
                act.drain()
                return act.activation(ap, ap, ACT.Ln, bias=1.0)

            act.sem_inc(kT_out["act"], 1)
            meet(act, "act", 1)
            with act.Fori(0, DEPTH) as l:
                act.wait_ge(par_out, l + 1)
                norm_high(l, C_N1)
                act.activation(wdt_hi[:], wdt_raw[:], ACT.Copy).then_inc(wdt_split, 1)
                norm_root(l * 2 + 1)
                meet(act, "act", stage(l, M_NORM1))

                def silu_xbc(i, g):
                    act.wait_ge(conv_done, l * 32 + i * 2 + (g + 1))
                    t = xc[:, ds(i * 4 + 2 * g, 2), :]
                    act.activation(t, t, ACT.Silu)

                def silu_z(i, g):
                    act.wait_ge(conv_done, l * 32 + i * 2 + (g + 7))
                    t = z[:, ds(i * 4 + 2 * g, 2), :]
                    act.activation(t, t, ACT.Silu)

                left = bodies(l, B_XBC, 3, None, silu_xbc)
                left = bodies(l, B_QKV, 3, left, None)
                left = bodies(l, B_Z, 2, left, silu_z)
                left = bodies(l, B_XP, 1, left, None)
                meet(act, "act", stage(l, M_IN))

                def z_logs(n, ap):
                    act.wait_ge(z_abs, l * 17 + n + 1)
                    log1p_exp(ap).then_inc(z_log, 1)

                def z_weights(n, ap):
                    act.wait_ge(z_arg, l * 17 + n + 1)
                    act.activation(ap, ap, ACT.Exp).then_inc(z_w, 1)

                def head(buf, n):
                    return buf[:].rearrange("p a c -> p (a c)")[:, 512 * (n % 2):512 * (n % 2) + 384]

                z_logs(0, head(za, 0))
                for n in range(8):
                    if n < 7:
                        z_logs(n + 1, head(za, n + 1))
                    else:
                        z_logs(8, za[0:SAMP, 0:8, :])
                    z_weights(n, head(zz, n))
                    r = slice(DH * (n % 2), DH * (n % 2) + DH)
                    act.wait_ge(o_mm, l * 16 + n + 1)
                    act.activation(hh[r, n // 2, 0:SEQ], ps[6 + n % 2][r, 0:SEQ], ACT.Copy).then_inc(o_hi, 1)
                z_weights(8, zn[:])

                def page_copies(b, between={}):
                    for p in range(PAGES):
                        if p in ACT_PAGES:
                            act.wait_ge(k_T, (l * NB + b) * PAGES + (p + PAGES + 1))
                            act.wait_ge(z_page, (l * NB + b) * PAGES + (p + 1))
                            act.activation(kT[:, p % 2, :], ps[4 + p % 2][:], ACT.Copy).then_inc(kT_out["act"], 1)
                        if p in between:
                            between[p]()

                def weigh(b, i, half):
                    if half == 0:
                        act.wait_ge(z_arg, b + (l * 17 + 10))
                    ap = zz_of[i][:, 8 * half:8 * half + 8, :]
                    mm = act.activation(ap, ap, ACT.Exp)
                    if half == 1:
                        mm.then_inc(z_w, 1)

                def outputs(b):
                    act.wait_ge(o_fold, b + (l * NB + 1))
                    act.activation(hh[:, 0:SBT, ds(b * NT + SEQ, NT)],
                                   ps[7][:, 0:SBT * NT].rearrange("p (j t) -> p j t", j=SBT), ACT.Copy
                                   ).then_inc(o_hi, 1)

                page_copies(0)
                z_logs(9, za[:])
                page_copies(1, {7: lambda: weigh(0, 0, 0), 9: lambda: weigh(0, 0, 1)})
                z_logs(10, za[:])
                with act.Fori(0, NB // 2 - 1) as bb:
                    for i in (1, 2):
                        b = bb * 2 + i
                        page_copies(bb * 2 + (i + 1), {1: lambda: outputs(bb * 2 + (i - 1)),
                                                       7: lambda: weigh(b, i % 2, 0), 9: lambda: weigh(b, i % 2, 1)})
                        z_logs(bb * 2 + (i + 10), za[:])
                outputs(NB - 2)
                weigh(NB - 1, 1, 0)
                weigh(NB - 1, 1, 1)
                outputs(NB - 1)
                meet(act, "act", stage(l, M_ATTN))

                act.wait_ge(dt_abs, l + 1)
                act.activation(dtb[:, 1:2], dtb[:, 1:2], ACT.Exp)
                log1p_exp(dtT[:, 1, :]).then_inc(dt_log, 1)
                act.wait_ge(cend_sum, l + 1)
                act.activation(cend[:], cend[:], ACT.Exp).then_inc(cend_exp, 1)
                for blk in range(3):
                    t0, T = tokens(blk)
                    act.wait_ge(blk_end, l * 3 + blk + 1)
                    act.activation(tk[0:T, 3, :], tk[0:T, 3, :], ACT.Exp).then_inc(blk_exp, 1)
                    for j in range(4):
                        n = blk * 4 + j
                        seg = seg2[n % 2]
                        act.wait_ge(c_seg, l * 12 + n + 1)
                        mm = act.activation(seg[0:T, :, 0:T], seg[0:T, :, 0:T], ACT.Exp)
                        if blk == 1 and j >= 2:
                            act.wait_ge(y_mm, l * 12 + n - 1)
                            alone(act)
                        if blk:
                            dst = cs2[j % 2][:] if blk == 1 else csS[:, 4 * j:4 * j + 4, :]
                            mm = act.activation(dst, ps[5 + j % 2][:, 0:4 * T].rearrange("p (h t) -> p h t", h=4),
                                                ACT.Exp)
                        mm.then_inc(c_exp, 1)
                with act.Fori(0, NB // 2) as bb:
                    for i in range(2):
                        act.wait_ge(s_T, bb * 2 + (l * NB + i + 1))
                        for c in range(2):
                            mm = act.activation(sT[:, i, c * 512:(c + 1) * 512], ps[(0, 1, 4, 7)[2 * i + c]][:],
                                                ACT.Copy)
                        mm.then_inc(s_Tout, 1)
                act.wait_ge(y_ms, l + 1)
                act.activation(rstd[:], rstd[:], ACT.Sqrt).then_inc(y_root, 1)
                act.wait_ge(y_normed, l + 1)
                act.activation(hh[:, SBT:SBT + SST, :], y[:], ACT.Copy).then_inc(y_hi, 1)
                act.wait_ge(p_mm, l + 1)
                for g in range(PLT):
                    mm = act.activation(hh[:, SBT + SST + g, :], ps[g][:, 0:TOK], ACT.Copy,
                                        scale=par[:, C_PS + g:C_PS + g + 1])
                mm.then_inc(p_hi, 1)
                meet(act, "act", stage(l, M_MIX))

                bodies(l, B_OUT, 4, None, None)
                meet(act, "act", stage(l, M_OUT))
                norm_high(l, C_N2)
                norm_root(l * 2 + 2)
                meet(act, "act", stage(l, M_NORM2))
                done = 10
                for part, tiles in enumerate(PARTS):
                    up, down = B_PART[part]

                    def silu_gate(i, g, done=done):
                        if g == 0:
                            act.wait_ge(conv_done, l * 32 + i + (done + 1))
                            act.activation(gc[:], gc[:], ACT.Silu).then_inc(silu_done, 1)

                    left = bodies(l, up, tiles // 2, None, silu_gate)
                    bodies(l, down, 4, left, None, tiles // 2)
                    done += tiles // 2
                meet(act, "act", stage(l, M_FFN))
            norm_root(2 * DEPTH + 1)

        @block.tensor
        def _(pe):
            def products(l, base, n, hi, lo, half=8):
                def one(b):
                    g0 = (l * BODIES + b)
                    for s in range(4):
                        if s % 2 == 0:
                            pe.wait_ge(group_out, g0 * 2 + (s // 2 + 1))
                        if s % 2 == 1 and base in DOWN:
                            pe.wait_ge(part_ready, l * 3 + DOWN.index(base) + 1)
                        for h in range(2):
                            pe.wait_ge(lo_done, g0 * 8 + (2 * s + h + 9))
                            for kk in range(h * half // 2, (h + 1) * half // 2):
                                for t in range(2):
                                    row = (s % 2) * half + kk
                                    out = ps[2 * (s // 2) + t][:, 0:TOK]
                                    w = slice(t * P, t * P + P)
                                    first, last = row == 0, row == 2 * half - 1
                                    pe.matmul(out, wh[:, s % 2, kk, w], hi[:, row, :], start=first, stop=False)
                                    pe.matmul(out, wh[:, s % 2, kk, w], lo[:, row, :], start=False, stop=False)
                                    mm = pe.matmul(out, wl[:, s % 2, kk, w], hi[:, row, :], start=False, stop=last)
                            mm.then_inc(unit_done, 1)

                if n == 1:
                    one(base)
                else:
                    with pe.Fori(0, n) as i:
                        one(i + base)

            DOWN = [down for _, down in B_PART]

            def norm_sum(n):
                pe.wait_ge(sq_acc, n)
                pe.matmul(ps[7][:, 0:TOK], ones, rstd[:], start=True, stop=True).then_inc(sq_sum, 1)

            pe.sem_inc(unit_done, 4)
            pe.sem_inc(k_T, PAGES)
            pe.sem_inc(z_page, 2)
            pe.wait_ge(first_loaded, 80)
            pe.transpose(ps[7][:, 0:KT], frows[:], ident[0:KT, 0:KT]).then_inc(first_T, 1)
            for n in range(12):
                c, j = n // 4, n % 4
                T = P if c < 2 else SAMP
                if c:
                    pe.wait_ge(first_out, n - 2)
                for i in range(4):
                    mm = pe.transpose(ps[j][:, i * T:(i + 1) * T], xrow[0:T, c, (4 * j + i) * P:(4 * j + i + 1) * P],
                                      ident[0:T, 0:T])
                mm.then_inc(first_T, 1)
            meet(pe, "pe", 1)

            with pe.Fori(0, DEPTH) as l:
                pe.wait_ge(rows_loaded, l * (16 * 16) + 16 * 16)
                for c, (n, col) in enumerate(((104, 0), (88, 104), (88, 192))):
                    mm = pe.transpose(ps[4][:, col:col + n], prow[0:n, c, :], ident[0:n, 0:n])
                mm.then_inc(rows_T, 1)
                for t in range(CVT):
                    mm = pe.transpose(ps[5][:, t * 24:t * 24 + 24], crow[:, t * P:(t + 1) * P], ident[0:24, 0:24])
                mm.then_inc(rows_T, 1)
                for t in range(PLT):
                    mm = pe.transpose(ps[6][:, t * 120:t * 120 + 120], plrow[:, t * P:(t + 1) * P],
                                      ident[0:120, 0:120])
                mm.then_inc(rows_T, 1)
                norm_sum(l * 2 + 1)
                meet(pe, "pe", stage(l, M_NORM1))

                pe.wait_ge(wdt_ready, l + 1)
                for t in range(KT):
                    pe.matmul(ps[4][0:SSH, 0:TOK], wdt_hi[:, t, :], hh[:, t, :], start=(t == 0), stop=False)
                    pe.matmul(ps[4][0:SSH, 0:TOK], wdt_hi[:, t, :], hl[:, t, :], start=False, stop=False)
                    mm = pe.matmul(ps[4][0:SSH, 0:TOK], wdt_lo[:, t, :], hh[:, t, :], start=False,
                                   stop=(t == KT - 1))
                mm.then_inc(dt_mm, 1)
                products(l, B_XBC, 3, hh, hl)
                products(l, B_QKV, 3, hh, hl)
                products(l, B_Z, 2, hh, hl)
                products(l, B_XP, 1, hh, hl)
                meet(pe, "pe", stage(l, M_IN))

                for n in range(6):
                    c, src = n // 2, (k, v)[n % 2]
                    T = P if c < 2 else SAMP
                    if n >= 2:
                        pe.wait_ge(tok_out, l * 6 + (n - 1))
                        alone(pe)
                    for t in range(SBT):
                        mm = pe.transpose(ps[4 + n % 2][0:T, t * P:(t + 1) * P], src[:, t, c * P:c * P + T], ident)
                    mm.then_inc(tok_T, 1)

                def head_z(n):
                    if n >= 2:
                        pe.wait_ge(z_out, l * 17 + (n - 1))
                        alone(pe)
                    r, b = slice(DH * (n % 2), DH * (n % 2) + DH), ps[n % 2]
                    pe.matmul(b[:, 0:SEQ], k[r, n // 2, 0:P], q[r, n // 2, 0:SEQ], start=True, stop=True)
                    pe.matmul(b[:, SEQ:SEQ + P], k[r, n // 2, P:SEQ], q[r, n // 2, P:SEQ], start=True, stop=True
                              ).then_inc(z_mm, 1)

                def head_sums(n):
                    pe.wait_ge(z_sp, l * 17 + (n + 1))
                    if n >= 2:
                        pe.wait_ge(z_arg, l * 17 + (n - 1))
                    b = ps[2 + n % 2]
                    s_ = sp[:].rearrange("p a c -> p (a c)")[:, 512 * (n % 2):512 * (n % 2) + 384]
                    pe.matmul(b[:, 0:P], tri_ge, s_[:, 0:P], start=True, stop=True)
                    pe.matmul(b[:, P:SEQ], tri_ge, s_[:, P:SEQ], start=True, stop=False)
                    pe.matmul(b[:, P:SEQ], ones, s_[:, SEQ:384], start=False, stop=True)
                    pe.matmul(b[:, SEQ:384], tri_ge, s_[:, SEQ:384], start=True, stop=True).then_inc(s_mm, 1)

                def head_out(n):
                    pe.wait_ge(z_w, l * 17 + (n + 1))
                    if n >= 2:
                        pe.wait_ge(o_out, l * 16 + (n - 1))
                    r, b = slice(DH * (n % 2), DH * (n % 2) + DH), ps[6 + n % 2]
                    w = zz[:].rearrange("p a c -> p (a c)")[:, 512 * (n % 2):512 * (n % 2) + 384]
                    pe.matmul(b[r, 0:P], v_tok[:, 0, n * DH:(n + 1) * DH], w[:, 0:P], start=True, stop=True)
                    pe.matmul(b[r, P:SEQ], v_tok[:, 0, n * DH:(n + 1) * DH], w[:, P:SEQ], start=True, stop=False)
                    pe.matmul(b[r, P:SEQ], v_tok[:, 1, n * DH:(n + 1) * DH], w[:, SEQ:384], start=False, stop=True
                              ).then_inc(o_mm, 1)

                head_z(0)
                pe.wait_ge(tok_out, l * 6 + 6)
                alone(pe)
                for n in range(8):
                    if n < 7:
                        head_z(n + 1)
                    else:
                        pe.wait_ge(z_out, l * 17 + 7)
                        alone(pe)
                        for h in range(SBH):
                            r = slice(DH * (h % 2), DH * (h % 2) + DH)
                            mm = pe.matmul(ps[4 * (h % 2)][0:SAMP, h * SAMP:(h + 1) * SAMP], k[r, h // 2, SEQ:TOK],
                                           q[r, h // 2, SEQ:TOK], start=True, stop=True)
                        mm.then_inc(z_mm, 1)
                    head_sums(n)
                    head_out(n)
                pe.wait_ge(z_sp, l * 17 + 9)
                pe.wait_ge(z_arg, l * 17 + 7)
                alone(pe)
                pe.matmul(ps[2][0:SAMP, :], tri_ge[0:SAMP, 0:SAMP], spn[:].rearrange("p h c -> p (h c)"), start=True,
                          stop=True).then_inc(s_mm, 1)

                def copied(g, p):
                    name, mine = ("dve", DVE_PAGES) if p % PAGES in DVE_PAGES else ("act", ACT_PAGES)
                    pe.wait_ge(kT_out[name], g * len(mine) + (len([m for m in mine if m <= p]) + 1))

                def page_z(b, p):
                    copied(l * NB + b, p)
                    if p == 0:
                        pe.wait_ge(z_out, b + l * 17 + 9)
                    for j in range(SBT):
                        mm = pe.matmul(ps[p // 8][:, (p % 8) * 64 + j * 16:(p % 8) * 64 + j * 16 + 16],
                                       kT[:, p % 2, j * P:(j + 1) * P],
                                       qd[:, j, ds(b, 1), :, :].rearrange("p b e t -> p (b e t)"),
                                       start=True, stop=True)
                    mm.then_inc(z_page, 1)

                def pages_z(b, between={}):
                    g = l * NB + b
                    for p in range(PAGES):
                        if p % 4 == 0:
                            pe.wait_ge(k_loaded[p // 4], g * 64 + 64)
                        copied(g, p - 2)
                        for j in range(SBT):
                            mm = pe.transpose(ps[4 + p % 2][:, j * P:(j + 1) * P], kring[:, p, j * P:(j + 1) * P],
                                              ident)
                        mm.then_inc(k_T, 1)
                        if p:
                            page_z(b, p - 1)
                        if p in between:
                            between[p]()
                    page_z(b, PAGES - 1)

                def pages_sums(b):
                    pe.wait_ge(z_sp, b + l * 17 + 10)
                    pe.wait_ge(z_arg, b + l * 17 + 9)
                    for half in range(2):
                        pe.matmul(ps[2 + half][:], tri_ge, sp[:, 8 * half:8 * half + 8, :], start=True, stop=False)
                        mm = pe.matmul(ps[2 + half][:], ones, rs[:, 8 * half:8 * half + 8, :], start=False, stop=True)
                    mm.then_inc(s_mm, 1)

                def pages_out(b, i, first=False):
                    pe.wait_ge(z_w, b + l * 17 + 10)
                    pe.wait_ge(v_loaded, (l * NB + b) * 256 + 256)
                    if first:
                        pe.wait_ge(o_out, l * 16 + 7)
                    else:
                        pe.wait_ge(o_masked, b + l * NB)
                    for p in range(PAGES):
                        pe.matmul(ps[6][0:SBH * NT, :], zz_of[i][:, p, :], vring[:, p, :], start=(p == 0), stop=False)
                    pe.matmul(ps[6][0:SBH * NT, :], znb[:], v_tok[0:SAMP, 2, :], start=False, stop=True
                              ).then_inc(o_mm, 1)

                def pages_fold(b):
                    pe.wait_ge(o_masked, b + (l * NB + 1))
                    pe.wait_ge(o_out, b + (l * 16 + 8))
                    for j in range(SBT):
                        mm = pe.matmul(ps[7][:, j * NT:(j + 1) * NT], o_rows[:, j * P:(j + 1) * P],
                                       con[0:SBH * NT, K_TOK:K_TOK + NT], start=True, stop=True)
                    mm.then_inc(o_fold, 1)

                pe.wait_ge(q_ready, l + 1)
                pe.wait_ge(z_out, l * 17 + 9)
                alone(pe)
                pages_z(0)
                pe.wait_ge(z_w, l * 17 + 9)
                alone(pe)
                pages_z(1, {3: lambda: pages_sums(0)})
                pages_out(0, 0, first=True)
                with pe.Fori(0, NB // 2 - 1) as bb:
                    for i in (1, 2):
                        b = bb * 2 + i
                        pages_z(bb * 2 + (i + 1), {1: lambda: pages_fold(bb * 2 + (i - 1)), 3: lambda: pages_sums(b)})
                        pages_out(b, i % 2)
                pages_fold(NB - 2)
                pages_sums(NB - 1)
                pages_out(NB - 1, 1)
                pages_fold(NB - 1)
                meet(pe, "pe", stage(l, M_ATTN))

                for c in range(3):
                    for t in range(4):
                        mm = pe.transpose(ps[c][0:27, t * P:(t + 1) * P], tail_c[:, 4 * c + t, :], ident)
                    mm.then_inc(ctail_T, 1)
                pe.wait_ge(cend_exp, l + 1)
                pe.wait_ge(sel_loaded, l * 16 + 16)
                for j in range(SST):
                    mm = pe.matmul(ps[3][:, j * 10:(j + 1) * 10], sel[:, j, :], cend[:], start=True, stop=True)
                mm.then_inc(dec_mm, 1)
                pe.wait_ge(dec_out, l + 1)
                pe.wait_ge(ctail_out, l * 3 + 3)
                for blk in range(3):
                    t0, T = tokens(blk)
                    cols = slice(t0, t0 + T)
                    if blk:
                        pe.wait_ge(y_out, l * 12 + blk * 4)
                        pe.wait_ge(st_new, l * 2 + blk)
                        alone(pe)
                    for t in range(SST + NG):
                        pe.transpose(ps[t // 4][0:T, (t % 4) * P:(t % 4 + 1) * P], xc[:, t, cols], ident)
                    for i in range(2):
                        mm = pe.transpose(ps[3][0:T, i * SSH:(i + 1) * SSH], dtT[:, i, cols], ident[0:SSH, 0:SSH])
                    mm.then_inc(blk_T, 1)
                    le = tri_le if blk < 2 else con[0:T, K_SLE:K_SLE + T]
                    one = ones if blk < 2 else con[0:T, K_SONE:K_SONE + T]
                    pe.wait_ge(blk_tok, l * 3 + blk + 1)
                    alone(pe)
                    pe.matmul(ps[3][0:T, 32:48], le, tk[0:T, 1, :], start=True, stop=True)
                    pe.matmul(ps[3][0:T, 48:64], one, tk[0:T, 1, :], start=True, stop=True)
                    for g in range(NG):
                        mm = pe.matmul(ps[4][0:T, g * T:(g + 1) * T], xc[:, SST + g, cols], xc[:, SST + NG + g, cols],
                                       start=True, stop=True)
                    mm.then_inc(blk_cum, 1)

                    def head_cums(j):
                        n = blk * 4 + j
                        if n >= 2:
                            pe.wait_ge(c_w, l * 12 + n - 1)
                        for i in range(4):
                            h = 4 * j + i
                            mm = pe.matmul(ps[5 + j % 2][:, i * T:(i + 1) * T],
                                           tk[0:T, 1, h:h + 1].broadcast_to([T, P]), le, start=True, stop=True)
                        mm.then_inc(c_mm, 1)

                    def head_ys(j):
                        n = blk * 4 + j
                        pe.wait_ge(c_w, l * 12 + n + 1)
                        if j >= 2:
                            pe.wait_ge(y_out, l * 12 + n - 1)
                        alone(pe)
                        for i in range(4):
                            h = 4 * j + i
                            out = ps[j % 2][DH * (i % 2):DH * (i % 2) + DH, (i // 2) * T:(i // 2 + 1) * T]
                            mm = pe.matmul(out, xtok[0:T, h * DH:(h + 1) * DH], wts[0:T, i, 0:T], start=True,
                                           stop=(blk != 1))
                            if blk == 1:
                                mm = pe.matmul(out, s1T[:, h * DH:(h + 1) * DH], cs2[j % 2][:, i, :], start=False,
                                               stop=True)
                        mm.then_inc(y_mm, 1)

                    head_cums(0)
                    for j in range(4):
                        if j < 3:
                            head_cums(j + 1)
                        head_ys(j)
                    if blk < 2:
                        pe.wait_ge(blk_xw, l * 3 + blk + 1)
                        pe.wait_ge(c_w, l * 12 + blk * 4 + 4)
                        if blk == 0:
                            for g, b in enumerate((2, 4)):
                                pe.matmul(ps[b][:], xtok[:, SSW + g * NS:SSW + (g + 1) * NS],
                                          xw[:, g * 512:(g + 1) * 512], start=True, stop=True)
                        for j in range(SST):
                            g = j // 4
                            mm = pe.matmul(ps[5 + g][:, (j % 4) * NS:(j % 4 + 1) * NS], xw[:, j * P:(j + 1) * P],
                                           xtok[:, SSW + g * NS:SSW + (g + 1) * NS], start=True, stop=True)
                        mm.then_inc(st_mm, 1)
                pe.wait_ge(blk_xw, l * 3 + 3)
                pe.wait_ge(y_out, l * 12 + 12)
                alone(pe)
                with pe.Fori(0, NB // 2) as bb:
                    for i in range(2):
                        pe.wait_ge(s_loaded[i], bb * 16 + (l * 64 + 16))
                        for j in range(SST):
                            mm = pe.transpose(ps[(0, 1, 4, 7)[2 * i + j // 4]][:, (j % 4) * P:(j % 4 + 1) * P],
                                              s_in[:, i, j, :], ident)
                        mm.then_inc(s_T, 1)
                    for i in range(2):
                        b = bb * 2 + i
                        pe.wait_ge(s_Tout, bb * 2 + (l * NB + i + 1))
                        for j in range(SST):
                            v5 = ps[2 + j // 4][:].rearrange("p (j e t) -> p j e t", j=4, e=2)
                            pe.matmul(v5[:, j % 4, :, ds(b * NT, NT)], sT[:, i, j * P:(j + 1) * P],
                                      csS[:, 2 * j:2 * j + 2, ds(b * NT, NT)], start=True, stop=True)
                        if i == 0:
                            pe.wait_ge(s_bm, bb + (l * (NB // 2) + 1))
                        else:
                            pe.wait_ge(s_new, bb * 2 + (l * NB + 1))
                        for j in range(SST):
                            g = j // 4
                            mm = pe.matmul(ps[5 + g][:, (j % 4) * NS:(j % 4 + 1) * NS], xw[0:SAMP, j * P:(j + 1) * P],
                                           bm[:, i, g * NS:(g + 1) * NS], start=True, stop=True)
                        mm.then_inc(s_mm2, 1)
                pe.wait_ge(y_acc, l + 1)
                pe.matmul(ps[7][:, 0:TOK], ones, rstd[:], start=True, stop=True).then_inc(y_sum, 1)
                pe.wait_ge(ptail_in, l + 1)
                for t in range(PLT):
                    mm = pe.transpose(ps[4][0:PH, t * P:(t + 1) * P], xp[:, t, SEQ:SEQ + PH], ident)
                mm.then_inc(ptail_T, 1)
                for t in range(PLT):
                    mm = pe.transpose(ps[5][0:NB * PH, t * P:(t + 1) * P], ptmp[:, t, :], ident)
                mm.then_inc(ptail_T, 1)
                pe.wait_ge(poolw_loaded, l * 16 + 16)
                pe.wait_ge(p_diff, l + 1)
                for g in range(PLT):
                    mm = pe.matmul(ps[g][:, 0:TOK], poolw[:, g, :], pdiff[:, g, :], start=True, stop=True)
                mm.then_inc(p_mm, 1)
                meet(pe, "pe", stage(l, M_MIX))

                products(l, B_OUT, 4, hh, hl)
                meet(pe, "pe", stage(l, M_OUT))
                pe.wait_ge(frow_loaded, l * 32 + 32)
                alone(pe)
                for t in range(FT):
                    r = slice(32 * (t // 22), 32 * (t // 22) + 16)
                    mm = pe.transpose(ps[4 + t // 22][:, (t % 22) * 16:(t % 22 + 1) * 16],
                                      frow[r, (t % 22) * P:(t % 22 + 1) * P], ident[r, r])
                mm.then_inc(frow_T, 1)
                norm_sum(l * 2 + 2)
                meet(pe, "pe", stage(l, M_NORM2))
                for part, tiles in enumerate(PARTS):
                    up, down = B_PART[part]
                    products(l, up, tiles // 2, hh, hl)
                    products(l, down, 4, ah, al, tiles // 2)
                for n in range(11):
                    if n >= 4:
                        pe.wait_ge(ftail_out, l * 11 + (n - 3))
                    for t in range(4):
                        mm = pe.transpose(ps[4 + n % 4][0:18, t * P:(t + 1) * P], tail_f[:, 4 * n + t, :], ident)
                    mm.then_inc(ftail_T, 1)
                meet(pe, "pe", stage(l, M_FFN))
            norm_sum(2 * DEPTH + 1)
            pe.wait_ge(root_taken, 1)
            for n in range(12):
                c, j = n // 4, n % 4
                T = P if c < 2 else SAMP
                if n >= 4:
                    pe.wait_ge(last_out, n - 3)
                for i in range(4):
                    mm = pe.transpose(ps[j][0:T, i * P:(i + 1) * P], x[:, 4 * j + i, c * P:c * P + T], ident)
                mm.then_inc(last_T, 1)

        @block.vector
        def _(dve):
            def lo(l, body, s, rows=8):
                for h in range(2):
                    dve.wait_ge(hi_done, (l * BODIES + body) * 8 + (2 * s + h + 1))
                    half = slice(h * rows // 2, (h + 1) * rows // 2)
                    dve.tensor_tensor(wl[:, s % 2, half, :], raw[:, s, half, :], wh[:, s % 2, half, :].bitcast(F32),
                                      ALU.subtract).then_inc(lo_done, 1)

            def body(l, b, before, after, rows=8):
                lo(l, b, 0, rows)
                lo(l, b, 1, rows)
                before and before()
                lo(l, b, 2, rows)
                lo(l, b, 3, rows)
                after()

            def bodies(l, base, n, pending, task, rows=8):
                def take(i, g):
                    u = (l * BODIES + i + base) * 8
                    dve.wait_ge(unit_done, u + (4 * g + 8))
                    task(i, g, (ps[2 * g], ps[2 * g + 1]))
                body(l, base, pending, lambda: take(0, 0), rows)
                if n > 1:
                    with dve.Fori(1, n) as i:
                        body(l, i + base, lambda: take(i - 1, 1), lambda: take(i, 0), rows)
                return lambda: take(n - 1, 1)

            def scaled(dst, bank, scale=None, n=TOK):
                if scale is None:
                    return dve.tensor_tensor(dst, bank[:, 0:TOK], rstd[:], ALU.mult)
                return dve.scalar_tensor_tensor(dst, bank[:, 0:TOK], scale, rstd[:], ALU.mult, ALU.mult)

            def norm_low(l, n, col):
                for t in range(KT):
                    dve.wait_ge(h_hi, (n - 1) * KT + (t + 1))
                    dve.scalar_tensor_tensor(hl[:, t, :], x[:, t, :], par[:, col + t:col + t + 1],
                                             hh[:, t, :].bitcast(F32), ALU.mult, ALU.subtract)

            def norm_scale(n):
                dve.wait_ge(squares, n)
                dve.tensor_reduce(rstd[:], sq[:].rearrange("p k t -> p t k"), AX.X, ALU.add).then_inc(sq_acc, 1)
                dve.wait_ge(sq_sum, n)
                dve.tensor_scalar(rstd[:], ps[7][:, 0:TOK], 1.0 / D, EPS, ALU.mult, ALU.add).then_inc(mean_sq, 1)
                dve.wait_ge(root, n)
                return dve.reciprocal(rstd[:], rstd[:])

            def split(c0, T):
                return None

            H3 = CVK - 1
            E0 = SEQ + H3

            def ext_fill(banks, hist, nh):
                e2 = ext[:, :, E0:].rearrange("p c (b t) -> p c b t", b=NB)
                alone(dve)
                dve.drain()
                for t in range(2):
                    dve.tensor_copy(e2[:, t, :, H3 - nh:H3], hist(t))
                    dve.tensor_tensor(ext[:, t, H3:E0], banks[t][:, 0:SEQ], rstd[:, 0:SEQ], ALU.mult)
                    mm = dve.tensor_tensor(e2[:, t, :, H3:], banks[t][:, SEQ:TOK].rearrange("p (b t) -> p b t", b=NB),
                                           rstd[:, SEQ:TOK].rearrange("p (b t) -> p b t", b=NB), ALU.mult)
                mm.then_inc(group_out, 1)
                dve.drain()
                return e2

            def conv(dst, e2, taps, wcol, bcol):
                first = H3 - (taps - 1)
                for kk in range(taps):
                    for t in range(2):
                        d1 = dst(t)[:, 0:SEQ]
                        d2 = dst(t)[:, SEQ:TOK].rearrange("p (b t) -> p b t", b=NB)
                        s1 = ext[:, t, first + kk:first + kk + SEQ]
                        s2 = e2[:, t, :, first + kk:first + kk + NT]
                        if kk == 0:
                            dve.tensor_scalar(d1, s1, wcol(kk, t), bcol(t), ALU.mult, ALU.add)
                            mm = dve.tensor_scalar(d2, s2, wcol(kk, t), bcol(t), ALU.mult, ALU.add)
                        else:
                            dve.scalar_tensor_tensor(d1, s1, wcol(kk, t), d1, ALU.mult, ALU.add)
                            mm = dve.scalar_tensor_tensor(d2, s2, wcol(kk, t), d2, ALU.mult, ALU.add)
                    if kk < taps - 1:
                        dve.drain()
                return mm

            dve.sem_inc(lo_done, 8)
            dve.sem_inc(group_out, 2)
            dve.sem_inc(kT_out["dve"], 1)
            dve.memset(ext[:], 0.0)
            dve.memset(xp[:, :, 0:PH], 0.0)
            dve.wait_ge(first_T, 1)
            dve.tensor_copy(fgain[:], ps[7][:, 0:KT]).then_inc(first_out, 1)
            for n in range(12):
                c, j = n // 4, n % 4
                T = P if c < 2 else SAMP
                dve.wait_ge(first_T, n + 2)
                dve.tensor_copy(x[:, 4 * j:4 * j + 4, c * P:c * P + T],
                                ps[j][:, 0:4 * T].rearrange("p (i t) -> p i t", i=4)).then_inc(first_out, 1)
            meet(dve, "dve", 1)

            with dve.Fori(0, DEPTH) as l:
                dve.wait_ge(rows_T, l * 3 + 1)
                dve.tensor_copy(par[:], ps[4][:, 0:NPAR]).then_inc(par_out, 1)
                dve.wait_ge(rows_T, l * 3 + 2)
                dve.tensor_copy(hist_c[:].rearrange("p c k -> p (c k)"), ps[5][:, 0:CVT * 24])
                dve.wait_ge(rows_T, l * 3 + 3)
                xps = xp[:, :, SEQ + PH:].rearrange("p g (b t) -> p g b t", b=NB)
                dve.tensor_copy(xps[:, :, :, 0:PH], ps[6][:, 0:480].rearrange("p (g b t) -> p g b t", g=PLT, b=NB))
                dve.tensor_copy(bias64[:].rearrange("p (h t) -> p h t", h=SBH),
                                hbias[:].unsqueeze(2).broadcast_to([P, SBH, NT]))
                for e in range(2):
                    r = slice(DH * e, DH * e + DH)
                    dve.tensor_copy(dskip[r, :], skips[r, :].rearrange("p (j e) -> p j e", e=2)[:, :, e])
                dve.drain()
                norm_low(l, l * 2 + 1, C_N1)
                dve.wait_ge(wdt_split, l + 1)
                dve.tensor_tensor(wdt_lo[:], wdt_raw[:], wdt_hi[:].bitcast(F32), ALU.subtract).then_inc(wdt_ready, 1)
                norm_scale(l * 2 + 1)
                meet(dve, "dve", stage(l, M_NORM1))

                def take_xbc(i, g, banks):
                    c0 = i * 4 + 2 * g
                    e2 = ext_fill(banks, lambda t: hist_c[:, ds(c0 + t, 1), :].rearrange("p c (b k) -> p (c b) k", b=NB), H3)
                    for t in range(2):
                        dve.tensor_copy(tail_c[:, ds(c0 + t, 1), 0:H3].rearrange("p c k -> p (c k)"), ext[:, t, SEQ:E0])
                        dve.tensor_copy(tail_c[:, ds(c0 + t, 1), H3:].rearrange("p c (b k) -> p (c b) k", b=NB),
                                        e2[:, t, :, NT:])
                    conv(lambda t: xc[:, ds(c0 + t, 1), :].rearrange("p c k -> p (c k)"), e2, CVK,
                         lambda kk, t: par[:, ds(c0 + (t + C_CW + kk * CVT), 1)],
                         lambda t: par[:, ds(c0 + (t + C_CB), 1)]).then_inc(conv_done, 1)

                def take_qkv(i, g, banks):
                    qkv = sb_qkv[:]
                    for t in range(2):
                        mm = scaled(qkv[:, ds(i * 4 + (2 * g + t), 1), :].rearrange("p c k -> p (c k)"), banks[t])
                    mm.then_inc(group_out, 1)

                def take_z(i, g, banks):
                    for t in range(2):
                        mm = scaled(z[:, ds(i * 4 + (2 * g + t), 1), :].rearrange("p c k -> p (c k)"), banks[t])
                    mm.then_inc(group_out, 1)
                    dve.drain().then_inc(conv_done, 1)

                def take_xp(i, g, banks):
                    for t in range(2):
                        j = 2 * g + t
                        dve.tensor_tensor(xp[:, j, PH:PH + SEQ], banks[t][:, 0:SEQ], rstd[:, 0:SEQ], ALU.mult)
                        mm = dve.tensor_tensor(xps[:, j, :, PH:], banks[t][:, SEQ:TOK].rearrange("p (b t) -> p b t", b=NB),
                                               rstd[:, SEQ:TOK].rearrange("p (b t) -> p b t", b=NB), ALU.mult)
                    mm.then_inc(group_out, 1)

                left = bodies(l, B_XBC, 3, None, take_xbc)
                left = bodies(l, B_QKV, 3, left, take_qkv)
                left = bodies(l, B_Z, 2, left, take_z)
                left = bodies(l, B_XP, 1, left, take_xp)
                left()
                dve.wait_ge(dt_mm, l + 1)
                dve.tensor_tensor(dtT[:, 0, :], ps[4][0:SSH, 0:TOK], rstd[0:SSH, :], ALU.mult)
                dve.drain()
                dve.tensor_scalar(q[:], q[:], DH ** -0.5, None, ALU.mult)
                meet(dve, "dve", stage(l, M_IN))

                dve.memset(qd[:], 0.0)
                dve.memset(rs[:, PAGES - 1, :], 0.0)
                dve.drain()
                for e in range(2):
                    r = slice(DH * e, DH * e + DH)
                    for j in range(SBT):
                        mm = dve.tensor_copy(qd[r, j, :, e, :], q[r, j, SEQ:TOK].rearrange("p (b t) -> p b t", b=NB))
                mm.then_inc(q_ready, 1)
                for n in range(6):
                    c, dst = n // 2, (k_tok, v_tok)[n % 2]
                    T = P if c < 2 else SAMP
                    dve.wait_ge(tok_T, l * 6 + n + 1)
                    dve.tensor_copy(dst[0:T, c, :], ps[4 + n % 2][0:T, :]).then_inc(tok_out, 1)

                def absolute(dst, src):
                    return dve.scalar_tensor_tensor(dst, src, -1.0, src, ALU.mult, ALU.max)

                def head(buf, n):
                    return buf[:].rearrange("p a c -> p (a c)")[:, 512 * (n % 2):512 * (n % 2) + 384]

                def head_in(n):
                    dve.wait_ge(z_mm, l * 9 + n + 1)
                    dve.scalar_tensor_tensor(head(zz, n), ps[n % 2][:, 0:384], hbias[:, n:n + 1],
                                             con[:, K_NEG:K_NEG + 384], ALU.add, ALU.add).then_inc(z_out, 1)
                    dve.drain()
                    absolute(head(za, n), head(zz, n)).then_inc(z_abs, 1)

                def softplus(n, dst, z_, l_):
                    dve.wait_ge(z_log, l * 17 + n + 1)
                    return dve.scalar_tensor_tensor(dst, z_, 0.0, l_, ALU.max, ALU.add)

                def argument(n, z_, s_):
                    dve.wait_ge(s_mm, l * 17 + n + 1)
                    return dve.tensor_tensor(z_, z_, s_, ALU.subtract)

                head_in(0)
                softplus(0, head(sp, 0), head(zz, 0), head(za, 0)).then_inc(z_sp, 1)
                for n in range(8):
                    if n < 7:
                        head_in(n + 1)
                    else:
                        dve.wait_ge(z_mm, l * 9 + 9)
                        for h in range(SBH):
                            mm = dve.scalar_tensor_tensor(zn[:, h, :], ps[4 * (h % 2)][0:SAMP, h * SAMP:(h + 1) * SAMP],
                                                          hbias[0:SAMP, h:h + 1], con[0:SAMP, K_SNEG:K_SNEG + SAMP],
                                                          ALU.add, ALU.add)
                        mm.then_inc(z_out, 1)
                        dve.drain()
                        absolute(za[0:SAMP, 0:8, :], zn[:]).then_inc(z_abs, 1)
                    argument(n, head(zz, n), ps[2 + n % 2][:, 0:384]).then_inc(z_arg, 1)
                    if n < 7:
                        softplus(n + 1, head(sp, n + 1), head(zz, n + 1), head(za, n + 1)).then_inc(z_sp, 1)
                    else:
                        softplus(8, spn[:], zn[:], za[0:SAMP, 0:8, :]).then_inc(z_sp, 1)
                    r = slice(DH * (n % 2), DH * (n % 2) + DH)
                    dve.wait_ge(o_hi, l * 16 + n + 1)
                    dve.tensor_tensor(hl[r, n // 2, 0:SEQ], ps[6 + n % 2][r, 0:SEQ], hh[r, n // 2, 0:SEQ].bitcast(F32),
                                      ALU.subtract).then_inc(o_out, 1)
                argument(8, zn[:].rearrange("p h c -> p (h c)"), ps[2][0:SAMP, :]).then_inc(z_arg, 1)

                def pages_in(b, i, first=False):
                    zz = zz_of[i]
                    dve.wait_ge(z_page, (l * NB + b) * PAGES + (PAGES + 2))
                    dve.wait_ge(o_mm, b + (l * 16 + (8 if first else 7)))
                    for half in range(2):
                        mm = dve.tensor_tensor(zz[:, 8 * half:8 * half + 8, :],
                                               ps[half][:].rearrange("p (a c) -> p a c", a=8),
                                               bias64[:].unsqueeze(1).broadcast_to([P, 8, 64]), ALU.add)
                    mm.then_inc(z_out, 1)
                    dve.drain()
                    absolute(za[:].rearrange("p a c -> p (a c)"), zz[:].rearrange("p a c -> p (a c)")).then_inc(z_abs, 1)
                    dve.tensor_copy(rs[0:SAMP, PAGES - 1, :].rearrange("p (h t) -> p h t", h=SBH),
                                    spn[:, :, ds(b * NT, NT)])
                    softplus(b + 9, sp[:].rearrange("p a c -> p (a c)"), zz[:].rearrange("p a c -> p (a c)"),
                             za[:].rearrange("p a c -> p (a c)"))
                    for p in reversed(range(PAGES - 1)):
                        dve.drain()
                        mm = dve.tensor_tensor(rs[:, p, :], rs[:, p + 1, :], sp[:, p + 1, :], ALU.add)
                    mm.then_inc(z_sp, 1)

                def pages_weigh(b, i):
                    zz = zz_of[i]
                    dve.tensor_copy(znb[:].rearrange("p (h t) -> p h t", h=SBH), zn[:, :, ds(b * NT, NT)])
                    dve.wait_ge(s_mm, b + l * 17 + 10)
                    for half in range(2):
                        zh = zz[:, 8 * half:8 * half + 8, :].rearrange("p a c -> p (a c)")
                        mm = dve.tensor_tensor(zh, zh, ps[2 + half][:], ALU.subtract)
                    mm.then_inc(z_arg, 1)

                def mask(b):
                    dve.wait_ge(o_mm, b + (l * 16 + 9))
                    dve.tensor_tensor(o_rows[:].rearrange("p (h d) -> p h d", h=SBH),
                                      ps[6][0:SBH * NT, :].rearrange("p (h d) -> p h d", h=SBH),
                                      con[0:SBH * NT, K_HEAD:K_HEAD + SBH].unsqueeze(2).broadcast_to(
                                          [SBH * NT, SBH, DH]), ALU.mult).then_inc(o_masked, 1)

                def outputs_low(b):
                    dve.wait_ge(o_hi, b + l * 16 + 9)
                    dst = (hl[:, 0:SBT, ds(b * NT + SEQ, NT)], hh[:, 0:SBT, ds(b * NT + SEQ, NT)].bitcast(F32))
                    dve.tensor_tensor(dst[0], ps[7][:, 0:SBT * NT].rearrange("p (j t) -> p j t", j=SBT), dst[1],
                                      ALU.subtract).then_inc(o_out, 1)

                def page_copies(b):
                    for p in DVE_PAGES:
                        dve.wait_ge(k_T, (l * NB + b) * PAGES + (p + PAGES + 1))
                        dve.wait_ge(z_page, (l * NB + b) * PAGES + (p + 1))
                        dve.tensor_copy(kT[:, p % 2, :], ps[4 + p % 2][:]).then_inc(kT_out["dve"], 1)

                page_copies(0)
                pages_in(0, 0, first=True)
                dve.wait_ge(z_w, l * 17 + 9)
                alone(dve)
                pages_weigh(0, 0)
                dve.wait_ge(kv_stored, l * 64 + 64)
                alone(dve)
                page_copies(1)
                pages_in(1, 1)
                mask(0)
                with dve.Fori(0, NB // 2 - 1) as bb:
                    for i in (1, 2):
                        b = bb * 2 + i
                        pages_weigh(b, i % 2)
                        outputs_low(bb * 2 + (i - 1))
                        page_copies(bb * 2 + (i + 1))
                        pages_in(bb * 2 + (i + 1), (i + 1) % 2)
                        mask(b)
                outputs_low(NB - 2)
                pages_weigh(NB - 1, 1)
                mask(NB - 1)
                outputs_low(NB - 1)
                meet(dve, "dve", stage(l, M_ATTN))

                dve.tensor_scalar(dtT[:, 0, :], dtT[:, 0, :], dtb[:, 0:1], None, ALU.add)
                dve.drain()
                absolute(dtT[:, 1, :], dtT[:, 0, :]).then_inc(dt_abs, 1)
                for c in range(3):
                    dve.wait_ge(ctail_T, l * 3 + c + 1)
                    dve.tensor_copy(ctail[:, c * 512:(c + 1) * 512], ps[c][0:27, :]).then_inc(ctail_out, 1)
                dve.wait_ge(dt_log, l + 1)
                dve.scalar_tensor_tensor(dtT[:, 0, :], dtT[:, 0, :], 0.0, dtT[:, 1, :], ALU.max, ALU.add)
                dve.drain()
                dve.tensor_scalar(dtT[:, 1, :], dtT[:, 0, :], dtb[:, 1:2], -1.0, ALU.mult, ALU.mult)
                dve.drain()
                dve.tensor_reduce(cend[:, 0:2], dtT[:, 1, 0:SEQ].rearrange("p (c t) -> p c t", c=2), AX.X, ALU.add)
                dve.tensor_reduce(cend[:, 2:10], dtT[:, 1, SEQ:TOK].rearrange("p (c t) -> p c t", c=NB), AX.X, ALU.add
                                  ).then_inc(cend_sum, 1)
                dve.wait_ge(dec_mm, l + 1)
                dve.tensor_copy(dec[:], ps[3][:, 0:80].rearrange("p (j c) -> p j c", j=SST)).then_inc(dec_out, 1)
                for blk in range(3):
                    t0, T = tokens(blk)
                    cols = slice(t0, t0 + T)
                    dve.wait_ge(blk_T, l * 3 + blk + 1)
                    for c, w in enumerate((512, 512, 256)):
                        dve.tensor_copy(xtok[0:T, c * 512:c * 512 + w], ps[c][0:T, 0:w])
                    dve.tensor_copy(tk[0:T, 0:2, :], ps[3][0:T, 0:32].rearrange("p (i h) -> p i h", i=2)
                                    ).then_inc(blk_tok, 1)
                    dve.wait_ge(blk_cum, l * 3 + blk + 1)
                    dve.tensor_copy(tk[0:T, 2, :], ps[3][0:T, 32:48])
                    dve.drain()
                    dve.tensor_tensor(tk[0:T, 3, :], ps[3][0:T, 48:64], tk[0:T, 2, :], ALU.subtract
                                      ).then_inc(blk_end, 1)
                    le = tri_le if blk < 2 else con[0:T, K_SLE:K_SLE + T]
                    dve.tensor_tensor(cbm[0:T, :, 0:T], ps[4][0:T, 0:2 * T].rearrange("p (g t) -> p g t", g=2),
                                      le.unsqueeze(1).broadcast_to([T, NG, T]), ALU.mult)
                    dve.wait_ge(blk_exp, l * 3 + blk + 1)
                    dve.tensor_tensor(tk[0:T, 4, :], tk[0:T, 3, :], tk[0:T, 0, :], ALU.mult)
                    dve.drain()
                    dve.tensor_tensor(xw[0:T, :].rearrange("p (h d) -> p h d", h=SSH),
                                      xtok[0:T, 0:SSW].rearrange("p (h d) -> p h d", h=SSH),
                                      tk[0:T, 4, :].unsqueeze(2).broadcast_to([T, SSH, DH]), ALU.mult
                                      ).then_inc(blk_xw, 1)

                    def exponents(j):
                        n = blk * 4 + j
                        dve.wait_ge(c_mm, l * 12 + n + 1)
                        for i in range(4):
                            mm = dve.tensor_scalar(seg2[n % 2][0:T, i, 0:T], ps[5 + j % 2][0:T, i * T:(i + 1) * T],
                                                   tk[0:T, 2, 4 * j + i:4 * j + i + 1], 0.0, ALU.subtract, ALU.min)
                        mm.then_inc(c_seg, 1)

                    def head_weights(j):
                        n = blk * 4 + j
                        dve.wait_ge(c_exp, l * 12 + n + 1)
                        if n:
                            dve.wait_ge(y_mm, l * 12 + n)
                        for i in range(4):
                            mm = dve.scalar_tensor_tensor(wts[0:T, i, 0:T], seg2[n % 2][0:T, i, 0:T],
                                                          tk[0:T, 0, 4 * j + i:4 * j + i + 1], cbm[0:T, j // 2, 0:T],
                                                          ALU.mult, ALU.mult)
                        if blk:
                            dst = cs2[j % 2][:] if blk == 1 else csS[:, 4 * j:4 * j + 4, :]
                            mm = dve.tensor_tensor(dst, dst, xc[:, SST + NG + j // 2, cols].unsqueeze(1).broadcast_to(
                                [P, 4, T]), ALU.mult)
                        mm.then_inc(c_w, 1)

                    def heads_out(j):
                        dve.wait_ge(y_mm, l * 12 + blk * 4 + j + 1)
                        for i in range(2):
                            mm = dve.scalar_tensor_tensor(y[:, 2 * j + i, cols], xc[:, 2 * j + i, cols],
                                                          dskip[:, 2 * j + i:2 * j + i + 1],
                                                          ps[j % 2][:, i * T:(i + 1) * T], ALU.mult, ALU.add)
                        mm.then_inc(y_out, 1)

                    exponents(0)
                    for j in range(4):
                        if j < 3:
                            exponents(j + 1)
                        head_weights(j)
                        if j:
                            heads_out(j - 1)
                    heads_out(3)
                    if blk == 0:
                        dve.wait_ge(st_mm, l * 2 + 1)
                        for g, b in enumerate((2, 4)):
                            dve.tensor_copy(s1T[:, g * 512:(g + 1) * 512], ps[b][:])
                        for g in range(NG):
                            mm = dve.tensor_copy(snat[:, 4 * g:4 * g + 4, :], ps[5 + g][:].rearrange("p (j n) -> p j n", j=4))
                        mm.then_inc(st_new, 1)
                    elif blk == 1:
                        dve.wait_ge(st_mm, l * 2 + 2)
                        alone(dve)
                        dve.drain()
                        for j in range(SST):
                            mm = dve.scalar_tensor_tensor(snew[:, j, :], snat[:, j, :], dec[:, j, 1:2],
                                                          ps[5 + j // 4][:, (j % 4) * NS:(j % 4 + 1) * NS],
                                                          ALU.mult, ALU.add)
                        mm.then_inc(st_new, 1)

                def states(bb, first=False):
                    for i in range(2):
                        mm = dve.tensor_scalar(bm[:, i, :], xtok[0:SAMP, SSW:], con[0:SAMP, ds(bb * 2 + (K_SEQ + i), 1)],
                                               None, ALU.mult)
                    mm.then_inc(s_bm, 1)
                    for i in range(2):
                        if not first:
                            dve.wait_ge(s_stored[i], bb * 16 + l * 64)
                        dve.wait_ge(s_mm2, bb * 2 + (l * NB + i + 1))
                        for j in range(SST):
                            mm = dve.scalar_tensor_tensor(s_new_rows[:, i, j, :], s_in[:, i, j, :],
                                                          dec[:, j, ds(bb * 2 + (2 + i), 1)],
                                                          ps[5 + j // 4][:, (j % 4) * NS:(j % 4 + 1) * NS],
                                                          ALU.mult, ALU.add)
                        mm.then_inc(s_new, 1)

                states(0, first=True)
                with dve.Fori(1, NB // 2) as bb:
                    states(bb)
                for c in range(2):
                    for e in range(2):
                        r = slice(DH * e, DH * e + DH)
                        dst = y[r, 4 * c:4 * c + 4, SEQ:TOK]
                        dve.tensor_tensor(dst, dst, ps[2 + c][r, :].rearrange("p (j e t) -> p j e t", j=4, e=2)[:, :, e, :],
                                          ALU.add)
                dve.drain()
                dve.tensor_tensor(y[:], y[:], z[:], ALU.mult).then_inc(y_gated, 1)
                dve.wait_ge(y_sq, l + 1)
                dve.tensor_reduce(rstd[:], sqy[:].rearrange("p k t -> p t k"), AX.X, ALU.add).then_inc(y_acc, 1)
                dve.tensor_copy(ptmp[:].rearrange("p g (b t) -> p g b t", b=NB), xps[:, :, :, NT:]).then_inc(ptail_in, 1)
                for g, win in enumerate(WINS):
                    src, w, bufs = xp[:, g, :], 1, [p1, p2]
                    while w < win:
                        dst = bufs[0][:]
                        bufs.reverse()
                        dve.tensor_tensor(dst[:, 2 * w - 1:], src[:, 2 * w - 1:], src[:, w - 1:XPL - w], ALU.add)
                        dve.drain()
                        src, w = dst, 2 * w
                    dve.scalar_tensor_tensor(pdiff[:, g, 0:SEQ], src[:, PH:PH + SEQ], 1.0 / win, xp[:, g, PH:PH + SEQ],
                                             ALU.mult, ALU.subtract)
                    mm = dve.scalar_tensor_tensor(
                        pdiff[:, g, SEQ:TOK].rearrange("p (b t) -> p b t", b=NB),
                        src[:, SEQ + PH:].rearrange("p (b t) -> p b t", b=NB)[:, :, PH:], 1.0 / win,
                        xps[:, g, :, PH:], ALU.mult, ALU.subtract)
                    dve.drain()
                    dve.tensor_tensor(pdiff[:, g, 0:16], src[:, PH:PH + 16], con[:, K_CNT + 16 * g:K_CNT + 16 * g + 16],
                                      ALU.mult)
                    dve.drain()
                    mm = dve.tensor_tensor(pdiff[:, g, 0:16], pdiff[:, g, 0:16], xp[:, g, PH:PH + 16], ALU.subtract)
                mm.then_inc(p_diff, 1)
                dve.wait_ge(y_sum, l + 1)
                dve.tensor_scalar(rstd[:], ps[7][:, 0:TOK], 1.0 / SSW, EPS, ALU.mult, ALU.add).then_inc(y_ms, 1)
                dve.wait_ge(ptail_T, l * 2 + 1)
                dve.tensor_copy(ptailP[:], ps[4][0:PH, :]).then_inc(ptail_out, 1)
                dve.wait_ge(ptail_T, l * 2 + 2)
                dve.tensor_copy(ptail[0:NB * PH, :], ps[5][0:NB * PH, :]).then_inc(ptail_out, 1)
                dve.wait_ge(y_root, l + 1)
                dve.reciprocal(rstd[:], rstd[:])
                dve.drain()
                for t in range(SST):
                    mm = dve.scalar_tensor_tensor(y[:, t, :], y[:, t, :], par[:, C_SN + t:C_SN + t + 1], rstd[:],
                                                  ALU.mult, ALU.mult)
                mm.then_inc(y_normed, 1)
                dve.wait_ge(y_hi, l + 1)
                dve.tensor_tensor(hl[:, SBT:SBT + SST, :], y[:], hh[:, SBT:SBT + SST, :].bitcast(F32), ALU.subtract)
                dve.wait_ge(p_hi, l + 1)
                for g in range(PLT):
                    dve.scalar_tensor_tensor(hl[:, SBT + SST + g, :], ps[g][:, 0:TOK], par[:, C_PS + g:C_PS + g + 1],
                                             hh[:, SBT + SST + g, :].bitcast(F32), ALU.mult, ALU.subtract)
                meet(dve, "dve", stage(l, M_MIX))

                def take_sum(i, g, banks):
                    for t in range(2):
                        dst = x[:, ds(i * 4 + (2 * g + t), 1), :].rearrange("p c k -> p (c k)")
                        mm = dve.tensor_tensor(dst, banks[t][:, 0:TOK], dst, ALU.add)
                    mm.then_inc(group_out, 1)

                left = bodies(l, B_OUT, 4, None, take_sum)
                left()
                meet(dve, "dve", stage(l, M_OUT))
                norm_low(l, l * 2 + 2, C_N2)
                dve.wait_ge(frow_T, l + 1)
                for half in range(2):
                    dve.tensor_copy(hist_f[:, 22 * half:22 * half + 22, :].rearrange("p c k -> p (c k)"),
                                    ps[4 + half][:, 0:22 * 16])
                norm_scale(l * 2 + 2)
                meet(dve, "dve", stage(l, M_NORM2))

                left, t0, done = None, 0, 0
                for part, tiles in enumerate(PARTS):
                    up, down = B_PART[part]

                    def take_gate_up(i, g, banks, t0=t0, done=done):
                        if g == 0:
                            c0 = i * 2 + t0
                            e2 = ext_fill(banks, lambda t: hist_f[:, ds(c0 + t, 1), :].rearrange(
                                "p c (b k) -> p (c b) k", b=NB), 2)
                            for t in range(2):
                                dve.tensor_copy(tail_f[:, ds(c0 + t, 1), 0:2].rearrange("p c k -> p (c k)"),
                                                ext[:, t, E0 - 2:E0])
                                dve.tensor_copy(tail_f[:, ds(c0 + t, 1), 2:].rearrange("p c (b k) -> p (c b) k", b=NB),
                                                e2[:, t, :, H3 + NT - 2:])
                            conv(lambda t: gc[:, t, :], e2, FK, lambda kk, t: par[:, ds(c0 + (t + C_FW + kk * FT), 1)],
                                 lambda t: par[:, ds(c0 + (t + C_FB), 1)]).then_inc(conv_done, 1)
                        else:
                            dve.wait_ge(silu_done, l * 22 + i + (done + 1))
                            for t in range(2):
                                dve.tensor_tensor(gc[:, t, :], gc[:, t, :], rstd[:], ALU.mult)
                            dve.drain()
                            for t in range(2):
                                mm = dve.tensor_tensor(gc[:, t, :], gc[:, t, :], banks[t][:, 0:TOK], ALU.mult)
                            mm.then_inc(group_out, 1)
                            dve.drain()
                            dve.tensor_copy(ah[:, ds(i * 2, 2), :], gc[:])
                            dve.drain()
                            dve.tensor_tensor(al[:, ds(i * 2, 2), :], gc[:], ah[:, ds(i * 2, 2), :].bitcast(F32),
                                              ALU.subtract)
                            dve.drain()

                    left = bodies(l, up, tiles // 2, left, take_gate_up)

                    def last_of_part(left=left):
                        left()
                        dve.drain().then_inc(part_ready, 1)

                    left = bodies(l, down, 4, last_of_part, take_sum, tiles // 2)
                    t0 += tiles
                    done += tiles // 2
                left()
                for n in range(11):
                    dve.wait_ge(ftail_T, l * 11 + n + 1)
                    dve.tensor_copy(ftail[:, n * 512:(n + 1) * 512], ps[4 + n % 4][0:18, :]).then_inc(ftail_out, 1)
                meet(dve, "dve", stage(l, M_FFN))

            norm_scale(2 * DEPTH + 1)
            dve.drain()
            for t in range(KT):
                mm = dve.scalar_tensor_tensor(x[:, t, :], x[:, t, :], fgain[:, t:t + 1], rstd[:], ALU.mult, ALU.mult)
            mm.then_inc(root_taken, 1)
            for n in range(12):
                c, j = n // 4, n % 4
                T = P if c < 2 else SAMP
                dve.wait_ge(last_T, n + 1)
                dve.tensor_copy(xrow[0:T, c, j * 512:(j + 1) * 512], ps[j][0:T, :]).then_inc(last_out, 1)


_INS = ["x_prompt", "x_sample", "cache_k", "cache_v", "page_table", "state_ssm", "state_ssm_conv", "state_pool",
        "state_ffn_conv", "norm1", "w_in", "sb_bias", "ssd_conv_w", "ssd_conv_b", "dt_bias", "a_log", "d_skip",
        "ssd_norm", "pool_w", "pool_scale", "w_out", "norm2", "w_gate", "w_up", "ffn_conv_w", "ffn_conv_b", "w_down",
        "final_norm"]
_OUTS = [
    ("y_prompt", (1, SEQ, D)), ("y_sample", (NB, NT, D)),
    ("new_k_prompt", (DEPTH, 1, SEQ, SBH, DH)), ("new_v_prompt", (DEPTH, 1, SEQ, SBH, DH)),
    ("new_ssm_prompt", (DEPTH, 1, SSH, DH, NS)), ("new_ssm_conv_prompt", (DEPTH, 1, CVK - 1, CVD)),
    ("new_pool_prompt", (DEPTH, 1, PH, POOLW)), ("new_ffn_conv_prompt", (DEPTH, 1, FK - 1, FF)),
    ("new_k_sample", (DEPTH, NB, NT, SBH, DH)), ("new_v_sample", (DEPTH, NB, NT, SBH, DH)),
    ("new_ssm_sample", (DEPTH, NB, SSH, DH, NS)), ("new_ssm_conv_sample", (DEPTH, NB, CVK - 1, CVD)),
    ("new_pool_sample", (DEPTH, NB, PH, POOLW)), ("new_ffn_conv_sample", (DEPTH, NB, FK - 1, FF)),
]


def shape_constants():
    import numpy as np
    i = np.arange(P)
    con = np.zeros((P, NCON), np.float32)
    con[:, K_ID:K_ID + P] = np.eye(P)
    con[:, K_GE:K_GE + P] = i[:, None] >= i[None, :]
    con[:, K_LE:K_LE + P] = i[:, None] <= i[None, :]
    con[:, K_ONE:K_ONE + P] = 1.0
    neg = np.where(i[:, None] < i[None, :], 0.0, NEG)
    con[:, K_NEG:K_NEG + P] = neg
    con[:, K_NEG + 2 * P:K_NEG + 3 * P] = neg
    s = np.arange(SAMP)
    same = (s[:, None] // NT) == (s[None, :] // NT)
    con[0:SAMP, K_SLE:K_SLE + SAMP] = same & (s[:, None] <= s[None, :])
    con[0:SAMP, K_SONE:K_SONE + SAMP] = same
    con[0:SAMP, K_SNEG:K_SNEG + SAMP] = np.where(same & (s[:, None] < s[None, :]), 0.0, NEG)
    for g, win in enumerate(WINS):
        con[:, K_CNT + 16 * g:K_CNT + 16 * g + 16] = 1.0 / np.minimum(win, np.arange(16) + 1)
    con[0:SAMP, K_SEQ:K_SEQ + NB] = (s[:, None] // NT) == np.arange(NB)[None, :]
    con[0:SAMP, K_HEAD:K_HEAD + SBH] = (s[:, None] // NT) == np.arange(SBH)[None, :]
    con[0:SAMP, K_TOK:K_TOK + NT] = (s[:, None] % NT) == np.arange(NT)[None, :]
    sel = np.zeros((SSH, SST, P), np.float32)
    for j in range(SST):
        for m in range(P):
            sel[2 * j + m // DH, j, m] = 1.0
    return con, sel


def kernel(**inputs):
    import numpy as _np
    import concourse.bacc as _bacc
    from concourse import mybir as _mybir
    from concourse.bass_utils import run_bass_kernel_spmd as _run

    nc = _bacc.Bacc("TRN2", target_bir_lowering=False, num_devices=1)
    arrays, ins, outs = {}, {}, {}
    con, sel = shape_constants()
    for name in _INS + ["con", "sel"]:
        arr = _np.ascontiguousarray({"con": con, "sel": sel}[name] if name in ("con", "sel") else inputs[name])
        arrays[f"in_{name}"] = arr
        ins[name] = nc.dram_tensor(f"in_{name}", arr.shape, _mybir.dt.from_np(arr.dtype), kind="ExternalInput").ap()
    for name, shape in _OUTS:
        outs[name] = nc.dram_tensor(f"out_{name}", shape, F32, kind="ExternalOutput").ap()
    build(nc, ins, outs)
    r = _run(nc, [arrays], core_ids=[0])
    return tuple(r.results[0][f"out_{name}"] for name, _ in _OUTS)
```

```python
import concourse.bass as bass
from concourse import mybir
from contextlib import ExitStack

F32 = mybir.dt.float32
F32R = mybir.dt.float32r
I32 = mybir.dt.int32
ALU = mybir.AluOpType
ACT = mybir.ActivationFunctionType
AX = mybir.AxisListType
ds = bass.ds

P = 128
D = 2048
DEPTH = 2
SEQ = 256
NB = 8
NT = 8
PAST = 2048
PAGE = 128
PAGES = PAST // PAGE
SAMP = NB * NT
TOK = SEQ + SAMP
KT = D // P
SBW = 512
SBH = 8
SBT = SBW // P
DH = 64
SSW = 1024
SSH = 16
SST = SSW // P
NG = 2
NS = 128
CVD = SSW + 2 * NG * NS
CVT = CVD // P
CVK = 4
POOLW = 512
PLT = POOLW // P
WINS = (2, 4, 8, 16)
PH = 15
FF = 5632
FT = FF // P
FK = 3
EPS = 1e-6
DTC = 3 * SBW + SSW + CVD
XPC = DTC + SSH
ZC = 3 * SBW
XBC = ZC + SSW
NEG = -1.0e30

PARTS = (16, 16, 12)

B_XBC, B_QKV, B_Z, B_XP, B_OUT = 0, 3, 6, 8, 9
B_PART = []
_b = 13
for _t in PARTS:
    B_PART.append((_b, _b + _t // 2))
    _b += _t // 2 + 4
BODIES = _b

DVE_PAGES = (2, 3, 12, 13, 14, 15)
ACT_PAGES = tuple(p for p in range(PAGES) if p not in DVE_PAGES)

POOL_BANKS = (0, 1, 4, 5)

M_IN, M_ATTN, M_MIX, M_OUT, M_FFN = 1, 2, 3, 4, 5
MEETS = 5

C_N1, C_N2, C_CW, C_CB, C_SN, C_PS = 0, 16, 32, 80, 92, 100
C_FW, C_FB, NPAR = 104, 236, 280

K_ID, K_GE, K_LE, K_ONE, K_NEG, K_SLE, K_SONE, K_SNEG, K_CNT, K_SEQ, K_HEAD, K_TOK, NCON = (
    0, 128, 256, 384, 512, 896, 960, 1024, 1088, 1152, 1160, 1162, 1194)


def build(nc, a, o):
    with ExitStack() as ctx:
        at = [16512]

        def sb_at(name, shape, dt, offset):
            return nc.alloc_sbuf_tensor_at(name, shape, dt, offset=offset)

        def size(shape):
            n = 4
            for s in shape[1:]:
                n *= s
            return n

        def sb(name, shape, dt=F32):
            off = at[0]
            at[0] += (size(shape) + 31) // 32 * 32
            return sb_at(name, shape, dt, off)

        def sem(name):
            return ctx.enter_context(nc.semaphore(name))

        x = sb("x", [P, KT, TOK])
        hh_at = at[0]
        hh = sb("hh", [P, KT, TOK], F32R)
        hl_at = at[0]
        hl = sb("hl", [P, KT, TOK], F32R)
        ah_at = at[0]
        ah = sb("ah", [P, KT, TOK], F32R)
        al_at = at[0]
        al = sb("al", [P, KT, TOK], F32R)
        raw_at = at[0]
        raw = sb("raw", [P, 4, 8, 256])
        w_at = at[0]
        wh = sb("wh", [P, 2, 8, 256], F32R)
        wl = sb("wl", [P, 2, 8, 256], F32R)
        con = sb("con", [P, NCON])
        par = sb("par", [P, NPAR])
        fgain = sb("fgain", [P, KT])
        hbias = sb("hbias", [P, SBH])
        bias64 = sb("bias64", [P, SBH * NT])
        dskip = sb("dskip", [P, SST])
        skips = sb("skips", [P, SSH])
        dtb = sb("dtb", [SSH, 2])
        ext = sb("ext", [P, 2, SEQ + CVK - 1 + NB * (NT + CVK - 1)])
        rstd = sb("rstd", [P, TOK])
        hist_c = sb("hist_c", [P, CVT, 24])
        tail_c = sb("tail_c", [P, CVT, 27])
        wdt_raw = sb("wdt_raw", [P, KT, SSH])
        wdt_hi = sb("wdt_hi", [P, KT, SSH], F32R)
        wdt_lo = sb("wdt_lo", [P, KT, SSH], F32R)
        dtT = sb("dtT", [SSH, 2, TOK])
        pages = sb("pages", [1, NB * PAGES], I32)
        xc_at = at[0]
        xc = sb("xc", [P, CVT, TOK])
        xp_at = at[0]
        XPL = SEQ + PH + NB * (NT + PH)
        xp = sb("xp", [P, PLT, XPL])
        assert at[0] <= nc.sbuf_usable_end, at[0]

        sb_qkv = sb_at("qkv", [P, 3 * SBT, TOK], F32, ah_at)
        q, k, v = (sb_qkv[:, i * SBT:(i + 1) * SBT, :] for i in range(3))
        z = sb_at("z", [P, SST, TOK], F32, ah_at + 15360)
        zz = sb_at("zz", [P, PAGES, SBH * NT], F32, ah_at + 25600)
        sp = sb_at("sp", [P, PAGES, SBH * NT], F32, ah_at + 25600 + 4096)
        rs = sb_at("rs", [P, PAGES, SBH * NT], F32, ah_at + 25600 + 8192)
        sq = sb_at("sq", [P, KT, TOK], F32, ah_at)
        prow = sb_at("prow", [P, 3, P], F32, al_at)
        crow = sb_at("crow", [24, CVD], F32, al_at + 1536)
        plrow = sb_at("plrow", [120, POOLW], F32, al_at + 1536 + 6144)
        frow = sb_at("frow", [48, FF // 2], F32, al_at)
        v_tok = sb_at("v_tok", [P, 3, SBW], F32, hh_at + 4 * TOK * 4)
        k_tok = sb_at("k_tok", [P, 3, SBW], F32, hh_at + 4 * TOK * 4 + 6144)
        zz_odd = sb_at("zz_odd", [P, PAGES, SBH * NT], F32, hh_at + 4 * TOK * 4 + 6144)
        zz_of = (zz, zz_odd)
        qd = sb_at("qd", [P, SBT, NB, 2, NT], F32, hh_at + 4 * TOK * 4 + 12288)
        kT = sb_at("kT", [P, 2, SBW], F32, hl_at + 4 * TOK * 4)
        zn = sb_at("zn", [SAMP, SBH, SAMP], F32, hl_at + 4 * TOK * 4 + 4096)
        spn = sb_at("spn", [SAMP, SBH, SAMP], F32, hl_at + 4 * TOK * 4 + 6144)
        za = sb_at("za", [P, PAGES, SBH * NT], F32, hl_at + 4 * TOK * 4 + 8192)
        o_rows = sb_at("o_rows", [P, P], F32, hl_at + 4 * TOK * 4 + 12288)
        znb = sb_at("znb", [SAMP, SBH * NT], F32, hl_at + 4 * TOK * 4 + 14336)
        kring = sb_at("kring", [P, PAGES, SBW], F32, raw_at)
        vring = sb_at("vring", [P, PAGES, SBW], F32, w_at)
        y = sb_at("y", [P, SST, TOK], F32, w_at)
        xtok = sb_at("xtok", [P, SSW + NG * NS], F32, w_at + 10240)
        xw = sb_at("xw", [P, SSW], F32, w_at + 15360)
        sT = sb_at("sT", [P, 2, SSW], F32, w_at + 19456)
        s1T = sT[:, 0, :]
        snat = sT[:, 1, :].rearrange("p (j n) -> p j n", j=SST)
        s_in = sb_at("s_in", [P, 4, SST, NS], F32, raw_at)
        s_new_rows = sb_at("s_new_rows", [P, 2, SST, NS], F32, xc_at)
        snew = sb_at("snew", [P, SST, NS], F32, w_at + 27648)
        seg2 = [sb_at("seg0", [P, 4, P], F32, ah_at), sb_at("seg1", [P, 4, P], F32, ah_at + 35840)]
        wts = sb_at("wts", [P, 4, P], F32, ah_at + 2048)
        cs2 = [sb_at("cs0", [P, 4, P], F32, ah_at + 4096), sb_at("cs1", [P, 4, P], F32, ah_at + 37888)]
        csS = sb_at("csS", [P, SSH, SAMP], F32, ah_at + 6144)
        cbm = sb_at("cbm", [P, NG, P], F32, ah_at + 10240)
        tk = sb_at("tk", [P, 8, SSH], F32, ah_at + 11264)
        dec = sb_at("dec", [P, SST, 10], F32, ah_at + 11776)
        cend = sb_at("cend", [SSH, 10], F32, ah_at + 12096)
        bm = sb_at("bm", [SAMP, 2, NG * NS], F32, ah_at + 12288)
        sel = sb_at("sel", [SSH, SST, P], F32, ah_at + 25600)
        ctail = sb_at("ctail", [27, CVD], F32, ah_at + 29696)
        p1 = sb_at("p1", [P, XPL], F32, hh_at + 4 * TOK * 4)
        p2 = sb_at("p2", [P, XPL], F32, hh_at + 4 * TOK * 4 + 1920)
        pdiff = sb_at("pdiff", [P, PLT, TOK], F32, hh_at + 4 * TOK * 4 + 3840)
        poolw = sb_at("poolw", [P, PLT, P], F32, hl_at + 4 * TOK * 4)
        ptmp = sb_at("ptmp", [P, PLT, NB * PH], F32, hl_at + 4 * TOK * 4 + 2048)
        ptailP = sb_at("ptailP", [PH, POOLW], F32, ah_at + 25600)
        ptail = sb_at("ptail", [P, POOLW], F32, ah_at + 27648)
        hist_f = sb_at("hist_f", [P, FT, 16], F32, xc_at)
        tail_f = sb_at("tail_f", [P, FT, 18], F32, xc_at + 2816)
        gc = sb_at("gc", [P, 2, TOK], F32, xc_at + 2816 + 3168)
        ftail = sb_at("ftail", [18, FF], F32, ah_at)
        xrow = sb_at("xrow", [P, 3, D], F32, ah_at)
        frows = sb_at("frows", [KT, P], F32, xc_at)

        def head_buf(n):
            buf, at0 = ((zz, 0), (zz, 512), (rs, 0))[n % 3]
            return buf[:].rearrange("p a c -> p (a c)")[:, at0:at0 + 384]

        ps = [ctx.enter_context(nc.psum_tensor(f"ps{i}", [P, 512], F32)) for i in range(8)]

        ident = con[:, K_ID:K_ID + P]
        tri_ge = con[:, K_GE:K_GE + P]
        tri_le = con[:, K_LE:K_LE + P]
        ones = con[:, K_ONE:K_ONE + P]

        at_stage = {n: sem(f"{n}_at_stage") for n in ("pe", "act", "dve", "pool")}
        raw_loaded = [sem(f"raw_loaded{i}") for i in range(4)]
        hi_done, lo_done, unit_done, group_out = sem("hi_done"), sem("lo_done"), sem("unit_done"), sem("group_out")
        conv_done, silu_done, part_ready = sem("conv_done"), sem("silu_done"), sem("part_ready")
        pages_loaded, first_loaded, first_T, first_out = (sem("pages_loaded"), sem("first_loaded"), sem("first_T"),
                                                          sem("first_out"))
        last_squares, last_summed = sem("last_squares"), sem("last_summed")
        last_T, last_out, last_stored, root_taken = sem("last_T"), sem("last_out"), sem("last_stored"), sem("root_taken")
        par_loaded, rows_loaded, rows_T, par_out = sem("par_loaded"), sem("rows_loaded"), sem("rows_T"), sem("par_out")
        frow_loaded, frow_T = sem("frow_loaded"), sem("frow_T")
        h_hi, h_lo, squares, sq_sum, mean_sq, root = (sem("h_hi"), sem("h_lo"), sem("squares"), sem("sq_sum"),
                                                      sem("mean_sq"), sem("root"))
        wdt_split, wdt_ready, dt_mm = sem("wdt_split"), sem("wdt_ready"), sem("dt_mm")
        tok_T, tok_out, kv_stored, q_ready = sem("tok_T"), sem("tok_out"), sem("kv_stored"), sem("q_ready")
        z_mm, z_out, z_abs, z_log, z_sp, s_mm, z_arg, z_w = (
            sem("z_mm"), sem("z_out"), sem("z_abs"), sem("z_log"), sem("z_sp"), sem("s_mm"), sem("z_arg"), sem("z_w"))
        o_mm, o_hi, o_out = sem("o_mm"), sem("o_hi"), sem("o_out")
        o_masked, o_fold = sem("o_masked"), sem("o_fold")
        k_loaded = [sem(f"k_loaded{i}") for i in range(4)]
        v_loaded, v_used = sem("v_loaded"), sem("v_used")
        k_T, z_page = sem("k_T"), sem("z_page")
        kT_out = {"act": sem("kT_out_act"), "dve": sem("kT_out_dve")}
        sel_loaded, dt_abs, dt_log, cend_sum, cend_exp, dec_mm, dec_out = (
            sem("sel_loaded"), sem("dt_abs"), sem("dt_log"), sem("cend_sum"), sem("cend_exp"), sem("dec_mm"),
            sem("dec_out"))
        ctail_T, ctail_out = sem("ctail_T"), sem("ctail_out")
        blk_T, blk_tok, blk_cum, blk_end, blk_exp, blk_xw = (
            sem("blk_T"), sem("blk_tok"), sem("blk_cum"), sem("blk_end"), sem("blk_exp"), sem("blk_xw"))
        c_mm, c_seg, c_exp, c_w, y_mm, y_out = (sem("c_mm"), sem("c_seg"), sem("c_exp"), sem("c_w"), sem("y_mm"),
                                                sem("y_out"))
        st_mm, st_new = sem("st_mm"), sem("st_new")
        s_loaded, s_stored = [sem(f"s_loaded{i}") for i in range(4)], [sem(f"s_stored{i}") for i in range(2)]
        s_T, s_Tout, s_bm, s_mm2, s_new = sem("s_T"), sem("s_Tout"), sem("s_bm"), sem("s_mm2"), sem("s_new")
        y_sq, y_sq_s, y_sum, y_ms, y_root, y_normed, y_hi = (
            sem("y_sq"), sem("y_sq_s"), sem("y_sum"), sem("y_ms"), sem("y_root"), sem("y_normed"), sem("y_hi"))
        poolw_loaded, p_diff, p_mm, p_hi, ptail_T, ptail_out, ptail_in = (
            sem("poolw_loaded"), sem("p_diff"), sem("p_mm"), sem("p_hi"), sem("ptail_T"), sem("ptail_out"),
            sem("ptail_in"))
        tail_stored, ftail_T, ftail_out = sem("tail_stored"), sem("ftail_T"), sem("ftail_out")

        passed = sem("passed")

        block = ctx.enter_context(nc.Block())

        def alone(eng):
            eng.sem_inc(passed, 1)

        def meet(eng, me, stage):
            if not isinstance(stage, int):
                alone(eng)
            eng.drain().then_inc(at_stage[me], 1)
            for other in at_stage:
                if other != me:
                    eng.wait_ge(at_stage[other], stage)
            if not isinstance(stage, int):
                alone(eng)

        def stage(l, m):
            return l * MEETS + (m + 1)

        def tokens(blk):
            return (blk * P, P) if blk < 2 else (SEQ, SAMP)

        def wrow(name, l, rows):
            return a[name][l].rearrange(rows, p=P)

        @block.sync
        def _(sync):
            def unit(l, body, s, w, row, rows, col):
                sync.wait_ge(lo_done, (l * BODIES + body) * 8 + (2 * s + 2))
                sync.dma_start(raw[:, s, 0:rows, :],
                               w.rearrange("l (k p) n -> l p k n", p=P)[l, :, row:row + rows, ds(col, 256)]
                               ).then_inc(raw_loaded[s], 16)

            def body(l, b, w, row, rows, col0, col1, w1=None):
                for s in range(4):
                    unit(l, b, s, w if s < 2 or w1 is None else w1, row + (s % 2) * rows, rows,
                         col0 if s < 2 else col1)

            sync.dma_start(pages[:], a["page_table"].rearrange("b p -> (b p)").unsqueeze(0)
                           ).then_inc(pages_loaded, 16)
            sync.wait_ge(pages_loaded, 16)
            with sync.Fori(0, DEPTH) as l:
                with sync.Fori(0, 3) as i:
                    body(l, i + B_XBC, a["w_in"], 0, 8, i * 512 + XBC, i * 512 + (XBC + 256))
                with sync.Fori(0, 3) as i:
                    body(l, i + B_QKV, a["w_in"], 0, 8, i * 512, i * 512 + 256)
                with sync.Fori(0, 2) as i:
                    body(l, i + B_Z, a["w_in"], 0, 8, i * 512 + ZC, i * 512 + (ZC + 256))
                body(l, B_XP, a["w_in"], 0, 8, XPC, XPC + 256)
                sync.wait_ge(at_stage["pe"], stage(l, M_IN))
                alone(sync)
                sync.wait_ge(at_stage["dve"], stage(l, M_IN))
                alone(sync)

                def keys(b, slots_free):
                    for c in range(4):
                        sync.wait_ge(k_T, slots_free + (4 * c + 4))
                        alone(sync)
                        for j in range(4 * c, 4 * c + 4):
                            page = sync.value_load(pages[0:1, ds(b * PAGES + j, 1)], min_val=0,
                                                   max_val=a["cache_k"].shape[1] - 1)
                            sync.dma_start(kring[:, j, :], a["cache_k"][l, page].rearrange("s h d -> s (h d)")
                                           ).then_inc(k_loaded[c], 16)

                with sync.Fori(0, NB) as b:
                    keys(b, (l * NB + b) * PAGES)
                sync.wait_ge(at_stage["pe"], stage(l, M_ATTN))
                alone(sync)

                def state_in(b, i):
                    sync.dma_start(s_in[:, i, :, :], a["state_ssm"][l, b].rearrange("(j e) p n -> (e p) j n", e=2)
                                   ).then_inc(s_loaded[i], 16)

                for i in range(4):
                    state_in(i, i)
                for i in range(4):
                    sync.wait_ge(s_new, l * NB + i + 1)
                    alone(sync)
                    state_in(4 + i, i)
                sync.wait_ge(s_new, l * NB + NB)
                alone(sync)
                with sync.Fori(0, 4) as i:
                    body(l, i + B_OUT, a["w_out"], 0, 8, i * 512, i * 512 + 256)
                t0 = 0
                for part, tiles in enumerate(PARTS):
                    up, down = B_PART[part]
                    with sync.Fori(0, tiles // 2) as i:
                        body(l, i + up, a["w_gate"], 0, 8, i * 256 + t0 * P, i * 256 + t0 * P, a["w_up"])
                    with sync.Fori(0, 4) as i:
                        body(l, i + down, a["w_down"], t0, tiles // 2, i * 512, i * 512 + 256)
                    t0 += tiles

        @block.gpsimd
        def _(pool):
            for dst, src in (
                (con[:], a["con"]),
                (frows[:], a["final_norm"].rearrange("(t p) -> t p", p=P)),
                (xrow[:, 0, :], a["x_prompt"][0, 0:P, :]),
                (xrow[:, 1, :], a["x_prompt"][0, P:SEQ, :]),
                (xrow[0:SAMP, 2, :], a["x_sample"].rearrange("b t d -> (b t) d")),
            ):
                pool.dma_start(dst, src).then_inc(first_loaded, 16)
            pool.wait_ge(pages_loaded, 16)
            meet(pool, "pool", 1)

            def square():
                def four(buf, t):
                    return buf[:, t:t + 4, :].rearrange("p k t -> p (k t)")
                for t in range(0, KT, 4):
                    pool.tensor_tensor(four(sq, t), four(x, t), four(x, t), ALU.mult)
                pool.drain()
                for t in (0, 8):
                    pool.tensor_tensor(four(sq, t), four(sq, t), four(sq, t + 4), ALU.add)
                pool.drain()
                pool.tensor_tensor(four(sq, 0), four(sq, 0), four(sq, 8), ALU.add).then_inc(squares, 1)

            with pool.Fori(0, DEPTH) as l:
                square()
                for dst, src in (
                    (crow[:], a["state_ssm_conv"][l].rearrange("b k c -> (b k) c")),
                    (plrow[:], a["state_pool"][l].rearrange("b k c -> (b k) c")),
                    (hbias[:], a["sb_bias"][l].unsqueeze(0).broadcast_to([P, SBH])),
                    (skips[:], a["d_skip"][l].unsqueeze(0).broadcast_to([P, SSH])),
                    (dtb[:, 0:1], a["dt_bias"][l].unsqueeze(1)),
                    (dtb[:, 1:2], a["a_log"][l].unsqueeze(1)),
                ):
                    pool.dma_start(dst, src).then_inc(rows_loaded, 16)
                meet(pool, "pool", stage(l, M_IN))

                pool.wait_ge(tok_out, l * 6 + 6)
                alone(pool)
                for name, src in (("k", k_tok), ("v", v_tok)):
                    pool.dma_start(o[f"new_{name}_prompt"][l, 0].rearrange("(c p) h d -> p c (h d)", p=P),
                                   src[:, 0:2, :]).then_inc(kv_stored, 16)
                    pool.dma_start(o[f"new_{name}_sample"][l].rearrange("b t h d -> (b t) (h d)"),
                                   src[0:SAMP, 2, :]).then_inc(kv_stored, 16)
                with pool.Fori(0, NB) as b:
                    for j in range(PAGES):
                        if j % 8 == 0:
                            pool.wait_ge(v_used, b * 2 + (l * NB * 2 + j // 8 + 1))
                            alone(pool)
                        page = pool.value_load(pages[0:1, ds(b * PAGES + j, 1)], min_val=0,
                                               max_val=a["cache_v"].shape[1] - 1)
                        pool.dma_start(vring[:, j, :], a["cache_v"][l, page].rearrange("s h d -> s (h d)")
                                       ).then_inc(v_loaded, 16)
                pool.wait_ge(kv_stored, l * 64 + 64)
                alone(pool)
                meet(pool, "pool", stage(l, M_ATTN))

                def state_out(bb, i):
                    pool.wait_ge(s_new, bb * 2 + (l * NB + i + 1))
                    alone(pool)
                    pool.dma_start(o["new_ssm_sample"][l, bb * 2 + i].rearrange("(j e) p n -> (e p) j n", e=2),
                                   s_new_rows[:, i, :, :]).then_inc(s_stored[i], 16)

                pool.dma_start(sel[:], a["sel"]).then_inc(sel_loaded, 16)
                pool.dma_start(poolw[:], a["pool_w"][l].rearrange("g c d -> c g d")).then_inc(poolw_loaded, 16)
                pool.wait_ge(ctail_out, l * 3 + 3)
                alone(pool)
                pool.dma_start(o["new_ssm_conv_prompt"][l, 0], ctail[0:3, :]).then_inc(tail_stored, 16)
                pool.dma_start(o["new_ssm_conv_sample"][l].rearrange("b k c -> (b k) c"), ctail[3:27, :]
                               ).then_inc(s_stored[1], 16)
                xps = xp[:, :, SEQ + PH:].rearrange("p g (b t) -> p g b t", b=NB)
                pool.tensor_copy(ptmp[:].rearrange("p g (b t) -> p g b t", b=NB), xps[:, :, :, NT:]).then_inc(ptail_in, 1)
                for g, win in enumerate(WINS):
                    src, w, bufs = xp[:, g, :], 1, [p1, p2]
                    while w < win:
                        dst = bufs[0][:]
                        bufs.reverse()
                        pool.tensor_tensor(dst[:, 2 * w - 1:], src[:, 2 * w - 1:], src[:, w - 1:XPL - w], ALU.add)
                        pool.drain()
                        src, w = dst, 2 * w
                    news = pdiff[:, g, SEQ:TOK].rearrange("p (b t) -> p b t", b=NB)
                    pool.tensor_scalar(pdiff[:, g, 0:SEQ], src[:, PH:PH + SEQ], 1.0 / win, None, ALU.mult)
                    pool.tensor_scalar(news, src[:, SEQ + PH:].rearrange("p (b t) -> p b t", b=NB)[:, :, PH:], 1.0 / win,
                                       None, ALU.mult)
                    pool.drain()
                    pool.tensor_tensor(pdiff[:, g, 0:16], src[:, PH:PH + 16], con[:, K_CNT + 16 * g:K_CNT + 16 * g + 16],
                                       ALU.mult)
                    pool.drain()
                    pool.tensor_tensor(pdiff[:, g, 0:SEQ], pdiff[:, g, 0:SEQ], xp[:, g, PH:PH + SEQ], ALU.subtract)
                    mm = pool.tensor_tensor(news, news, xps[:, g, :, PH:], ALU.subtract)
                mm.then_inc(p_diff, 1)

                def gate(blk):
                    cols = slice(blk * P, (blk + 1) * P)
                    pool.wait_ge(y_out, l * 12 + 4 * blk + 4)
                    alone(pool)
                    pool.tensor_tensor(y[:, :, cols], y[:, :, cols], z[:, :, cols], ALU.mult)
                    pool.drain()
                    pool.tensor_tensor(z[:, :, cols], y[:, :, cols], y[:, :, cols], ALU.mult)
                    pool.drain()
                    pool.tensor_tensor(z[:, 0:4, cols], z[:, 0:4, cols], z[:, 4:8, cols], ALU.add).then_inc(y_sq, 1)

                gate(0)
                pool.wait_ge(st_new, l * 2 + 2)
                alone(pool)
                pool.dma_start(o["new_ssm_prompt"][l, 0].rearrange("(j e) p n -> (e p) j n", e=2), snew[:]
                               ).then_inc(s_stored[0], 16)
                gate(1)
                with pool.Fori(0, NB // 2) as bb:
                    for i in range(2):
                        state_out(bb, i)
                pool.wait_ge(ptail_out, l * 2 + 2)
                alone(pool)
                pool.dma_start(o["new_pool_prompt"][l, 0], ptailP[:]).then_inc(tail_stored, 16)
                pool.dma_start(o["new_pool_sample"][l].rearrange("b k c -> (b k) c"), ptail[0:NB * PH, :]
                               ).then_inc(tail_stored, 16)
                for i in range(2):
                    pool.wait_ge(s_stored[i], l * 80 + 80)
                    alone(pool)
                pool.wait_ge(tail_stored, l * 80 + 48)
                alone(pool)
                meet(pool, "pool", stage(l, M_MIX))
                meet(pool, "pool", stage(l, M_OUT))
                square()
                for half in range(2):
                    pool.dma_start(frow[32 * half:32 * half + 16, :],
                                   a["state_ffn_conv"][l].rearrange("b k c -> (b k) c")[
                                       :, half * (FF // 2):(half + 1) * (FF // 2)]).then_inc(frow_loaded, 16)
                pool.wait_ge(ftail_out, l * 11 + 11)
                alone(pool)
                pool.dma_start(o["new_ffn_conv_prompt"][l, 0], ftail[0:2, :]).then_inc(tail_stored, 16)
                pool.dma_start(o["new_ffn_conv_sample"][l].rearrange("b k c -> (b k) c"), ftail[2:18, :]
                               ).then_inc(tail_stored, 16)
                pool.wait_ge(tail_stored, l * 80 + 80)
                alone(pool)
                meet(pool, "pool", stage(l, M_FFN))
            pool.wait_ge(last_out, 12)
            pool.dma_start(o["y_prompt"][0].rearrange("(c p) d -> p c d", p=P), xrow[:, 0:2, :]
                           ).then_inc(last_stored, 16)
            pool.dma_start(o["y_sample"].rearrange("b t d -> (b t) d"), xrow[0:SAMP, 2, :]).then_inc(last_stored, 16)
            pool.wait_ge(last_stored, 32)

        @block.scalar
        def _(act):
            def hi(l, body, s, rows=8):
                act.wait_ge(raw_loaded[s], (l * BODIES + body + 1) * 16)
                for h in range(2):
                    act.wait_ge(unit_done, (l * BODIES + body) * 8 + (2 * s + h + 1))
                    half = slice(h * rows // 2, (h + 1) * rows // 2)
                    act.activation(wh[:, s % 2, half, :], raw[:, s, half, :], ACT.Copy).then_inc(hi_done, 1)

            def body(l, b, first, second, rows=8, ahead=False):
                if not ahead:
                    hi(l, b, 0, rows)
                first and first()
                for s in range(1, 4):
                    hi(l, b, s, rows)
                second and second()

            def bodies(l, base, n, pending, task, rows=8, ahead=False):
                body(l, base, *(pending or (None, None)), rows, ahead)
                if n > 1:
                    with act.Fori(1, n) as i:
                        body(l, i + base, task and (lambda: task(i - 1, 0)), task and (lambda: task(i - 1, 1)), rows)
                return task and (lambda: task(n - 1, 0), lambda: task(n - 1, 1))

            def norm_high(l, col):
                for t in range(KT):
                    act.activation(hh[:, t, :], x[:, t, :], ACT.Copy, scale=par[:, col + t:col + t + 1]
                                   ).then_inc(h_hi, 1)

            def norm_root(n):
                act.wait_ge(mean_sq, n)
                act.activation(rstd[:], rstd[:], ACT.Sqrt).then_inc(root, 1)

            def log1p_exp(ap):
                act.activation(ap, ap, ACT.Exp, scale=-1.0)
                act.drain()
                return act.activation(ap, ap, ACT.Ln, bias=1.0)

            meet(act, "act", 1)
            with act.Fori(0, DEPTH) as l:
                for dst, src in (
                    (prow[0:16, 0, :], wrow("norm1", l, "(t p) -> t p")),
                    (prow[16:32, 0, :], wrow("norm2", l, "(t p) -> t p")),
                    (prow[32:80, 0, :], wrow("ssd_conv_w", l, "k (t p) -> (k t) p")),
                    (prow[80:92, 0, :], wrow("ssd_conv_b", l, "(t p) -> t p")),
                    (prow[92:100, 0, :], wrow("ssd_norm", l, "(t p) -> t p")),
                    (prow[100:104, 0, :], wrow("pool_scale", l, "(t p) -> t p")),
                    (prow[0:88, 1, :], wrow("ffn_conv_w", l, "k (t p) -> (k t) p")[0:88, :]),
                    (prow[0:44, 2, :], wrow("ffn_conv_w", l, "k (t p) -> (k t) p")[88:132, :]),
                    (prow[44:88, 2, :], wrow("ffn_conv_b", l, "(t p) -> t p")),
                    (wdt_raw[:], a["w_in"].rearrange("l (k p) n -> l p k n", p=P)[l, :, :, DTC:DTC + SSH]),
                ):
                    act.dma_start(dst, src).then_inc(par_loaded, 16)
                act.wait_ge(par_out, l + 1)
                act.activation(wdt_hi[:], wdt_raw[:], ACT.Copy).then_inc(wdt_split, 1)
                norm_high(l, C_N1)

                def silu_xbc(i, g):
                    act.wait_ge(conv_done, l * 32 + i * 2 + (g + 1))
                    t = xc[:, ds(i * 4 + 2 * g, 2), :]
                    act.activation(t, t, ACT.Silu)

                def silu_z(i, g):
                    act.wait_ge(conv_done, l * 32 + i * 2 + (g + 7))
                    t = z[:, ds(i * 4 + 2 * g, 2), :]
                    act.activation(t, t, ACT.Silu)

                left = bodies(l, B_XBC, 3, (None, lambda: norm_root(l * 2 + 1)), silu_xbc)
                left = bodies(l, B_QKV, 3, left, None)
                left = bodies(l, B_Z, 2, left, silu_z)
                left = bodies(l, B_XP, 1, left, None)
                meet(act, "act", stage(l, M_IN))

                def z_logs(n, ap):
                    act.wait_ge(z_abs, l * 17 + n + 1)
                    log1p_exp(ap).then_inc(z_log, 1)

                def z_weights(n, ap):
                    act.wait_ge(z_arg, l * 17 + n + 1)
                    act.activation(ap, ap, ACT.Exp).then_inc(z_w, 1)

                def head(buf, n):
                    return buf[:].rearrange("p a c -> p (a c)")[:, 512 * (n % 2):512 * (n % 2) + 384]

                def head_high(n):
                    r = slice(DH * (n % 2), DH * (n % 2) + DH)
                    act.wait_ge(o_mm, l * 16 + n + 1)
                    act.activation(hh[r, n // 2, 0:SEQ], ps[6 + n % 2][r, 0:SEQ], ACT.Copy).then_inc(o_hi, 1)

                z_logs(0, head(za, 0))
                for n in range(8):
                    if n < 7:
                        z_logs(n + 1, head(za, n + 1))
                    else:
                        z_logs(8, za[0:SAMP, 0:8, :])
                    z_weights(n, head_buf(n))
                    if n:
                        head_high(n - 1)
                head_high(7)
                z_weights(8, zn[:])

                def page_copies(b, between={}):
                    for p in range(PAGES):
                        if p in ACT_PAGES:
                            act.wait_ge(k_T, (l * NB + b) * PAGES + (p + PAGES + 1))
                            act.wait_ge(z_page, (l * NB + b) * PAGES + (p + 1))
                            act.activation(kT[:, p % 2, :], ps[4 + p % 2][:], ACT.Copy).then_inc(kT_out["act"], 1)
                        if p in between:
                            between[p]()

                def weigh(b, i):
                    z_weights(b + 9, zz_of[i][:])

                def outputs(b):
                    act.wait_ge(o_fold, b + (l * NB + 1))
                    act.activation(hh[:, 0:SBT, ds(b * NT + SEQ, NT)],
                                   ps[7][:, 0:SBT * NT].rearrange("p (j t) -> p j t", j=SBT), ACT.Copy
                                   ).then_inc(o_hi, 1)

                page_copies(0)
                page_copies(1, {1: lambda: z_logs(9, za[:]), 11: lambda: weigh(0, 0)})
                with act.Fori(0, NB // 2 - 1) as bb:
                    for i in (1, 2):
                        b = bb * 2 + i
                        page_copies(bb * 2 + (i + 1), {1: lambda: z_logs(b + 9, za[:]),
                                                       2: lambda: outputs(bb * 2 + (i - 1)),
                                                       11: lambda: weigh(b, i % 2)})
                z_logs(NB + 8, za[:])
                outputs(NB - 2)
                weigh(NB - 1, 1)
                outputs(NB - 1)
                meet(act, "act", stage(l, M_ATTN))

                act.wait_ge(dt_abs, l + 1)
                act.activation(dtb[:, 1:2], dtb[:, 1:2], ACT.Exp)
                log1p_exp(dtT[:, 1, :]).then_inc(dt_log, 1)
                act.wait_ge(cend_sum, l + 1)
                act.activation(cend[:], cend[:], ACT.Exp).then_inc(cend_exp, 1)
                for blk in range(3):
                    t0, T = tokens(blk)
                    act.wait_ge(blk_end, l * 3 + blk + 1)
                    act.activation(tk[0:T, 3, :], tk[0:T, 3, :], ACT.Exp).then_inc(blk_exp, 1)
                    for j in range(4):
                        n = blk * 4 + j
                        seg = seg2[n % 2]
                        act.wait_ge(c_seg, l * 12 + n + 1)
                        mm = act.activation(seg[0:T, :, 0:T], seg[0:T, :, 0:T], ACT.Exp)
                        if blk == 1 and j >= 2:
                            act.wait_ge(y_mm, l * 12 + n - 1)
                            alone(act)
                        if blk:
                            dst = cs2[j % 2][:] if blk == 1 else csS[:, 4 * j:4 * j + 4, :]
                            mm = act.activation(dst, ps[5 + j % 2][:, 0:4 * T].rearrange("p (h t) -> p h t", h=4),
                                                ACT.Exp)
                        mm.then_inc(c_exp, 1)
                with act.Fori(0, NB // 4) as qq:
                    for i in range(4):
                        act.wait_ge(s_T, qq * 4 + (l * NB + i + 1))
                        for c in range(2):
                            mm = act.activation(sT[:, i % 2, c * 512:(c + 1) * 512], ps[(0, 1, 4, 7)[2 * (i % 2) + c]][:],
                                                ACT.Copy)
                        mm.then_inc(s_Tout, 1)
                act.wait_ge(p_mm, l + 1)
                for g in range(PLT):
                    mm = act.activation(hh[:, SBT + SST + g, :], ps[POOL_BANKS[g]][:, 0:TOK], ACT.Copy,
                                        scale=par[:, C_PS + g:C_PS + g + 1])
                mm.then_inc(p_hi, 1)
                act.wait_ge(y_ms, l + 1)
                act.activation(rstd[:], rstd[:], ACT.Sqrt).then_inc(y_root, 1)
                for t in range(SST):
                    act.wait_ge(y_normed, l * SST + t + 1)
                    act.activation(hh[:, SBT + t, :], y[:, t, :], ACT.Copy).then_inc(y_hi, 1)
                meet(act, "act", stage(l, M_MIX))

                bodies(l, B_OUT, 4, None, None)
                hi(l, B_PART[0][0], 0)
                meet(act, "act", stage(l, M_OUT))
                norm_high(l, C_N2)
                done = 10
                for part, tiles in enumerate(PARTS):
                    up, down = B_PART[part]

                    def silu_gate(i, g, done=done):
                        if g == 0:
                            act.wait_ge(conv_done, l * 32 + i + (done + 1))
                            act.activation(gc[:], gc[:], ACT.Silu).then_inc(silu_done, 1)

                    left = bodies(l, up, tiles // 2, None if part else (None, lambda: norm_root(l * 2 + 2)), silu_gate,
                                  ahead=not part)
                    bodies(l, down, 4, left, None, tiles // 2)
                    done += tiles // 2
                meet(act, "act", stage(l, M_FFN))
            act.activation(sq[:, 0:8, :], x[:, 0:8, :], ACT.Square).then_inc(last_squares, 1)
            norm_root(2 * DEPTH + 1)

        @block.tensor
        def _(pe):
            def products(l, base, n, hi, lo, half=8, between=None, ready=None):
                def one(b, between=None, ready=None):
                    g0 = (l * BODIES + b)
                    for s in range(4):
                        if s % 2 == 0:
                            pe.wait_ge(group_out, g0 * 2 + (s // 2 + 1))
                        if s % 2 == 1 and base in DOWN:
                            pe.wait_ge(part_ready, l * 3 + DOWN.index(base) + 1)
                        for h in range(2):
                            pe.wait_ge(lo_done, g0 * 8 + (2 * s + h + 9))
                            for kk in range(h * half // 2, (h + 1) * half // 2):
                                if ready and s < 2:
                                    ready((s % 2) * half + kk)
                                for t in range(2):
                                    row = (s % 2) * half + kk
                                    out = ps[2 * (s // 2) + t][:, 0:TOK]
                                    w = slice(t * P, t * P + P)
                                    first, last = row == 0, row == 2 * half - 1
                                    pe.matmul(out, wh[:, s % 2, kk, w], hi[:, row, :], start=first, stop=False)
                                    pe.matmul(out, wh[:, s % 2, kk, w], lo[:, row, :], start=False, stop=False)
                                    mm = pe.matmul(out, wl[:, s % 2, kk, w], hi[:, row, :], start=False, stop=last)
                            mm.then_inc(unit_done, 1)
                        if s == 1 and between:
                            between()

                if between or n == 1:
                    one(base, between, ready)
                if n > 1:
                    with pe.Fori(1 if between else 0, n) as i:
                        one(i + base)

            DOWN = [down for _, down in B_PART]

            def norm_sum(n, squared=None):
                if squared is None:
                    pe.wait_ge(squares, n)
                else:
                    pe.wait_ge(squared, 1)
                for t in range(4):
                    mm = pe.matmul(ps[7][:, 0:TOK], ones, sq[:, t, :], start=(t == 0), stop=(t == 3))
                mm.then_inc(sq_sum, 1)

            pe.sem_inc(unit_done, 4)
            pe.sem_inc(k_T, PAGES)
            pe.sem_inc(v_used, 2)
            pe.sem_inc(z_page, 2)
            pe.wait_ge(first_loaded, 80)
            pe.transpose(ps[7][:, 0:KT], frows[:], ident[0:KT, 0:KT]).then_inc(first_T, 1)
            for n in range(12):
                c, j = n // 4, n % 4
                T = P if c < 2 else SAMP
                if c:
                    pe.wait_ge(first_out, n - 2)
                for i in range(4):
                    mm = pe.transpose(ps[j][:, i * T:(i + 1) * T], xrow[0:T, c, (4 * j + i) * P:(4 * j + i + 1) * P],
                                      ident[0:T, 0:T])
                mm.then_inc(first_T, 1)
            meet(pe, "pe", 1)

            with pe.Fori(0, DEPTH) as l:
                pe.wait_ge(par_loaded, l * (10 * 16) + 10 * 16)
                for c, (n, col) in enumerate(((104, 0), (88, 104), (88, 192))):
                    mm = pe.transpose(ps[4][:, col:col + n], prow[0:n, c, :], ident[0:n, 0:n])
                mm.then_inc(rows_T, 1)

                def histories():
                    pe.wait_ge(rows_loaded, l * (6 * 16) + 6 * 16)
                    alone(pe)
                    for t in range(CVT):
                        mm = pe.transpose(ps[5][:, t * 24:t * 24 + 24], crow[:, t * P:(t + 1) * P], ident[0:24, 0:24])
                    mm.then_inc(rows_T, 1)
                    for t in range(PLT):
                        mm = pe.transpose(ps[6][:, t * 120:t * 120 + 120], plrow[:, t * P:(t + 1) * P],
                                          ident[0:120, 0:120])
                    mm.then_inc(rows_T, 1)


                pe.wait_ge(wdt_ready, l + 1)
                for t in range(KT):
                    pe.wait_ge(h_lo, l * 32 + t + 1)
                    pe.matmul(ps[4][0:SSH, 0:TOK], wdt_hi[:, t, :], hh[:, t, :], start=(t == 0), stop=False)
                    pe.matmul(ps[4][0:SSH, 0:TOK], wdt_hi[:, t, :], hl[:, t, :], start=False, stop=False)
                    mm = pe.matmul(ps[4][0:SSH, 0:TOK], wdt_lo[:, t, :], hh[:, t, :], start=False,
                                   stop=(t == KT - 1))
                mm.then_inc(dt_mm, 1)
                products(l, B_XBC, 3, hh, hl, between=lambda: (norm_sum(l * 2 + 1), histories()))
                products(l, B_QKV, 3, hh, hl)
                products(l, B_Z, 2, hh, hl)
                products(l, B_XP, 1, hh, hl)
                meet(pe, "pe", stage(l, M_IN))

                for n in range(6):
                    c, src = n // 2, (k, v)[n % 2]
                    T = P if c < 2 else SAMP
                    if n >= 2:
                        pe.wait_ge(tok_out, l * 6 + (n - 1))
                        alone(pe)
                    for t in range(SBT):
                        mm = pe.transpose(ps[4 + n % 2][0:T, t * P:(t + 1) * P], src[:, t, c * P:c * P + T], ident)
                    mm.then_inc(tok_T, 1)

                def head_z(n):
                    if n >= 2:
                        pe.wait_ge(z_out, l * 17 + (n - 1))
                        alone(pe)
                    r, b = slice(DH * (n % 2), DH * (n % 2) + DH), ps[n % 2]
                    pe.matmul(b[:, 0:SEQ], k[r, n // 2, 0:P], q[r, n // 2, 0:SEQ], start=True, stop=True)
                    pe.matmul(b[:, SEQ:SEQ + P], k[r, n // 2, P:SEQ], q[r, n // 2, P:SEQ], start=True, stop=True
                              ).then_inc(z_mm, 1)

                def head_sums(n):
                    pe.wait_ge(z_sp, l * 17 + (n + 1))
                    if n >= 2:
                        pe.wait_ge(z_arg, l * 17 + (n - 1))
                    b = ps[2 + n % 2]
                    s_ = sp[:].rearrange("p a c -> p (a c)")[:, 512 * (n % 2):512 * (n % 2) + 384]
                    pe.matmul(b[:, 0:P], tri_ge, s_[:, 0:P], start=True, stop=True)
                    pe.matmul(b[:, P:SEQ], tri_ge, s_[:, P:SEQ], start=True, stop=False)
                    pe.matmul(b[:, P:SEQ], ones, s_[:, SEQ:384], start=False, stop=True)
                    pe.matmul(b[:, SEQ:384], tri_ge, s_[:, SEQ:384], start=True, stop=True).then_inc(s_mm, 1)

                def head_out(n):
                    pe.wait_ge(z_w, l * 17 + (n + 1))
                    if n >= 2:
                        pe.wait_ge(o_out, l * 16 + (n - 1))
                    r, b = slice(DH * (n % 2), DH * (n % 2) + DH), ps[6 + n % 2]
                    w = head_buf(n)
                    pe.matmul(b[r, 0:P], v_tok[:, 0, n * DH:(n + 1) * DH], w[:, 0:P], start=True, stop=True)
                    pe.matmul(b[r, P:SEQ], v_tok[:, 0, n * DH:(n + 1) * DH], w[:, P:SEQ], start=True, stop=False)
                    pe.matmul(b[r, P:SEQ], v_tok[:, 1, n * DH:(n + 1) * DH], w[:, SEQ:384], start=False, stop=True
                              ).then_inc(o_mm, 1)

                head_z(0)
                pe.wait_ge(tok_out, l * 6 + 6)
                alone(pe)
                for n in range(8):
                    if n < 7:
                        head_z(n + 1)
                    else:
                        pe.wait_ge(z_out, l * 17 + 7)
                        alone(pe)
                        for h in range(SBH):
                            r = slice(DH * (h % 2), DH * (h % 2) + DH)
                            mm = pe.matmul(ps[4 * (h % 2)][0:SAMP, h * SAMP:(h + 1) * SAMP], k[r, h // 2, SEQ:TOK],
                                           q[r, h // 2, SEQ:TOK], start=True, stop=True)
                        mm.then_inc(z_mm, 1)
                    head_sums(n)
                    if n:
                        head_out(n - 1)
                head_out(7)
                pe.wait_ge(z_sp, l * 17 + 9)
                pe.wait_ge(z_arg, l * 17 + 7)
                alone(pe)
                pe.matmul(ps[2][0:SAMP, :], tri_ge[0:SAMP, 0:SAMP], spn[:].rearrange("p h c -> p (h c)"), start=True,
                          stop=True).then_inc(s_mm, 1)

                def copied(g, p):
                    name, mine = ("dve", DVE_PAGES) if p % PAGES in DVE_PAGES else ("act", ACT_PAGES)
                    before = len([m for m in mine if m <= p % PAGES]) - (len(mine) if p < 0 else 0)
                    pe.wait_ge(kT_out[name], g * len(mine) + (before + (2 if name == "dve" else 0)))

                def page_z(b, p):
                    copied(l * NB + b, p)
                    if p == 0:
                        pe.wait_ge(z_out, b + l * 17 + 9)
                    for j in range(SBT):
                        mm = pe.matmul(ps[p // 8][:, (p % 8) * 64 + j * 16:(p % 8) * 64 + j * 16 + 16],
                                       kT[:, p % 2, j * P:(j + 1) * P],
                                       qd[:, j, ds(b, 1), :, :].rearrange("p b e t -> p (b e t)"),
                                       start=True, stop=True)
                    mm.then_inc(z_page, 1)

                def pages_z(b, between={}):
                    g = l * NB + b
                    for p in range(PAGES):
                        if p % 4 == 0:
                            pe.wait_ge(k_loaded[p // 4], g * 64 + 64)
                        copied(g, p - 2)
                        for j in range(SBT):
                            mm = pe.transpose(ps[4 + p % 2][:, j * P:(j + 1) * P], kring[:, p, j * P:(j + 1) * P],
                                              ident)
                        mm.then_inc(k_T, 1)
                        if p:
                            page_z(b, p - 1)
                        if p in between:
                            between[p]()
                    page_z(b, PAGES - 1)

                def pages_sums(b):
                    pe.wait_ge(z_sp, b + l * 17 + 10)
                    pe.wait_ge(z_arg, b + l * 17 + 9)
                    for half in range(2):
                        pe.matmul(ps[2 + half][:], tri_ge, sp[:, 8 * half:8 * half + 8, :], start=True, stop=False)
                        mm = pe.matmul(ps[2 + half][:], ones, rs[:, 8 * half:8 * half + 8, :], start=False, stop=True)
                    mm.then_inc(s_mm, 1)

                def pages_out(b, i, first=False):
                    pe.wait_ge(z_w, b + l * 17 + 10)
                    pe.wait_ge(v_loaded, (l * NB + b) * 256 + 256)
                    if first:
                        pe.wait_ge(o_out, l * 16 + 7)
                    else:
                        pe.wait_ge(o_masked, b + l * NB)
                    for p in range(PAGES):
                        for j in range(SBT):
                            mm = pe.matmul(ps[6][32 * j:32 * j + 16, 0:P], zz_of[i][:, p, 16 * j:16 * j + 16],
                                           vring[:, p, j * P:(j + 1) * P], start=(p == 0), stop=False)
                        if p % 8 == 7:
                            mm.then_inc(v_used, 1)
                    for j in range(SBT):
                        mm = pe.matmul(ps[6][32 * j:32 * j + 16, 0:P], znb[:, 16 * j:16 * j + 16],
                                       v_tok[0:SAMP, 2, j * P:(j + 1) * P], start=False, stop=True)
                    mm.then_inc(o_mm, 1)

                def pages_fold(b):
                    pe.wait_ge(o_masked, b + (l * NB + 1))
                    pe.wait_ge(o_out, b + (l * 16 + 8))
                    pe.matmul(ps[7][:, 0:SBT * NT], o_rows[:], con[:, K_TOK:K_TOK + SBT * NT], start=True, stop=True
                              ).then_inc(o_fold, 1)

                pe.wait_ge(q_ready, l + 1)
                pe.wait_ge(z_out, l * 17 + 9)
                alone(pe)
                pages_z(0)
                pe.wait_ge(z_w, l * 17 + 9)
                alone(pe)
                pages_z(1, {7: lambda: pages_sums(0)})
                pages_out(0, 0, first=True)
                with pe.Fori(0, NB // 2 - 1) as bb:
                    for i in (1, 2):
                        b = bb * 2 + i
                        pages_z(bb * 2 + (i + 1), {2: lambda: pages_fold(bb * 2 + (i - 1)), 7: lambda: pages_sums(b)})
                        pages_out(b, i % 2)
                pages_fold(NB - 2)
                pages_sums(NB - 1)
                pages_out(NB - 1, 1)
                pages_fold(NB - 1)
                meet(pe, "pe", stage(l, M_ATTN))

                for c in range(3):
                    for t in range(4):
                        mm = pe.transpose(ps[c][0:27, t * P:(t + 1) * P], tail_c[:, 4 * c + t, :], ident)
                    mm.then_inc(ctail_T, 1)
                pe.wait_ge(cend_exp, l + 1)
                pe.wait_ge(sel_loaded, l * 16 + 16)
                for j in range(SST):
                    mm = pe.matmul(ps[3][:, j * 10:(j + 1) * 10], sel[:, j, :], cend[:], start=True, stop=True)
                mm.then_inc(dec_mm, 1)
                pe.wait_ge(dec_out, l + 1)
                pe.wait_ge(ctail_out, l * 3 + 3)
                for blk in range(3):
                    t0, T = tokens(blk)
                    cols = slice(t0, t0 + T)
                    if blk:
                        pe.wait_ge(y_out, l * 12 + blk * 4)
                        pe.wait_ge(st_new, l * 2 + blk)
                        alone(pe)
                    if blk == 1:
                        pe.wait_ge(ptail_in, l + 1)
                        alone(pe)
                        for t in range(PLT):
                            mm = pe.transpose(ps[7][0:PH, t * P:(t + 1) * P], xp[:, t, SEQ:SEQ + PH], ident)
                        mm.then_inc(ptail_T, 1)
                    elif blk == 2:
                        pe.wait_ge(ptail_out, l * 2 + 1)
                        alone(pe)
                        for t in range(PLT):
                            mm = pe.transpose(ps[7][0:NB * PH, t * P:(t + 1) * P], ptmp[:, t, :], ident)
                        mm.then_inc(ptail_T, 1)
                    for t in range(SST + NG):
                        pe.transpose(ps[t // 4][0:T, (t % 4) * P:(t % 4 + 1) * P], xc[:, t, cols], ident)
                    for i in range(2):
                        mm = pe.transpose(ps[3][0:T, i * SSH:(i + 1) * SSH], dtT[:, i, cols], ident[0:SSH, 0:SSH])
                    mm.then_inc(blk_T, 1)
                    le = tri_le if blk < 2 else con[0:T, K_SLE:K_SLE + T]
                    one = ones if blk < 2 else con[0:T, K_SONE:K_SONE + T]
                    pe.wait_ge(blk_tok, l * 3 + blk + 1)
                    alone(pe)
                    pe.matmul(ps[3][0:T, 32:48], le, tk[0:T, 1, :], start=True, stop=True)
                    pe.matmul(ps[3][0:T, 48:64], one, tk[0:T, 1, :], start=True, stop=True)
                    for g in range(NG):
                        mm = pe.matmul(ps[4][0:T, g * T:(g + 1) * T], xc[:, SST + g, cols], xc[:, SST + NG + g, cols],
                                       start=True, stop=True)
                    mm.then_inc(blk_cum, 1)

                    def head_cums(j):
                        n = blk * 4 + j
                        if j >= 2:
                            pe.wait_ge(c_exp, l * 12 + n - 1)
                        for i in range(4):
                            h = 4 * j + i
                            mm = pe.matmul(ps[5 + j % 2][:, i * T:(i + 1) * T],
                                           tk[0:T, 1, h:h + 1].broadcast_to([T, P]), le, start=True, stop=True)
                        mm.then_inc(c_mm, 1)

                    def head_ys(j):
                        n = blk * 4 + j
                        pe.wait_ge(c_w, l * 12 + n + 1)
                        if j >= 2:
                            pe.wait_ge(y_out, l * 12 + n - 1)
                        alone(pe)
                        for i in range(4):
                            h = 4 * j + i
                            out = ps[j % 2][DH * (i % 2):DH * (i % 2) + DH, (i // 2) * T:(i // 2 + 1) * T]
                            mm = pe.matmul(out, xtok[0:T, h * DH:(h + 1) * DH], wts[0:T, i, 0:T], start=True,
                                           stop=(blk != 1))
                            if blk == 1:
                                mm = pe.matmul(out, s1T[:, h * DH:(h + 1) * DH], cs2[j % 2][:, i, :], start=False,
                                               stop=True)
                        mm.then_inc(y_mm, 1)

                    head_cums(0)
                    head_cums(1)
                    for j in range(4):
                        if j < 2:
                            head_cums(j + 2)
                        head_ys(j)
                    if blk < 2:
                        pe.wait_ge(blk_xw, l * 3 + blk + 1)
                        pe.wait_ge(c_w, l * 12 + blk * 4 + 4)
                        if blk == 0:
                            for g, b in enumerate((2, 4)):
                                pe.matmul(ps[b][:], xtok[:, SSW + g * NS:SSW + (g + 1) * NS],
                                          xw[:, g * 512:(g + 1) * 512], start=True, stop=True)
                        for j in range(SST):
                            g = j // 4
                            mm = pe.matmul(ps[5 + g][:, (j % 4) * NS:(j % 4 + 1) * NS], xw[:, j * P:(j + 1) * P],
                                           xtok[:, SSW + g * NS:SSW + (g + 1) * NS], start=True, stop=True)
                        mm.then_inc(st_mm, 1)
                pe.wait_ge(blk_xw, l * 3 + 3)
                pe.wait_ge(y_out, l * 12 + 12)
                alone(pe)
                def states(qq, pair):
                    for i in range(2):
                        pe.wait_ge(s_loaded[2 * pair + i], qq * 16 + (l * 32 + 16))
                        for j in range(SST):
                            mm = pe.transpose(ps[(0, 1, 4, 7)[2 * i + j // 4]][:, (j % 4) * P:(j % 4 + 1) * P],
                                              s_in[:, 2 * pair + i, j, :], ident)
                        mm.then_inc(s_T, 1)
                    for i in range(2):
                        b = qq * 4 + (2 * pair + i)
                        pe.wait_ge(s_Tout, qq * 4 + (l * NB + 2 * pair + i + 1))
                        for j in range(SST):
                            v5 = ps[2 + j // 4][:].rearrange("p (j e t) -> p j e t", j=4, e=2)
                            pe.matmul(v5[:, j % 4, :, ds(b * NT, NT)], sT[:, i, j * P:(j + 1) * P],
                                      csS[:, 2 * j:2 * j + 2, ds(b * NT, NT)], start=True, stop=True)
                        if i == 0:
                            pe.wait_ge(s_bm, qq * 2 + (l * (NB // 2) + pair + 1))
                        else:
                            pe.wait_ge(s_new, qq * 4 + (l * NB + 2 * pair + 1))
                        for j in range(SST):
                            g = j // 4
                            mm = pe.matmul(ps[5 + g][:, (j % 4) * NS:(j % 4 + 1) * NS], xw[0:SAMP, j * P:(j + 1) * P],
                                           bm[:, i, g * NS:(g + 1) * NS], start=True, stop=True)
                        mm.then_inc(s_mm2, 1)

                with pe.Fori(0, NB // 4) as qq:
                    states(qq, 0)
                    states(qq, 1)
                pe.wait_ge(poolw_loaded, l * 16 + 16)
                pe.wait_ge(p_diff, l + 1)
                pe.wait_ge(s_new, l * NB + NB)
                alone(pe)
                for g in range(PLT):
                    mm = pe.matmul(ps[POOL_BANKS[g]][:, 0:TOK], poolw[:, g, :], pdiff[:, g, :], start=True, stop=True)
                mm.then_inc(p_mm, 1)
                for sq_done, n, cols in ((y_sq, l * 2 + 2, slice(0, SEQ)), (y_sq_s, l + 1, slice(SEQ, TOK))):
                    pe.wait_ge(sq_done, n)
                    alone(pe)
                    for t in range(4):
                        mm = pe.matmul(ps[7][:, cols], ones, z[:, t, cols], start=(t == 0), stop=(t == 3))
                mm.then_inc(y_sum, 1)
                meet(pe, "pe", stage(l, M_MIX))

                products(l, B_OUT, 4, hh, hl)
                meet(pe, "pe", stage(l, M_OUT))

                def gate_history():
                    pe.wait_ge(frow_loaded, l * 32 + 32)
                    alone(pe)
                    for t in range(FT):
                        r = slice(32 * (t // 22), 32 * (t // 22) + 16)
                        mm = pe.transpose(ps[4 + t // 22][:, (t % 22) * 16:(t % 22 + 1) * 16],
                                          frow[r, (t % 22) * P:(t % 22 + 1) * P], ident[r, r])
                    mm.then_inc(frow_T, 1)


                def h_ready(row):
                    pe.wait_ge(h_lo, row + (l * 32 + 17))

                for part, tiles in enumerate(PARTS):
                    up, down = B_PART[part]
                    products(l, up, tiles // 2, hh, hl, between=None if part else (lambda: (norm_sum(l * 2 + 2), gate_history())),
                             ready=None if part else h_ready)
                    products(l, down, 4, ah, al, tiles // 2)
                for n in range(11):
                    if n >= 4:
                        pe.wait_ge(ftail_out, l * 11 + (n - 3))
                    for t in range(4):
                        mm = pe.transpose(ps[4 + n % 4][0:18, t * P:(t + 1) * P], tail_f[:, 4 * n + t, :], ident)
                    mm.then_inc(ftail_T, 1)
                meet(pe, "pe", stage(l, M_FFN))
            norm_sum(2 * DEPTH + 1, last_summed)
            pe.wait_ge(root_taken, 1)
            for n in range(12):
                c, j = n // 4, n % 4
                T = P if c < 2 else SAMP
                if n >= 4:
                    pe.wait_ge(last_out, n - 3)
                for i in range(4):
                    mm = pe.transpose(ps[j][0:T, i * P:(i + 1) * P], x[:, 4 * j + i, c * P:c * P + T], ident)
                mm.then_inc(last_T, 1)

        @block.vector
        def _(dve):
            def lo(l, body, s, rows=8):
                for h in range(2):
                    dve.wait_ge(hi_done, (l * BODIES + body) * 8 + (2 * s + h + 1))
                    half = slice(h * rows // 2, (h + 1) * rows // 2)
                    dve.tensor_tensor(wl[:, s % 2, half, :], raw[:, s, half, :], wh[:, s % 2, half, :].bitcast(F32),
                                      ALU.subtract).then_inc(lo_done, 1)

            def body(l, b, before, after, rows=8, ahead=False):
                if not ahead:
                    lo(l, b, 0, rows)
                lo(l, b, 1, rows)
                before and before()
                lo(l, b, 2, rows)
                lo(l, b, 3, rows)
                after()

            def bodies(l, base, n, pending, task, rows=8, scale=None, ahead=False):
                def take(i, g):
                    u = (l * BODIES + i + base) * 8
                    dve.wait_ge(unit_done, u + (4 * g + 8))
                    task(i, g, (ps[2 * g], ps[2 * g + 1]))
                body(l, base, pending, lambda: (scale and scale(), take(0, 0)), rows, ahead)
                if n > 1:
                    with dve.Fori(1, n) as i:
                        body(l, i + base, lambda: take(i - 1, 1), lambda: take(i, 0), rows)
                return lambda: take(n - 1, 1)

            def scaled(dst, bank, scale=None, n=TOK):
                if scale is None:
                    return dve.tensor_tensor(dst, bank[:, 0:TOK], rstd[:], ALU.mult)
                return dve.scalar_tensor_tensor(dst, bank[:, 0:TOK], scale, rstd[:], ALU.mult, ALU.mult)

            def norm_low(l, n, col):
                for t in range(KT):
                    dve.wait_ge(h_hi, (n - 1) * KT + (t + 1))
                    dve.scalar_tensor_tensor(hl[:, t, :], x[:, t, :], par[:, col + t:col + t + 1],
                                             hh[:, t, :].bitcast(F32), ALU.mult, ALU.subtract).then_inc(h_lo, 1)

            def norm_scale(n):
                dve.wait_ge(sq_sum, n)
                dve.tensor_scalar(rstd[:], ps[7][:, 0:TOK], 1.0 / D, EPS, ALU.mult, ALU.add).then_inc(mean_sq, 1)
                dve.wait_ge(root, n)
                dve.reciprocal(rstd[:], rstd[:])
                dve.drain()

            H3 = CVK - 1
            E0 = SEQ + H3

            def ext_fill(banks, hist, nh):
                e2 = ext[:, :, E0:].rearrange("p c (b t) -> p c b t", b=NB)
                alone(dve)
                dve.drain()
                for t in range(2):
                    dve.tensor_copy(e2[:, t, :, H3 - nh:H3], hist(t))
                    dve.tensor_tensor(ext[:, t, H3:E0], banks[t][:, 0:SEQ], rstd[:, 0:SEQ], ALU.mult)
                    mm = dve.tensor_tensor(e2[:, t, :, H3:], banks[t][:, SEQ:TOK].rearrange("p (b t) -> p b t", b=NB),
                                           rstd[:, SEQ:TOK].rearrange("p (b t) -> p b t", b=NB), ALU.mult)
                mm.then_inc(group_out, 1)
                dve.drain()
                return e2

            def conv(dst, e2, taps, wcol, bcol):
                first = H3 - (taps - 1)
                for kk in range(taps):
                    for t in range(2):
                        d1 = dst(t)[:, 0:SEQ]
                        d2 = dst(t)[:, SEQ:TOK].rearrange("p (b t) -> p b t", b=NB)
                        s1 = ext[:, t, first + kk:first + kk + SEQ]
                        s2 = e2[:, t, :, first + kk:first + kk + NT]
                        if kk == 0:
                            dve.tensor_scalar(d1, s1, wcol(kk, t), bcol(t), ALU.mult, ALU.add)
                            mm = dve.tensor_scalar(d2, s2, wcol(kk, t), bcol(t), ALU.mult, ALU.add)
                        else:
                            dve.scalar_tensor_tensor(d1, s1, wcol(kk, t), d1, ALU.mult, ALU.add)
                            mm = dve.scalar_tensor_tensor(d2, s2, wcol(kk, t), d2, ALU.mult, ALU.add)
                    if kk < taps - 1:
                        dve.drain()
                return mm

            dve.sem_inc(lo_done, 8)
            dve.sem_inc(group_out, 2)
            dve.sem_inc(kT_out["dve"], 2)
            dve.memset(ext[:], 0.0)
            dve.memset(xp[:, :, 0:PH], 0.0)
            dve.wait_ge(first_T, 1)
            dve.tensor_copy(fgain[:], ps[7][:, 0:KT]).then_inc(first_out, 1)
            for n in range(12):
                c, j = n // 4, n % 4
                T = P if c < 2 else SAMP
                dve.wait_ge(first_T, n + 2)
                dve.tensor_copy(x[:, 4 * j:4 * j + 4, c * P:c * P + T],
                                ps[j][:, 0:4 * T].rearrange("p (i t) -> p i t", i=4)).then_inc(first_out, 1)
            meet(dve, "dve", 1)

            with dve.Fori(0, DEPTH) as l:
                dve.wait_ge(rows_T, l * 3 + 1)
                dve.tensor_copy(par[:], ps[4][:, 0:NPAR]).then_inc(par_out, 1)
                dve.drain()
                dve.wait_ge(wdt_split, l + 1)
                alone(dve)
                dve.tensor_tensor(wdt_lo[:], wdt_raw[:], wdt_hi[:].bitcast(F32), ALU.subtract).then_inc(wdt_ready, 1)
                norm_low(l, l * 2 + 1, C_N1)

                xps = xp[:, :, SEQ + PH:].rearrange("p g (b t) -> p g b t", b=NB)

                def histories():
                    dve.wait_ge(rows_T, l * 3 + 2)
                    dve.tensor_copy(hist_c[:].rearrange("p c k -> p (c k)"), ps[5][:, 0:CVT * 24])
                    dve.wait_ge(rows_T, l * 3 + 3)
                    dve.tensor_copy(xps[:, :, :, 0:PH], ps[6][:, 0:480].rearrange("p (g b t) -> p g b t", g=PLT, b=NB))
                    dve.tensor_copy(bias64[:].rearrange("p (h t) -> p h t", h=SBH),
                                    hbias[:].unsqueeze(2).broadcast_to([P, SBH, NT]))
                    for e in range(2):
                        r = slice(DH * e, DH * e + DH)
                        dve.tensor_copy(dskip[r, :], skips[r, :].rearrange("p (j e) -> p j e", e=2)[:, :, e])
                    dve.drain()

                def take_xbc(i, g, banks):
                    c0 = i * 4 + 2 * g
                    e2 = ext_fill(banks, lambda t: hist_c[:, ds(c0 + t, 1), :].rearrange("p c (b k) -> p (c b) k", b=NB), H3)
                    for t in range(2):
                        dve.tensor_copy(tail_c[:, ds(c0 + t, 1), 0:H3].rearrange("p c k -> p (c k)"), ext[:, t, SEQ:E0])
                        dve.tensor_copy(tail_c[:, ds(c0 + t, 1), H3:].rearrange("p c (b k) -> p (c b) k", b=NB),
                                        e2[:, t, :, NT:])
                    conv(lambda t: xc[:, ds(c0 + t, 1), :].rearrange("p c k -> p (c k)"), e2, CVK,
                         lambda kk, t: par[:, ds(c0 + (t + C_CW + kk * CVT), 1)],
                         lambda t: par[:, ds(c0 + (t + C_CB), 1)]).then_inc(conv_done, 1)

                def take_qkv(i, g, banks):
                    qkv = sb_qkv[:]
                    for t in range(2):
                        mm = scaled(qkv[:, ds(i * 4 + (2 * g + t), 1), :].rearrange("p c k -> p (c k)"), banks[t])
                    mm.then_inc(group_out, 1)

                def take_z(i, g, banks):
                    for t in range(2):
                        mm = scaled(z[:, ds(i * 4 + (2 * g + t), 1), :].rearrange("p c k -> p (c k)"), banks[t])
                    mm.then_inc(group_out, 1)
                    dve.drain().then_inc(conv_done, 1)

                def take_xp(i, g, banks):
                    for t in range(2):
                        j = 2 * g + t
                        dve.tensor_tensor(xp[:, j, PH:PH + SEQ], banks[t][:, 0:SEQ], rstd[:, 0:SEQ], ALU.mult)
                        mm = dve.tensor_tensor(xps[:, j, :, PH:], banks[t][:, SEQ:TOK].rearrange("p (b t) -> p b t", b=NB),
                                               rstd[:, SEQ:TOK].rearrange("p (b t) -> p b t", b=NB), ALU.mult)
                    mm.then_inc(group_out, 1)

                left = bodies(l, B_XBC, 3, None, take_xbc, scale=lambda: (norm_scale(l * 2 + 1), histories()))
                left = bodies(l, B_QKV, 3, left, take_qkv)
                left = bodies(l, B_Z, 2, left, take_z)
                left = bodies(l, B_XP, 1, left, take_xp)
                left()
                dve.wait_ge(dt_mm, l + 1)
                dve.tensor_tensor(dtT[:, 0, :], ps[4][0:SSH, 0:TOK], rstd[0:SSH, :], ALU.mult)
                dve.drain()
                dve.tensor_scalar(q[:], q[:], DH ** -0.5, None, ALU.mult)
                meet(dve, "dve", stage(l, M_IN))

                dve.memset(qd[:], 0.0)
                dve.memset(rs[:, PAGES - 1, :], 0.0)
                dve.memset(o_rows[:], 0.0)
                dve.drain()
                for e in range(2):
                    r = slice(DH * e, DH * e + DH)
                    for j in range(SBT):
                        mm = dve.tensor_copy(qd[r, j, :, e, :], q[r, j, SEQ:TOK].rearrange("p (b t) -> p b t", b=NB))
                mm.then_inc(q_ready, 1)
                for n in range(6):
                    c, dst = n // 2, (k_tok, v_tok)[n % 2]
                    T = P if c < 2 else SAMP
                    dve.wait_ge(tok_T, l * 6 + n + 1)
                    dve.tensor_copy(dst[0:T, c, :], ps[4 + n % 2][0:T, :]).then_inc(tok_out, 1)

                def absolute(dst, src):
                    return dve.scalar_tensor_tensor(dst, src, -1.0, src, ALU.mult, ALU.max)

                def head(buf, n):
                    return buf[:].rearrange("p a c -> p (a c)")[:, 512 * (n % 2):512 * (n % 2) + 384]

                def head_in(n):
                    dve.wait_ge(z_mm, l * 9 + n + 1)
                    dve.scalar_tensor_tensor(head_buf(n), ps[n % 2][:, 0:384], hbias[:, n:n + 1],
                                             con[:, K_NEG:K_NEG + 384], ALU.add, ALU.add).then_inc(z_out, 1)
                    dve.drain()
                    absolute(head(za, n), head_buf(n)).then_inc(z_abs, 1)

                def softplus(n, dst, z_, l_):
                    dve.wait_ge(z_log, l * 17 + n + 1)
                    return dve.scalar_tensor_tensor(dst, z_, 0.0, l_, ALU.max, ALU.add)

                def argument(n, z_, s_):
                    dve.wait_ge(s_mm, l * 17 + n + 1)
                    return dve.tensor_tensor(z_, z_, s_, ALU.subtract)

                def head_low(n):
                    r = slice(DH * (n % 2), DH * (n % 2) + DH)
                    dve.wait_ge(o_hi, l * 16 + n + 1)
                    dve.tensor_tensor(hl[r, n // 2, 0:SEQ], ps[6 + n % 2][r, 0:SEQ], hh[r, n // 2, 0:SEQ].bitcast(F32),
                                      ALU.subtract).then_inc(o_out, 1)

                head_in(0)
                softplus(0, head(sp, 0), head_buf(0), head(za, 0)).then_inc(z_sp, 1)
                for n in range(8):
                    if n < 7:
                        head_in(n + 1)
                    else:
                        dve.wait_ge(z_mm, l * 9 + 9)
                        for h in range(SBH):
                            mm = dve.scalar_tensor_tensor(zn[:, h, :], ps[4 * (h % 2)][0:SAMP, h * SAMP:(h + 1) * SAMP],
                                                          hbias[0:SAMP, h:h + 1], con[0:SAMP, K_SNEG:K_SNEG + SAMP],
                                                          ALU.add, ALU.add)
                        mm.then_inc(z_out, 1)
                        dve.drain()
                        absolute(za[0:SAMP, 0:8, :], zn[:]).then_inc(z_abs, 1)
                    argument(n, head_buf(n), ps[2 + n % 2][:, 0:384]).then_inc(z_arg, 1)
                    if n < 7:
                        softplus(n + 1, head(sp, n + 1), head_buf(n + 1), head(za, n + 1)).then_inc(z_sp, 1)
                    else:
                        softplus(8, spn[:], zn[:], za[0:SAMP, 0:8, :]).then_inc(z_sp, 1)
                    if n:
                        head_low(n - 1)
                head_low(7)
                argument(8, zn[:].rearrange("p h c -> p (h c)"), ps[2][0:SAMP, :]).then_inc(z_arg, 1)

                def pages_in(b, i, first=False):
                    zz = zz_of[i]
                    dve.wait_ge(z_page, (l * NB + b) * PAGES + (PAGES + 2))
                    dve.wait_ge(o_mm, b + (l * 16 + (8 if first else 7)))
                    for half in range(2):
                        mm = dve.tensor_tensor(zz[:, 8 * half:8 * half + 8, :],
                                               ps[half][:].rearrange("p (a c) -> p a c", a=8),
                                               bias64[:].unsqueeze(1).broadcast_to([P, 8, 64]), ALU.add)
                    mm.then_inc(z_out, 1)
                    dve.drain()
                    absolute(za[:].rearrange("p a c -> p (a c)"), zz[:].rearrange("p a c -> p (a c)")).then_inc(z_abs, 1)

                def pages_sp(b, i):
                    zz = zz_of[i]
                    dve.tensor_copy(rs[0:SAMP, PAGES - 1, :].rearrange("p (h t) -> p h t", h=SBH),
                                    spn[:, :, ds(b * NT, NT)])
                    softplus(b + 9, sp[:].rearrange("p a c -> p (a c)"), zz[:].rearrange("p a c -> p (a c)"),
                             za[:].rearrange("p a c -> p (a c)"))
                    for p in reversed(range(PAGES - 1)):
                        dve.drain()
                        mm = dve.tensor_tensor(rs[:, p, :], rs[:, p + 1, :], sp[:, p + 1, :], ALU.add)
                    mm.then_inc(z_sp, 1)

                def pages_weigh(b, i):
                    zz = zz_of[i]
                    dve.tensor_copy(znb[:].rearrange("p (h t) -> p h t", h=SBH), zn[:, :, ds(b * NT, NT)])
                    dve.wait_ge(s_mm, b + l * 17 + 10)
                    for half in range(2):
                        zh = zz[:, 8 * half:8 * half + 8, :].rearrange("p a c -> p (a c)")
                        mm = dve.tensor_tensor(zh, zh, ps[2 + half][:], ALU.subtract)
                    mm.then_inc(z_arg, 1)

                def mask(b):
                    dve.wait_ge(o_mm, b + (l * 16 + 9))
                    for j in range(SBT):
                        r = slice(32 * j, 32 * j + 16)
                        mm = dve.tensor_tensor(o_rows[r, :].rearrange("p (e d) -> p e d", e=2),
                                               ps[6][r, 0:P].rearrange("p (e d) -> p e d", e=2),
                                               con[r, K_HEAD:K_HEAD + 2].unsqueeze(2).broadcast_to([16, 2, DH]),
                                               ALU.mult)
                    mm.then_inc(o_masked, 1)

                def outputs_low(b):
                    dve.wait_ge(o_hi, b + l * 16 + 9)
                    dst = (hl[:, 0:SBT, ds(b * NT + SEQ, NT)], hh[:, 0:SBT, ds(b * NT + SEQ, NT)].bitcast(F32))
                    dve.tensor_tensor(dst[0], ps[7][:, 0:SBT * NT].rearrange("p (j t) -> p j t", j=SBT), dst[1],
                                      ALU.subtract).then_inc(o_out, 1)

                def page_copies(b, pages):
                    for p in pages:
                        dve.wait_ge(k_T, (l * NB + b) * PAGES + (p + PAGES + 1))
                        dve.wait_ge(z_page, (l * NB + b) * PAGES + (p + 1))
                        dve.tensor_copy(kT[:, p % 2, :], ps[4 + p % 2][:]).then_inc(kT_out["dve"], 1)

                early, late = DVE_PAGES[:2], DVE_PAGES[2:]
                page_copies(0, DVE_PAGES)
                pages_in(0, 0, first=True)
                page_copies(1, early)
                pages_sp(0, 0)
                dve.wait_ge(z_w, l * 17 + 9)
                alone(dve)
                pages_weigh(0, 0)
                page_copies(1, late)
                dve.wait_ge(kv_stored, l * 64 + 64)
                alone(dve)
                pages_in(1, 1)
                mask(0)
                with dve.Fori(0, NB // 2 - 1) as bb:
                    for i in (1, 2):
                        b = bb * 2 + i
                        page_copies(bb * 2 + (i + 1), early)
                        pages_sp(b, i % 2)
                        pages_weigh(b, i % 2)
                        outputs_low(bb * 2 + (i - 1))
                        page_copies(bb * 2 + (i + 1), late)
                        pages_in(bb * 2 + (i + 1), (i + 1) % 2)
                        mask(b)
                pages_sp(NB - 1, 1)
                outputs_low(NB - 2)
                pages_weigh(NB - 1, 1)
                mask(NB - 1)
                outputs_low(NB - 1)
                meet(dve, "dve", stage(l, M_ATTN))

                dve.tensor_scalar(dtT[:, 0, :], dtT[:, 0, :], dtb[:, 0:1], None, ALU.add)
                dve.drain()
                absolute(dtT[:, 1, :], dtT[:, 0, :]).then_inc(dt_abs, 1)
                for c in range(3):
                    dve.wait_ge(ctail_T, l * 3 + c + 1)
                    dve.tensor_copy(ctail[:, c * 512:(c + 1) * 512], ps[c][0:27, :]).then_inc(ctail_out, 1)
                dve.wait_ge(dt_log, l + 1)
                dve.scalar_tensor_tensor(dtT[:, 0, :], dtT[:, 0, :], 0.0, dtT[:, 1, :], ALU.max, ALU.add)
                dve.drain()
                dve.tensor_scalar(dtT[:, 1, :], dtT[:, 0, :], dtb[:, 1:2], -1.0, ALU.mult, ALU.mult)
                dve.drain()
                dve.tensor_reduce(cend[:, 0:2], dtT[:, 1, 0:SEQ].rearrange("p (c t) -> p c t", c=2), AX.X, ALU.add)
                dve.tensor_reduce(cend[:, 2:10], dtT[:, 1, SEQ:TOK].rearrange("p (c t) -> p c t", c=NB), AX.X, ALU.add
                                  ).then_inc(cend_sum, 1)
                dve.wait_ge(dec_mm, l + 1)
                dve.tensor_copy(dec[:], ps[3][:, 0:80].rearrange("p (j c) -> p j c", j=SST)).then_inc(dec_out, 1)
                for blk in range(3):
                    t0, T = tokens(blk)
                    cols = slice(t0, t0 + T)
                    dve.wait_ge(blk_T, l * 3 + blk + 1)
                    for c, w in enumerate((512, 512, 256)):
                        dve.tensor_copy(xtok[0:T, c * 512:c * 512 + w], ps[c][0:T, 0:w])
                    dve.tensor_copy(tk[0:T, 0:2, :], ps[3][0:T, 0:32].rearrange("p (i h) -> p i h", i=2)
                                    ).then_inc(blk_tok, 1)
                    dve.wait_ge(blk_cum, l * 3 + blk + 1)
                    dve.tensor_copy(tk[0:T, 2, :], ps[3][0:T, 32:48])
                    dve.drain()
                    dve.tensor_tensor(tk[0:T, 3, :], ps[3][0:T, 48:64], tk[0:T, 2, :], ALU.subtract
                                      ).then_inc(blk_end, 1)
                    le = tri_le if blk < 2 else con[0:T, K_SLE:K_SLE + T]
                    dve.tensor_tensor(cbm[0:T, :, 0:T], ps[4][0:T, 0:2 * T].rearrange("p (g t) -> p g t", g=2),
                                      le.unsqueeze(1).broadcast_to([T, NG, T]), ALU.mult)
                    dve.wait_ge(blk_exp, l * 3 + blk + 1)
                    dve.tensor_tensor(tk[0:T, 4, :], tk[0:T, 3, :], tk[0:T, 0, :], ALU.mult)
                    dve.drain()
                    dve.tensor_tensor(xw[0:T, :].rearrange("p (h d) -> p h d", h=SSH),
                                      xtok[0:T, 0:SSW].rearrange("p (h d) -> p h d", h=SSH),
                                      tk[0:T, 4, :].unsqueeze(2).broadcast_to([T, SSH, DH]), ALU.mult
                                      ).then_inc(blk_xw, 1)

                    def exponents(j):
                        n = blk * 4 + j
                        dve.wait_ge(c_mm, l * 12 + n + 1)
                        for i in range(4):
                            mm = dve.tensor_scalar(seg2[n % 2][0:T, i, 0:T], ps[5 + j % 2][0:T, i * T:(i + 1) * T],
                                                   tk[0:T, 2, 4 * j + i:4 * j + i + 1], 0.0, ALU.subtract, ALU.min)
                        mm.then_inc(c_seg, 1)

                    def head_weights(j):
                        n = blk * 4 + j
                        dve.wait_ge(c_exp, l * 12 + n + 1)
                        if n:
                            dve.wait_ge(y_mm, l * 12 + n)
                        for i in range(4):
                            mm = dve.scalar_tensor_tensor(wts[0:T, i, 0:T], seg2[n % 2][0:T, i, 0:T],
                                                          tk[0:T, 0, 4 * j + i:4 * j + i + 1], cbm[0:T, j // 2, 0:T],
                                                          ALU.mult, ALU.mult)
                        if blk:
                            dst = cs2[j % 2][:] if blk == 1 else csS[:, 4 * j:4 * j + 4, :]
                            mm = dve.tensor_tensor(dst, dst, xc[:, SST + NG + j // 2, cols].unsqueeze(1).broadcast_to(
                                [P, 4, T]), ALU.mult)
                        mm.then_inc(c_w, 1)

                    def heads_out(j):
                        dve.wait_ge(y_mm, l * 12 + blk * 4 + j + 1)
                        for i in range(2):
                            mm = dve.scalar_tensor_tensor(y[:, 2 * j + i, cols], xc[:, 2 * j + i, cols],
                                                          dskip[:, 2 * j + i:2 * j + i + 1],
                                                          ps[j % 2][:, i * T:(i + 1) * T], ALU.mult, ALU.add)
                        mm.then_inc(y_out, 1)

                    if blk:
                        dve.wait_ge(ptail_T, l * 2 + blk)
                        rows = PH if blk == 1 else NB * PH
                        dve.tensor_copy((ptailP[:] if blk == 1 else ptail[0:rows, :]), ps[7][0:rows, :]
                                        ).then_inc(ptail_out, 1)
                    exponents(0)
                    exponents(1)
                    for j in range(4):
                        head_weights(j)
                        if j < 2:
                            dve.drain()
                            exponents(j + 2)
                        if j:
                            heads_out(j - 1)
                    heads_out(3)
                    if blk == 0:
                        dve.wait_ge(st_mm, l * 2 + 1)
                        for g, b in enumerate((2, 4)):
                            dve.tensor_copy(s1T[:, g * 512:(g + 1) * 512], ps[b][:])
                        for g in range(NG):
                            mm = dve.tensor_copy(snat[:, 4 * g:4 * g + 4, :], ps[5 + g][:].rearrange("p (j n) -> p j n", j=4))
                        mm.then_inc(st_new, 1)
                    elif blk == 1:
                        dve.wait_ge(st_mm, l * 2 + 2)
                        alone(dve)
                        dve.drain()
                        for j in range(SST):
                            mm = dve.scalar_tensor_tensor(snew[:, j, :], snat[:, j, :], dec[:, j, 1:2],
                                                          ps[5 + j // 4][:, (j % 4) * NS:(j % 4 + 1) * NS],
                                                          ALU.mult, ALU.add)
                        mm.then_inc(st_new, 1)

                def states(qq, pair):
                    for i in range(2):
                        mm = dve.tensor_scalar(bm[:, i, :], xtok[0:SAMP, SSW:],
                                               con[0:SAMP, ds(qq * 4 + (K_SEQ + 2 * pair + i), 1)], None, ALU.mult)
                    mm.then_inc(s_bm, 1)
                    for i in range(2):
                        dve.wait_ge(s_stored[i], qq * 32 + (l * 80 + 16 * pair + 16))
                        dve.wait_ge(s_mm2, qq * 4 + (l * NB + 2 * pair + i + 1))
                        for j in range(SST):
                            mm = dve.scalar_tensor_tensor(s_new_rows[:, i, j, :], s_in[:, 2 * pair + i, j, :],
                                                          dec[:, j, ds(qq * 4 + (2 + 2 * pair + i), 1)],
                                                          ps[5 + j // 4][:, (j % 4) * NS:(j % 4 + 1) * NS],
                                                          ALU.mult, ALU.add)
                        mm.then_inc(s_new, 1)

                with dve.Fori(0, NB // 4) as qq:
                    states(qq, 0)
                    states(qq, 1)
                for c in range(2):
                    for e in range(2):
                        r = slice(DH * e, DH * e + DH)
                        dst = y[r, 4 * c:4 * c + 4, SEQ:TOK]
                        dve.tensor_tensor(dst, dst, ps[2 + c][r, :].rearrange("p (j e t) -> p j e t", j=4, e=2)[:, :, e, :],
                                          ALU.add)
                dve.drain()
                cols = slice(SEQ, TOK)
                dve.tensor_tensor(y[:, :, cols], y[:, :, cols], z[:, :, cols], ALU.mult)
                dve.drain()
                dve.tensor_tensor(z[:, :, cols], y[:, :, cols], y[:, :, cols], ALU.mult)
                dve.drain()
                dve.tensor_tensor(z[:, 0:4, cols], z[:, 0:4, cols], z[:, 4:8, cols], ALU.add).then_inc(y_sq_s, 1)
                dve.wait_ge(p_hi, l + 1)
                for g in range(PLT):
                    dve.scalar_tensor_tensor(hl[:, SBT + SST + g, :], ps[POOL_BANKS[g]][:, 0:TOK],
                                             par[:, C_PS + g:C_PS + g + 1],
                                             hh[:, SBT + SST + g, :].bitcast(F32), ALU.mult, ALU.subtract)
                dve.wait_ge(y_sum, l + 1)
                dve.tensor_scalar(rstd[:], ps[7][:, 0:TOK], 1.0 / SSW, EPS, ALU.mult, ALU.add).then_inc(y_ms, 1)
                dve.wait_ge(y_root, l + 1)
                dve.reciprocal(rstd[:], rstd[:])
                dve.drain()
                for t in range(SST):
                    dve.scalar_tensor_tensor(y[:, t, :], y[:, t, :], par[:, C_SN + t:C_SN + t + 1], rstd[:],
                                             ALU.mult, ALU.mult).then_inc(y_normed, 1)
                for t in range(SST):
                    dve.wait_ge(y_hi, l * SST + t + 1)
                    dve.tensor_tensor(hl[:, SBT + t, :], y[:, t, :], hh[:, SBT + t, :].bitcast(F32), ALU.subtract)
                meet(dve, "dve", stage(l, M_MIX))

                def take_sum(i, g, banks):
                    for t in range(2):
                        dst = x[:, ds(i * 4 + (2 * g + t), 1), :].rearrange("p c k -> p (c k)")
                        mm = dve.tensor_tensor(dst, banks[t][:, 0:TOK], dst, ALU.add)
                    mm.then_inc(group_out, 1)

                left = bodies(l, B_OUT, 4, None, take_sum)
                lo(l, B_PART[0][0], 0)
                left()
                meet(dve, "dve", stage(l, M_OUT))
                norm_low(l, l * 2 + 2, C_N2)

                def gate_history():
                    dve.wait_ge(frow_T, l + 1)
                    for half in range(2):
                        dve.tensor_copy(hist_f[:, 22 * half:22 * half + 22, :].rearrange("p c k -> p (c k)"),
                                        ps[4 + half][:, 0:22 * 16])
                    dve.drain()

                left, t0, done = None, 0, 0
                for part, tiles in enumerate(PARTS):
                    up, down = B_PART[part]

                    def take_gate_up(i, g, banks, t0=t0, done=done):
                        if g == 0:
                            c0 = i * 2 + t0
                            e2 = ext_fill(banks, lambda t: hist_f[:, ds(c0 + t, 1), :].rearrange(
                                "p c (b k) -> p (c b) k", b=NB), 2)
                            for t in range(2):
                                dve.tensor_copy(tail_f[:, ds(c0 + t, 1), 0:2].rearrange("p c k -> p (c k)"),
                                                ext[:, t, E0 - 2:E0])
                                dve.tensor_copy(tail_f[:, ds(c0 + t, 1), 2:].rearrange("p c (b k) -> p (c b) k", b=NB),
                                                e2[:, t, :, H3 + NT - 2:])
                            conv(lambda t: gc[:, t, :], e2, FK, lambda kk, t: par[:, ds(c0 + (t + C_FW + kk * FT), 1)],
                                 lambda t: par[:, ds(c0 + (t + C_FB), 1)]).then_inc(conv_done, 1)
                        else:
                            dve.wait_ge(silu_done, l * 22 + i + (done + 1))
                            for t in range(2):
                                dve.tensor_tensor(gc[:, t, :], gc[:, t, :], rstd[:], ALU.mult)
                            dve.drain()
                            for t in range(2):
                                mm = dve.tensor_tensor(gc[:, t, :], gc[:, t, :], banks[t][:, 0:TOK], ALU.mult)
                            mm.then_inc(group_out, 1)
                            dve.drain()
                            dve.tensor_copy(ah[:, ds(i * 2, 2), :], gc[:])
                            dve.drain()
                            dve.tensor_tensor(al[:, ds(i * 2, 2), :], gc[:], ah[:, ds(i * 2, 2), :].bitcast(F32),
                                              ALU.subtract)
                            dve.drain()

                    left = bodies(l, up, tiles // 2, left, take_gate_up,
                                  scale=None if part else (lambda: (norm_scale(l * 2 + 2), gate_history())),
                                  ahead=not part)

                    def last_of_part(left=left):
                        left()
                        dve.drain().then_inc(part_ready, 1)

                    left = bodies(l, down, 4, last_of_part, take_sum, tiles // 2)
                    t0 += tiles
                    done += tiles // 2
                left()
                for n in range(11):
                    dve.wait_ge(ftail_T, l * 11 + n + 1)
                    dve.tensor_copy(ftail[:, n * 512:(n + 1) * 512], ps[4 + n % 4][0:18, :]).then_inc(ftail_out, 1)
                meet(dve, "dve", stage(l, M_FFN))

            dve.tensor_tensor(sq[:, 8:16, :], x[:, 8:16, :], x[:, 8:16, :], ALU.mult)
            dve.wait_ge(last_squares, 1)
            dve.drain()
            dve.tensor_tensor(sq[:, 0:8, :], sq[:, 0:8, :], sq[:, 8:16, :], ALU.add)
            dve.drain()
            dve.tensor_tensor(sq[:, 0:4, :], sq[:, 0:4, :], sq[:, 4:8, :], ALU.add).then_inc(last_summed, 1)
            norm_scale(2 * DEPTH + 1)
            for t in range(KT):
                mm = dve.scalar_tensor_tensor(x[:, t, :], x[:, t, :], fgain[:, t:t + 1], rstd[:], ALU.mult, ALU.mult)
            mm.then_inc(root_taken, 1)
            for n in range(12):
                c, j = n // 4, n % 4
                T = P if c < 2 else SAMP
                dve.wait_ge(last_T, n + 1)
                dve.tensor_copy(xrow[0:T, c, j * 512:(j + 1) * 512], ps[j][0:T, :]).then_inc(last_out, 1)


_INS = ["x_prompt", "x_sample", "cache_k", "cache_v", "page_table", "state_ssm", "state_ssm_conv", "state_pool",
        "state_ffn_conv", "norm1", "w_in", "sb_bias", "ssd_conv_w", "ssd_conv_b", "dt_bias", "a_log", "d_skip",
        "ssd_norm", "pool_w", "pool_scale", "w_out", "norm2", "w_gate", "w_up", "ffn_conv_w", "ffn_conv_b", "w_down",
        "final_norm"]
_OUTS = [
    ("y_prompt", (1, SEQ, D)), ("y_sample", (NB, NT, D)),
    ("new_k_prompt", (DEPTH, 1, SEQ, SBH, DH)), ("new_v_prompt", (DEPTH, 1, SEQ, SBH, DH)),
    ("new_ssm_prompt", (DEPTH, 1, SSH, DH, NS)), ("new_ssm_conv_prompt", (DEPTH, 1, CVK - 1, CVD)),
    ("new_pool_prompt", (DEPTH, 1, PH, POOLW)), ("new_ffn_conv_prompt", (DEPTH, 1, FK - 1, FF)),
    ("new_k_sample", (DEPTH, NB, NT, SBH, DH)), ("new_v_sample", (DEPTH, NB, NT, SBH, DH)),
    ("new_ssm_sample", (DEPTH, NB, SSH, DH, NS)), ("new_ssm_conv_sample", (DEPTH, NB, CVK - 1, CVD)),
    ("new_pool_sample", (DEPTH, NB, PH, POOLW)), ("new_ffn_conv_sample", (DEPTH, NB, FK - 1, FF)),
]


def shape_constants():
    import numpy as np
    i = np.arange(P)
    con = np.zeros((P, NCON), np.float32)
    con[:, K_ID:K_ID + P] = np.eye(P)
    con[:, K_GE:K_GE + P] = i[:, None] >= i[None, :]
    con[:, K_LE:K_LE + P] = i[:, None] <= i[None, :]
    con[:, K_ONE:K_ONE + P] = 1.0
    neg = np.where(i[:, None] < i[None, :], 0.0, NEG)
    con[:, K_NEG:K_NEG + P] = neg
    con[:, K_NEG + 2 * P:K_NEG + 3 * P] = neg
    s = np.arange(SAMP)
    same = (s[:, None] // NT) == (s[None, :] // NT)
    con[0:SAMP, K_SLE:K_SLE + SAMP] = same & (s[:, None] <= s[None, :])
    con[0:SAMP, K_SONE:K_SONE + SAMP] = same
    con[0:SAMP, K_SNEG:K_SNEG + SAMP] = np.where(same & (s[:, None] < s[None, :]), 0.0, NEG)
    for g, win in enumerate(WINS):
        con[:, K_CNT + 16 * g:K_CNT + 16 * g + 16] = 1.0 / np.minimum(win, np.arange(16) + 1)
    con[0:SAMP, K_SEQ:K_SEQ + NB] = (s[:, None] // NT) == np.arange(NB)[None, :]
    used = (i % 32) < 2 * NT
    con[:, K_HEAD:K_HEAD + 2] = ((i[:, None] % 32) // NT) == np.arange(2)[None, :]
    con[:, K_TOK:K_TOK + SBT * NT] = used[:, None] & (
        (i[:, None] // 32 * NT + i[:, None] % NT) == np.arange(SBT * NT)[None, :])
    sel = np.zeros((SSH, SST, P), np.float32)
    for j in range(SST):
        for m in range(P):
            sel[2 * j + m // DH, j, m] = 1.0
    return con, sel


def kernel(**inputs):
    import numpy as _np
    import concourse.bacc as _bacc
    from concourse import mybir as _mybir
    from concourse.bass_utils import run_bass_kernel_spmd as _run

    nc = _bacc.Bacc("TRN2", target_bir_lowering=False, num_devices=1)
    arrays, ins, outs = {}, {}, {}
    con, sel = shape_constants()
    for name in _INS + ["con", "sel"]:
        arr = _np.ascontiguousarray({"con": con, "sel": sel}[name] if name in ("con", "sel") else inputs[name])
        arrays[f"in_{name}"] = arr
        ins[name] = nc.dram_tensor(f"in_{name}", arr.shape, _mybir.dt.from_np(arr.dtype), kind="ExternalInput").ap()
    for name, shape in _OUTS:
        outs[name] = nc.dram_tensor(f"out_{name}", shape, F32, kind="ExternalOutput").ap()
    build(nc, ins, outs)
    r = _run(nc, [arrays], core_ids=[0])
    return tuple(r.results[0][f"out_{name}"] for name, _ in _OUTS)
```
